# Optimizing a Trainium2 kernel written in Bass

```python
import jax
import jax.numpy as jnp
from jax import lax
import numpy as np
import jax, jax.numpy as jnp

D_MODEL = 1024
BATCH = 1
SEQ = 256
DEPTH = 1

CTX_LEN = 256
GRID_W = 64
EPS = 1e-6

ML_WIDTH = D_MODEL // 2
ML_HEADS = 4
ML_HEAD_DIM = ML_WIDTH // ML_HEADS
ML_CHUNK = 128
GLA_WIDTH = D_MODEL - ML_WIDTH
GLA_HEADS = 4
GLA_DV = GLA_WIDTH // GLA_HEADS
GLA_KEY_WIDTH = GLA_WIDTH // 2
GLA_DK = GLA_KEY_WIDTH // GLA_HEADS
GLA_RANK = 16
GLA_TAU = 16.0
GLA_CHUNK = 64
CONV_W = 3
MIX_WIDTH = ML_WIDTH + GLA_WIDTH
PROJ_WIDTHS = (ML_WIDTH, ML_WIDTH, ML_WIDTH, ML_WIDTH, 4 * ML_HEADS,
               GLA_KEY_WIDTH, GLA_KEY_WIDTH, GLA_WIDTH, GLA_WIDTH, 2 * GLA_RANK)
P_TOTAL = sum(PROJ_WIDTHS)

PEER_HEADS = 8
PEER_NKEYS = 128
PEER_EXPERTS = PEER_NKEYS * PEER_NKEYS
PEER_TOPK = 16
PEER_QDIM = 256
PEER_BLOCK = 128


def rms_norm(x, g):
    xf = x.astype(jnp.float32)
    y = xf * lax.rsqrt(jnp.mean(xf * xf, axis=-1, keepdims=True) + EPS)
    return y.astype(x.dtype) * g

def head_rms(h, g):
    y = h * lax.rsqrt(jnp.mean(h * h, axis=-1, keepdims=True) + EPS)
    return y.reshape(h.shape[:2] + (-1,)) * g

def short_conv(u, w, on_grid):
    bz, n, ch = u.shape
    if on_grid:
        rows = n // GRID_W
        u = u.reshape(bz * rows, GRID_W, ch)
    y = lax.conv_general_dilated(u, w[:, None, :].astype(u.dtype), (1,),
                                 [(CONV_W // 2, CONV_W // 2)],
                                 dimension_numbers=('NWC', 'WIO', 'NWC'),
                                 feature_group_count=ch)
    return y.reshape(bz, n, ch)

def to_chunks(t, size):
    bz, n, hh = t.shape[:3]
    t = t.reshape((bz, n // size, size, hh) + t.shape[3:])
    return jnp.moveaxis(t, 3, 1)

def from_chunks(t):
    bz, hh, nc, ll, d = t.shape
    return jnp.moveaxis(t, 1, 3).reshape(bz, nc * ll, hh, d)

def orient(t, direction):
    return jnp.flip(t, axis=1) if direction == 1 else t

def prep_mixers(z, conv_w, gate_b, lr_w2, alpha_b, on_grid):
    bz, n, _ = z.shape
    f32 = jnp.float32
    mq, mk, mv, mo, mg, gq, gk, gv, gr, glr = jnp.split(
        z, np.cumsum(PROJ_WIDTHS)[:-1].tolist(), axis=-1)
    mq, mk = jnp.split(jax.nn.silu(short_conv(jnp.concatenate([mq, mk], axis=-1), conv_w, on_grid)),
                       2, axis=-1)
    gates = (mg + gate_b).astype(f32).reshape(bz, n, 2, 2, ML_HEADS)
    alpha = jnp.einsum('bndr,drk->bndk', glr.reshape(bz, n, 2, GLA_RANK), lr_w2) + alpha_b
    return {
        'ml_q': mq.astype(f32).reshape(bz, n, ML_HEADS, ML_HEAD_DIM),
        'ml_k': (mk.astype(f32) * ML_HEAD_DIM ** -0.5).reshape(bz, n, ML_HEADS, ML_HEAD_DIM),
        'ml_v': mv.astype(f32).reshape(bz, n, ML_HEADS, ML_HEAD_DIM),
        'ml_o': mo,
        'ml_ig': gates[:, :, :, 0],
        'ml_lf': jax.nn.log_sigmoid(gates[:, :, :, 1]),
        'gla_q': (gq.astype(f32) * GLA_DK ** -0.5).reshape(bz, n, GLA_HEADS, GLA_DK),
        'gla_k': gk.astype(f32).reshape(bz, n, GLA_HEADS, GLA_DK),
        'gla_v': gv.astype(f32).reshape(bz, n, GLA_HEADS, GLA_DV),
        'gla_r': gr,
        'gla_la': (jax.nn.log_sigmoid(alpha.astype(f32)) / GLA_TAU).reshape(
            bz, n, 2, GLA_HEADS, GLA_DK),
    }

def mlstm_states(k, v, logf, ig, init):
    b = jnp.cumsum(logf, axis=-1)
    b_end = b[..., -1]
    w_log = b_end[..., None] - b + ig
    m_loc = jnp.max(w_log, axis=-1)
    w = jnp.exp(w_log - m_loc[..., None])
    c_loc = jnp.einsum('bhcld,bhcle->bhcde', w[..., None] * v, k)
    n_loc = jnp.einsum('bhcl,bhcle->bhce', w, k)

    def step(carry, inp):
        cm, nv, m = carry
        be, ml, cl, nl = inp
        m_new = jnp.maximum(be + m, ml)
        a = jnp.exp(be + m - m_new)
        bb = jnp.exp(ml - m_new)
        c_new = a[..., None, None] * cm + bb[..., None, None] * cl
        n_new = a[..., None] * nv + bb[..., None] * nl
        return (c_new, n_new, m_new), (cm, nv, m)

    xs = tuple(jnp.moveaxis(t, 2, 0) for t in (b_end, m_loc, c_loc, n_loc))
    final, starts = lax.scan(step, init, xs)
    starts = tuple(jnp.moveaxis(t, 0, 2) for t in starts)
    return starts, final

def mlstm_outputs(q, k, v, logf, ig, starts):
    c_s, n_s, m_s = starts
    ll = q.shape[-2]
    tri = jnp.tril(jnp.ones((ll, ll), dtype=bool))
    b = jnp.cumsum(logf, axis=-1)
    d_log = jnp.where(tri, b[..., :, None] - b[..., None, :] + ig[..., None, :], -jnp.inf)
    inter_log = b + m_s[..., None]
    m_t = jnp.maximum(inter_log, jnp.max(d_log, axis=-1))
    scores = jnp.einsum('bhctd,bhcsd->bhcts', q, k) * jnp.exp(d_log - m_t[..., None])
    inter = jnp.exp(inter_log - m_t)
    num = (jnp.einsum('bhcts,bhcsd->bhctd', scores, v)
           + inter[..., None] * jnp.einsum('bhcde,bhcte->bhctd', c_s, q))
    den = scores.sum(-1) + inter * jnp.einsum('bhce,bhcte->bhct', n_s, q)
    return num / jnp.maximum(jnp.abs(den), jnp.exp(-m_t))[..., None]

def mlstm_direction(lat, ctx, with_ctx_out):
    q, k, v, lf, ig = lat
    qc, kc, vc, lfc, igc = ctx
    bz, hh, _, _, d = q.shape
    init = (jnp.zeros((bz, hh, d, d), jnp.float32), jnp.zeros((bz, hh, d), jnp.float32),
            jnp.zeros((bz, hh), jnp.float32))
    ctx_starts, ctx_final = mlstm_states(kc, vc, lfc, igc, init)
    lat_starts, _ = mlstm_states(k, v, lf, ig, ctx_final)
    h = mlstm_outputs(q, k, v, lf, ig, lat_starts)
    hc = mlstm_outputs(qc, kc, vc, lfc, igc, ctx_starts) if with_ctx_out else None
    return h, hc

def gla_states(k, v, loga, init):
    b = jnp.cumsum(loga, axis=-2)
    b_end = b[..., -1, :]
    s_loc = jnp.einsum('bhcld,bhcle->bhcde', k * jnp.exp(b_end[..., None, :] - b), v)

    def step(s, inp):
        be, sl = inp
        return jnp.exp(be)[..., None] * s + sl, s

    final, starts = lax.scan(step, init, (jnp.moveaxis(b_end, 2, 0), jnp.moveaxis(s_loc, 2, 0)))
    return jnp.moveaxis(starts, 0, 2), final

def gla_outputs(q, k, v, loga, s_start):
    ll = q.shape[-2]
    tri = jnp.tril(jnp.ones((ll, ll), dtype=bool))
    b = jnp.cumsum(loga, axis=-2)
    ref = b[..., ll // 2, :][..., None, :]
    att = jnp.einsum('bhctd,bhcsd->bhcts', q * jnp.exp(b - ref), k * jnp.exp(ref - b))
    att = jnp.where(tri, att, 0.0)
    return (jnp.einsum('bhcts,bhcse->bhcte', att, v)
            + jnp.einsum('bhctd,bhcde->bhcte', q * jnp.exp(b), s_start))

def gla_direction(lat, ctx, with_ctx_out):
    q, k, v, la = lat
    qc, kc, vc, lac = ctx
    bz, hh = q.shape[:2]
    init = jnp.zeros((bz, hh, GLA_DK, GLA_DV), jnp.float32)
    ctx_starts, ctx_final = gla_states(kc, vc, lac, init)
    lat_starts, _ = gla_states(k, v, la, ctx_final)
    h = gla_outputs(q, k, v, la, lat_starts)
    hc = gla_outputs(qc, kc, vc, lac, ctx_starts) if with_ctx_out else None
    return h, hc

def ml_inputs(p, d):
    return [to_chunks(orient(t, d), ML_CHUNK)
            for t in (p['ml_q'], p['ml_k'], p['ml_v'], p['ml_lf'][:, :, d], p['ml_ig'][:, :, d])]

def gla_inputs(p, d):
    return [to_chunks(orient(t, d), GLA_CHUNK)
            for t in (p['gla_q'], p['gla_k'], p['gla_v'], p['gla_la'][:, :, d])]

def mix_out(ml_h, ml_o, gla_h, gla_r, ml_g, gla_g, w_out, dtype):
    ml = jax.nn.sigmoid(ml_o) * head_rms(ml_h, ml_g)
    gl = jax.nn.silu(gla_r) * head_rms(gla_h, gla_g)
    return (jnp.concatenate([ml, gl], axis=-1) @ w_out).astype(dtype)

def token_mixer(h_lat, h_ctx, w_in, conv_w, gate_b, lr_w2, alpha_b, ml_g, gla_g, w_out,
                with_ctx_out):
    lat = prep_mixers(h_lat @ w_in, conv_w, gate_b, lr_w2, alpha_b, True)
    ctx = prep_mixers(h_ctx @ w_in, conv_w, gate_b, lr_w2, alpha_b, False)
    ml_lat, ml_ctx, gla_lat, gla_ctx = [], [], [], []
    for d in range(2):
        h, hc = mlstm_direction(ml_inputs(lat, d), ml_inputs(ctx, d), with_ctx_out)
        ml_lat.append(orient(from_chunks(h), d))
        g, gc = gla_direction(gla_inputs(lat, d), gla_inputs(ctx, d), with_ctx_out)
        gla_lat.append(orient(from_chunks(g), d))
        if with_ctx_out:
            ml_ctx.append(orient(from_chunks(hc), d))
            gla_ctx.append(orient(from_chunks(gc), d))
    y = mix_out(ml_lat[0] + ml_lat[1], lat['ml_o'], gla_lat[0] + gla_lat[1], lat['gla_r'],
                ml_g, gla_g, w_out, h_lat.dtype)
    yc = None
    if with_ctx_out:
        yc = mix_out(ml_ctx[0] + ml_ctx[1], ctx['ml_o'], gla_ctx[0] + gla_ctx[1], ctx['gla_r'],
                     ml_g, gla_g, w_out, h_ctx.dtype)
    return y, yc

def peer_ffn(h, wq, keys, u_tab, v_tab):
    bz, n, d = h.shape
    blocks = h.reshape(bz * n // PEER_BLOCK, PEER_BLOCK, d)

    def retrieve(xb):
        q = (xb @ wq).reshape(PEER_BLOCK, PEER_HEADS, 2, PEER_QDIM // 2)
        s = jnp.einsum('tphq,phkq->tphk', q, keys)
        top_s, top_i = lax.top_k(s, PEER_TOPK)
        cand = top_s[:, :, 0, :, None] + top_s[:, :, 1, None, :]
        best_s, best_c = lax.top_k(cand.reshape(PEER_BLOCK, PEER_HEADS, PEER_TOPK * PEER_TOPK),
                                   PEER_TOPK)
        i1 = jnp.take_along_axis(top_i[:, :, 0], best_c // PEER_TOPK, axis=-1)
        i2 = jnp.take_along_axis(top_i[:, :, 1], best_c % PEER_TOPK, axis=-1)
        idx = i1 * PEER_NKEYS + i2
        g = jax.nn.softmax(best_s.astype(jnp.float32), axis=-1).astype(xb.dtype)
        act = jax.nn.gelu(jnp.einsum('tpkd,td->tpk', u_tab[idx], xb), approximate=False)
        return jnp.einsum('tpk,tpkd->td', g * act, v_tab[idx])

    return lax.map(retrieve, blocks).reshape(bz, n, d)

def first_inputs(seed: int = 0) -> dict:
    key = jax.random.key(seed)
    ks = jax.random.split(key, 24)

    def nrm(k, shape, scale):
        return jax.random.normal(k, shape, jnp.float32) * scale

    f_bias = jnp.linspace(3.0, 6.0, ML_HEADS, dtype=jnp.float32)
    i_part = nrm(ks[8], (DEPTH, 2, 1, ML_HEADS), 0.1)
    f_part = f_bias + nrm(ks[9], (DEPTH, 2, 1, ML_HEADS), 0.1)
    ml_gate_b = jnp.concatenate([i_part, f_part], axis=2).reshape(DEPTH, 4 * ML_HEADS)
    return {
        'x': nrm(ks[0], (BATCH, SEQ, D_MODEL), 1.0),
        'c': nrm(ks[1], (BATCH, D_MODEL), 1.0),
        'ctx': nrm(ks[2], (BATCH, CTX_LEN, D_MODEL), 1.0),
        'c_ctx': nrm(ks[3], (D_MODEL,), 1.0),
        'w_mod': nrm(ks[4], (DEPTH, D_MODEL, 6 * D_MODEL), 0.5 * D_MODEL ** -0.5),
        'b_mod': nrm(ks[5], (DEPTH, 6 * D_MODEL), 0.02),
        'norm1_g': 1.0 + nrm(ks[6], (DEPTH, D_MODEL), 0.02),
        'w_in': nrm(ks[7], (DEPTH, D_MODEL, P_TOTAL), D_MODEL ** -0.5),
        'ml_conv_w': nrm(ks[10], (DEPTH, CONV_W, 2 * ML_WIDTH), CONV_W ** -0.5),
        'ml_gate_b': ml_gate_b,
        'ml_norm_g': 1.0 + nrm(ks[11], (DEPTH, ML_WIDTH), 0.02),
        'gla_lr_w2': nrm(ks[12], (DEPTH, 2, GLA_RANK, GLA_KEY_WIDTH), GLA_RANK ** -0.5),
        'gla_alpha_b': nrm(ks[13], (DEPTH, 2, GLA_KEY_WIDTH), 0.1),
        'gla_norm_g': 1.0 + nrm(ks[14], (DEPTH, GLA_WIDTH), 0.02),
        'w_out': nrm(ks[15], (DEPTH, MIX_WIDTH, D_MODEL), MIX_WIDTH ** -0.5),
        'norm2_g': 1.0 + nrm(ks[16], (DEPTH, D_MODEL), 0.02),
        'peer_wq': nrm(ks[17], (DEPTH, D_MODEL, PEER_HEADS * PEER_QDIM), D_MODEL ** -0.5),
        'peer_keys': nrm(ks[18], (DEPTH, PEER_HEADS, 2, PEER_NKEYS, PEER_QDIM // 2),
                         (PEER_QDIM // 2) ** -0.5),
        'peer_u': nrm(ks[19], (DEPTH, PEER_EXPERTS, D_MODEL), D_MODEL ** -0.5),
        'peer_v': nrm(ks[20], (DEPTH, PEER_EXPERTS, D_MODEL), PEER_HEADS ** -0.5),
        'norm_f_g': 1.0 + nrm(ks[21], (D_MODEL,), 0.02),
    }

def first_block(x, c, ctx, c_ctx, w_mod, b_mod, norm1_g, w_in, ml_conv_w, ml_gate_b, ml_norm_g,
              gla_lr_w2, gla_alpha_b, gla_norm_g, w_out, norm2_g, peer_wq, peer_keys, peer_u,
              peer_v, norm_f_g):
    cond = jax.nn.silu(c)
    cond_ctx = jax.nn.silu(c_ctx)
    for layer in range(DEPTH):
        update_ctx = layer + 1 < DEPTH
        mod = (cond @ w_mod[layer] + b_mod[layer])[:, None, :]
        mod_c = cond_ctx @ w_mod[layer] + b_mod[layer]
        sh1, sc1, g1, sh2, sc2, g2 = jnp.split(mod, 6, axis=-1)
        csh1, csc1, cg1, csh2, csc2, cg2 = jnp.split(mod_c, 6, axis=-1)

        h = rms_norm(x, norm1_g[layer]) * (1.0 + sc1) + sh1
        hc = rms_norm(ctx, norm1_g[layer]) * (1.0 + csc1) + csh1
        y, yc = token_mixer(h, hc, w_in[layer], ml_conv_w[layer], ml_gate_b[layer],
                            gla_lr_w2[layer], gla_alpha_b[layer], ml_norm_g[layer],
                            gla_norm_g[layer], w_out[layer], update_ctx)
        x = x + g1 * y
        h2 = rms_norm(x, norm2_g[layer]) * (1.0 + sc2) + sh2
        x = x + g2 * peer_ffn(h2, peer_wq[layer], peer_keys[layer], peer_u[layer], peer_v[layer])

        if update_ctx:
            ctx = ctx + cg1 * yc
            hc2 = rms_norm(ctx, norm2_g[layer]) * (1.0 + csc2) + csh2
            ctx = ctx + cg2 * peer_ffn(hc2, peer_wq[layer], peer_keys[layer], peer_u[layer],
                                       peer_v[layer])
    return rms_norm(x, norm_f_g)


DEPTH_2 = 2

HEAD_DIM = 64
ROPE_THETA = 10000.0
ATTN_SCALE = HEAD_DIM ** -0.5
Q_BLOCK = 128

ATT_WIDTH = D_MODEL // 2
ATT_HEADS = ATT_WIDTH // HEAD_DIM
ATT_KV_HEADS = ATT_HEADS // 4
ATT_GROUP = ATT_HEADS // ATT_KV_HEADS
ATT_KV_WIDTH = ATT_KV_HEADS * HEAD_DIM
POOL_WINDOWS = (2, 4, 8, 16)
POOL_WIDTH = D_MODEL // 4
POOL_GROUP_DIM = POOL_WIDTH // len(POOL_WINDOWS)
NA_WIDTH = D_MODEL // 4
NA_HEADS = NA_WIDTH // HEAD_DIM
NA_KH_MAX = 8
NA_KW = 16

MIX_WIDTH_2 = ATT_WIDTH + POOL_WIDTH + NA_WIDTH
IN_SPLITS = (ATT_WIDTH, ATT_KV_WIDTH, ATT_KV_WIDTH, ATT_WIDTH,
             POOL_WIDTH, POOL_WIDTH,
             NA_WIDTH, NA_WIDTH, NA_WIDTH, NA_WIDTH)
IN_OFFSETS = tuple(int(o) for o in np.cumsum((0,) + IN_SPLITS))
IN_WIDTH = IN_OFFSETS[-1]
SPLIT_POINTS = IN_OFFSETS[1:-1]


def rms_norm_2(x, g):
    xf = x.astype(jnp.float32)
    y = xf * lax.rsqrt(jnp.mean(xf * xf, axis=-1, keepdims=True) + EPS)
    return (y * g.astype(jnp.float32)).astype(x.dtype)

def rope_axis(x, pos):
    half = x.shape[-1] // 2
    inv_freq = ROPE_THETA ** (-jnp.arange(half, dtype=jnp.float32) / half)
    ang = pos.astype(jnp.float32)[:, None] * inv_freq[None, :]
    cos = jnp.cos(ang)[None, :, None, :]
    sin = jnp.sin(ang)[None, :, None, :]
    xf = x.astype(jnp.float32)
    x1, x2 = xf[..., :half], xf[..., half:]
    return jnp.concatenate([x1 * cos - x2 * sin, x2 * cos + x1 * sin], axis=-1).astype(x.dtype)

def rope_2d(x, row, col):
    h = HEAD_DIM // 2
    return jnp.concatenate([rope_axis(x[..., :h], row), rope_axis(x[..., h:], col)], axis=-1)

def dense_attn(q, k, v):
    s = jnp.einsum("bqkgd,bskd->bkgqs", q, k).astype(jnp.float32)
    p = jax.nn.softmax(s, axis=-1).astype(v.dtype)
    o = jnp.einsum("bkgqs,bskd->bqkgd", p, v)
    return o.reshape(o.shape[0], o.shape[1], -1)

def global_gqa(q, k, v, k_ctx, v_ctx):
    bsz, seq = q.shape[:2]
    n_blk = seq // Q_BLOCK
    kk = jnp.concatenate([k, k_ctx], axis=1)
    vv = jnp.concatenate([v, v_ctx], axis=1)
    qb = jnp.moveaxis(q.reshape(bsz, n_blk, Q_BLOCK, ATT_KV_HEADS, ATT_GROUP, HEAD_DIM), 1, 0)
    o = lax.map(lambda qi: dense_attn(qi, kk, vv), qb)
    return jnp.moveaxis(o, 0, 1).reshape(bsz, seq, ATT_WIDTH)

def multi_pool(z):
    bsz, length, width = z.shape
    zf = z.astype(jnp.float32)
    cs = jnp.concatenate([jnp.zeros((bsz, 1, width), jnp.float32), jnp.cumsum(zf, axis=1)], axis=1)
    t = np.arange(length)
    outs = []
    for g, w in enumerate(POOL_WINDOWS):
        lo = np.maximum(t - w // 2, 0)
        hi = np.minimum(t + w // 2 - 1, length - 1)
        cnt = jnp.asarray((hi - lo + 1).astype(np.float32))[None, :, None]
        sl = slice(g * POOL_GROUP_DIM, (g + 1) * POOL_GROUP_DIM)
        seg = cs[:, :, sl]
        outs.append((seg[:, hi + 1] - seg[:, lo]) / cnt - zf[:, :, sl])
    return jnp.concatenate(outs, axis=-1).astype(z.dtype)

def pool_branch(z, w, s):
    bsz, length = z.shape[:2]
    pooled = multi_pool(z).reshape(bsz, length, len(POOL_WINDOWS), POOL_GROUP_DIM)
    y = jnp.einsum("blgi,gio->blgo", pooled, w).reshape(bsz, length, POOL_WIDTH)
    return y * s

def neighbourhood_attn(q, k, v, k_ctx, v_ctx, rpb, rows):
    bsz = q.shape[0]
    kh = min(NA_KH_MAX, rows)
    qg = q.reshape(bsz, rows, GRID_W, NA_HEADS, HEAD_DIM)
    kg = k.reshape(bsz, rows, GRID_W, NA_HEADS, HEAD_DIM)
    vg = v.reshape(bsz, rows, GRID_W, NA_HEADS, HEAD_DIM)
    c_idx = np.arange(GRID_W)
    c0 = np.clip(c_idx - NA_KW // 2, 0, GRID_W - NA_KW)
    cols = c0[:, None] + np.arange(NA_KW)[None, :]
    dcol = cols - c_idx[:, None] + NA_KW - 1
    n_nb = kh * NA_KW

    def row_block(r):
        r0 = jnp.clip(r - kh // 2, 0, rows - kh)
        k_band = lax.dynamic_slice_in_dim(kg, r0, kh, axis=1)
        v_band = lax.dynamic_slice_in_dim(vg, r0, kh, axis=1)
        k_nb = k_band[:, :, cols]
        v_nb = v_band[:, :, cols]
        q_r = lax.dynamic_index_in_dim(qg, r, axis=1, keepdims=False)
        s_nb = jnp.einsum("bqhd,bmqnhd->bhqmn", q_r, k_nb).astype(jnp.float32)
        drow = r0 + jnp.arange(kh) - r + NA_KH_MAX - 1
        bias = rpb[:, drow[:, None, None], dcol[None, :, :]]
        s_nb = s_nb + jnp.transpose(bias, (0, 2, 1, 3)).astype(jnp.float32)[None]
        s_ctx = jnp.einsum("bqhd,bchd->bhqc", q_r, k_ctx).astype(jnp.float32)
        s = jnp.concatenate([s_nb.reshape(bsz, NA_HEADS, GRID_W, n_nb), s_ctx], axis=-1)
        p = jax.nn.softmax(s, axis=-1).astype(v.dtype)
        p_nb = p[..., :n_nb].reshape(bsz, NA_HEADS, GRID_W, kh, NA_KW)
        p_ctx = p[..., n_nb:]
        return (jnp.einsum("bhqmn,bmqnhd->bqhd", p_nb, v_nb)
                + jnp.einsum("bhqc,bchd->bqhd", p_ctx, v_ctx))

    o = lax.map(row_block, jnp.arange(rows))
    return jnp.moveaxis(o, 0, 1).reshape(bsz, rows * GRID_W, NA_WIDTH)

def second_inputs(seed: int = 0) -> dict:
    key = jax.random.key(seed)
    ks = jax.random.split(key, 16)
    f32 = jnp.float32
    n = lambda k, shape: jax.random.normal(k, shape, f32)
    return {
        "x": n(ks[0], (BATCH, SEQ, D_MODEL)),
        "c": n(ks[1], (BATCH, D_MODEL)),
        "ctx": n(ks[2], (BATCH, CTX_LEN, D_MODEL)),
        "c_ctx": n(ks[3], (D_MODEL,)),
        "norm_gain": 1.0 + 0.02 * n(ks[4], (DEPTH_2, D_MODEL)),
        "w_mod": 0.5 * D_MODEL ** -0.5 * n(ks[5], (DEPTH_2, D_MODEL, 3 * D_MODEL)),
        "b_mod": 0.02 * n(ks[6], (DEPTH_2, 3 * D_MODEL)),
        "w_in": D_MODEL ** -0.5 * n(ks[7], (DEPTH_2, D_MODEL, IN_WIDTH)),
        "att_q_gain": 1.0 + 0.02 * n(ks[8], (DEPTH_2, HEAD_DIM)),
        "att_k_gain": 1.0 + 0.02 * n(ks[9], (DEPTH_2, HEAD_DIM)),
        "pool_w": POOL_GROUP_DIM ** -0.5 * n(ks[10], (DEPTH_2, len(POOL_WINDOWS), POOL_GROUP_DIM, POOL_GROUP_DIM)),
        "pool_scale": 1.0 + 0.02 * n(ks[11], (DEPTH_2, POOL_WIDTH)),
        "na_q_gain": 1.0 + 0.02 * n(ks[12], (DEPTH_2, HEAD_DIM)),
        "na_k_gain": 1.0 + 0.02 * n(ks[13], (DEPTH_2, HEAD_DIM)),
        "na_rpb": 0.1 * n(ks[14], (DEPTH_2, NA_HEADS, 2 * NA_KH_MAX - 1, 2 * NA_KW - 1)),
        "w_out": MIX_WIDTH_2 ** -0.5 * n(ks[15], (DEPTH_2, MIX_WIDTH_2, D_MODEL)),
    }

def second_block(x, c, ctx, c_ctx, norm_gain, w_mod, b_mod, w_in, att_q_gain, att_k_gain,
              pool_w, pool_scale, na_q_gain, na_k_gain, na_rpb, w_out):
    bsz, seq, _ = x.shape
    n_ctx = ctx.shape[1]
    rows = seq // GRID_W
    t = jnp.arange(seq)
    row, col = t // GRID_W, t % GRID_W
    silu = jax.nn.silu
    for l in range(DEPTH_2):
        last = l == DEPTH_2 - 1
        shift, scale, gate = jnp.split(silu(c) @ w_mod[l] + b_mod[l], 3, axis=-1)
        shift_c, scale_c, gate_c = jnp.split(silu(c_ctx) @ w_mod[l] + b_mod[l], 3, axis=-1)
        h = rms_norm_2(x, norm_gain[l]) * (1 + scale[:, None]) + shift[:, None]
        hc = rms_norm_2(ctx, norm_gain[l]) * (1 + scale_c) + shift_c

        aq, ak, av, ag, bz, bg, nq, nk, nv, ng = jnp.split(h @ w_in[l], SPLIT_POINTS, axis=-1)
        if last:
            ak_c, av_c = jnp.split(hc @ w_in[l][:, IN_OFFSETS[1]:IN_OFFSETS[3]], 2, axis=-1)
            nk_c, nv_c = jnp.split(hc @ w_in[l][:, IN_OFFSETS[7]:IN_OFFSETS[9]], 2, axis=-1)
        else:
            (aq_c, ak_c, av_c, ag_c, bz_c, bg_c,
             nq_c, nk_c, nv_c, ng_c) = jnp.split(hc @ w_in[l], SPLIT_POINTS, axis=-1)

        ak_c = rms_norm_2(ak_c.reshape(bsz, n_ctx, ATT_KV_HEADS, HEAD_DIM), att_k_gain[l])
        av_c = av_c.reshape(bsz, n_ctx, ATT_KV_HEADS, HEAD_DIM)
        nk_c = rms_norm_2(nk_c.reshape(bsz, n_ctx, NA_HEADS, HEAD_DIM), na_k_gain[l])
        nv_c = nv_c.reshape(bsz, n_ctx, NA_HEADS, HEAD_DIM)

        aq = rope_2d(rms_norm_2(aq.reshape(bsz, seq, ATT_HEADS, HEAD_DIM), att_q_gain[l]), row, col) * ATTN_SCALE
        aq = aq.reshape(bsz, seq, ATT_KV_HEADS, ATT_GROUP, HEAD_DIM)
        ak = rope_2d(rms_norm_2(ak.reshape(bsz, seq, ATT_KV_HEADS, HEAD_DIM), att_k_gain[l]), row, col)
        av = av.reshape(bsz, seq, ATT_KV_HEADS, HEAD_DIM)
        a_out = global_gqa(aq, ak, av, ak_c, av_c)
        b_out = pool_branch(bz, pool_w[l], pool_scale[l])
        nq = rms_norm_2(nq.reshape(bsz, seq, NA_HEADS, HEAD_DIM), na_q_gain[l]) * ATTN_SCALE
        nk = rms_norm_2(nk.reshape(bsz, seq, NA_HEADS, HEAD_DIM), na_k_gain[l])
        nv = nv.reshape(bsz, seq, NA_HEADS, HEAD_DIM)
        n_out = neighbourhood_attn(nq, nk, nv, nk_c, nv_c, na_rpb[l], rows)

        y = jnp.concatenate([a_out * silu(ag), b_out * silu(bg), n_out * silu(ng)], axis=-1) @ w_out[l]

        if not last:
            aq_c = rms_norm_2(aq_c.reshape(bsz, n_ctx, ATT_HEADS, HEAD_DIM), att_q_gain[l]) * ATTN_SCALE
            a_out_c = dense_attn(aq_c.reshape(bsz, n_ctx, ATT_KV_HEADS, ATT_GROUP, HEAD_DIM), ak_c, av_c)
            b_out_c = pool_branch(bz_c, pool_w[l], pool_scale[l])
            nq_c = rms_norm_2(nq_c.reshape(bsz, n_ctx, NA_HEADS, HEAD_DIM), na_q_gain[l]) * ATTN_SCALE
            n_out_c = dense_attn(nq_c[:, :, :, None, :], nk_c, nv_c)
            yc = jnp.concatenate([a_out_c * silu(ag_c), b_out_c * silu(bg_c), n_out_c * silu(ng_c)],
                                 axis=-1) @ w_out[l]
            ctx = ctx + gate_c * yc

        x = x + gate[:, None] * y
    return x


def setup_inputs(seed=0):
    out = dict(first_inputs(seed))
    for name, value in second_inputs(seed + 1).items():
        if name != "x":
            out[name + "_2"] = value
    return out


def reference(
    x, c, ctx, c_ctx, w_mod, b_mod, norm1_g, w_in, ml_conv_w, ml_gate_b, ml_norm_g, gla_lr_w2,
    gla_alpha_b, gla_norm_g, w_out, norm2_g, peer_wq, peer_keys, peer_u, peer_v, norm_f_g, c_2,
    ctx_2, c_ctx_2, norm_gain_2, w_mod_2, b_mod_2, w_in_2, att_q_gain_2, att_k_gain_2, pool_w_2,
    pool_scale_2, na_q_gain_2, na_k_gain_2, na_rpb_2, w_out_2,
):
    x = first_block(
        x, c, ctx, c_ctx, w_mod, b_mod, norm1_g, w_in, ml_conv_w, ml_gate_b, ml_norm_g,
        gla_lr_w2, gla_alpha_b, gla_norm_g, w_out, norm2_g, peer_wq, peer_keys, peer_u, peer_v,
        norm_f_g,
    )
    return second_block(
        x, c_2, ctx_2, c_ctx_2, norm_gain_2, w_mod_2, b_mod_2, w_in_2, att_q_gain_2,
        att_k_gain_2, pool_w_2, pool_scale_2, na_q_gain_2, na_k_gain_2, na_rpb_2, w_out_2,
    )


_drawn_inputs = setup_inputs


def setup_inputs(seed=0):
    import zlib

    import numpy as np

    out = dict(_drawn_inputs(seed))
    spreads = {}
    factors = {'norm1_g': 7.104,
     'ml_norm_g': 28.588,
     'gla_alpha_b': 6.839,
     'gla_norm_g': 8.0,
     'norm2_g': 6.04,
     'norm_f_g': 2.727,
     'ctx_2': 3.488,
     'norm_gain_2': 8.0,
     'b_mod_2': 4.913,
     'att_q_gain_2': 8.0,
     'att_k_gain_2': 8.0,
     'pool_scale_2': 8.0,
     'na_q_gain_2': 8.0,
     'na_k_gain_2': 8.0,
     'na_rpb_2': 26.56}
    for name, (base, spread) in spreads.items():
        noise = np.random.default_rng([zlib.crc32(name.encode()), seed]).standard_normal(out[name].shape)
        drawn = base * np.exp(spread * noise) if base else spread * noise
        out[name] = jnp.asarray(drawn.astype(out[name].dtype))
    for name, factor in factors.items():
        out[name] = (out[name] * factor).astype(out[name].dtype)
    return out
```

```python
from contextlib import ExitStack
import numpy as np
import concourse.bass as bass
from concourse import mybir

F32 = mybir.dt.float32
F32R = mybir.dt.float32r
U32 = mybir.dt.uint32
ACT = mybir.ActivationFunctionType
ALU = mybir.AluOpType
AX = mybir.AxisListType.X

P = 128
D = 1024
C = D // P
T = 256
NT = T // P
GRID = 64
EPS = 1e-6
WT = 2048
WC = WT // C
WSLOTS = 4
HALF = WT // 2
SPLIT1 = (0, 1, 2)
U_HALF = 32 // WSLOTS
N_SPLIT1 = 2 * len(SPLIT1) * U_HALF
N_SPLIT2 = N_SPLIT1 + 2 * WSLOTS * U_HALF
NB = 6
HEADS = 4
GRANK = 16
GC = 64
NGC = T // GC
PH, PK, TOPK = 8, 128, 16
NEG = -1e30
BIG = -3e38

MQ, MK, MV, MO, MG = 0, 512, 1024, 1536, 2048
GQ, GK, GV, GR, GLR = 2064, 2320, 2576, 3088, 3600
IN_TILES = ([(None, 48)] + [(MQ + i * WC, WC) for i in range(2)] + [(MK + i * WC, WC) for i in range(2)]
            + [(MV + i * WC, WC) for i in range(2)] + [(MO + i * WC, WC) for i in range(2)]
            + [(GQ, WC), (GK, WC)] + [(GV + i * WC, WC) for i in range(2)] + [(GR + i * WC, WC) for i in range(2)])
N_MOD1, N_IN, N_OUT, N_WQ = 6 * D // WC, len(IN_TILES), D // WC, 2048 // WC
N_MOD2 = 3 * D // WC
MOD_UNITS = (N_MOD1 + 2 * N_MOD2) // 2
MOD_FIRST = 4
MOD_LATER = {"gr": 1, "mlstm": 2, "alpha": 1, "kdn": 2, "state": 1, "att": 1}
N_PRE = N_MOD1 + 2 * N_MOD2 + N_IN + N_OUT + N_WQ + 1
N_PEER = 64
IN2 = 2816
N_IN2 = IN2 // WC
N_TILES = N_PRE + 2 * N_PEER + 2 * (N_IN2 + N_OUT)
AQ, AK, AV, AG, BZ, BG, NQ, NK, NV, NG = 0, 512, 640, 768, 1280, 1536, 1792, 2048, 2304, 2560
WINDOWS = (2, 4, 8, 16)


N_CONST, N_CONST2 = 7, 7


def gla_chunk(n, d):
    if n < NGC:
        return NGC + n if d == 0 else 2 * NGC - 1 - n
    return n - NGC if d == 0 else 2 * NGC - 1 - n


def attn_list(layer):
    return [(layer, src, kind, tt, h) for src in ((0, 1) if layer == 0 else (0,))
            for kind, heads in (("a", 8), ("n", 4)) for tt in range(NT) for h in range(heads)]


ATTN_ALL = attn_list(0) + attn_list(1)
ATTN_GROUPS = list(dict.fromkeys(a[:4] for a in ATTN_ALL))


def attn_index(a):
    return ATTN_ALL.index(a)


def attn_group(*g):
    return ATTN_GROUPS.index(g)


def qk_pairs(layer, src):
    ps = [("aqT", h, AQ + 64 * h) for h in range(0, 8, 2)] + [("akT", 0, AK)]
    ps += [("nqT", h, NQ + 64 * h) for h in (0, 2)] + [("nkT", h, NK + 64 * h) for h in (0, 2)]
    if layer == 1 and src == 1:
        ps = [q for q in ps if q[0] in ("akT", "nkT")]
    return ps


def norm_groups(layer, src):
    gs = [(AQ, 8, "aq"), (AK, 2, "ak"), (NQ, 4, "nq"), (NK, 4, "nk")]
    if layer == 1 and src == 1:
        gs = [g for g in gs if g[2] in ("ak", "nk")]
    return gs


def n_norms(layer, src):
    return NT * sum(g[1] for g in norm_groups(layer, src))


def z_tiles(layer, src):
    return (2, 8, 9) if layer == 1 and src == 1 else tuple(range(N_IN2))


class Layout:
    def __init__(self):
        self.at, self.n = {}, 0

    def add(self, name, n):
        self.at[name] = (self.n, n)
        self.n += n

    def __getitem__(self, name):
        o, n = self.at[name]
        return slice(o, o + n)


def layouts():
    a, b, c, v, r1, r2 = (Layout() for _ in range(6))
    for n, w in (("ident", P), ("ones", P), ("zero", P), ("iota", P)):
        a.add(n, w)
    for n, w in (("tri_ml", 2 * 256), ("tri_gla", 2 * P), ("sel", HEADS * P), ("reset", 2 * T), ("half", 2)):
        b.add(n, w)
    for n, w in (("cos", NT * 64), ("sin", NT * 64), ("namask", GRID)):
        c.add(n, w)
    for n, w in (("cond", 4 * C), ("bmod1", 48), ("bmod2", 48), ("norm1", C), ("norm2", C), ("normg2", 2 * C),
                 ("conv", 3 * C), ("alpha_b", 4), ("gate_b", 4)):
        v.add(n, w)
    for n, w in (("ml_g", 512), ("gla_g", 512)):
        r1.add(n, w)
    for layer in range(2):
        for n, w in ((f"aq{layer}", 64), (f"ak{layer}", 64), (f"nq{layer}", 64), (f"nk{layer}", 64),
                     (f"pool{layer}", 256)):
            r2.add(n, w)
    return a, b, c, v, r1, r2


def constants():
    a, b, c, _, _, _ = layouts()
    A = np.zeros((P, a.n), np.float32)
    A[:, a["ident"]] = np.eye(P)
    A[:, a["ones"]] = 1
    A[:, a["iota"]] = np.arange(P)
    B = np.zeros((P, b.n), np.float32)
    s, t = np.arange(P)[:, None], np.arange(P)[None, :]
    fwd = np.where(t >= s, 0, NEG)
    bwd = np.where(t <= s, 0, NEG)
    B[:, b["tri_ml"]] = np.concatenate([fwd, fwd, bwd, bwd], 1)
    same = s // GC == t // GC
    B[:, b["tri_gla"]] = np.concatenate([(same & (t >= s)), (same & (t <= s))], 1)
    for h in range(HEADS):
        B[h, b["sel"].start + h * P:b["sel"].start + (h + 1) * P] = 1
    B[:, b["reset"]] = (np.arange(2 * T) % GC != 0)
    B[:, b["half"]] = np.concatenate([s < GC, s >= GC], 1)
    Cc = np.zeros((P, c.n), np.float32)
    inv = (10000.0 ** (-np.arange(16, dtype=np.float32) / np.float32(16))).astype(np.float32)
    for tt in range(NT):
        tok = tt * P + np.arange(P)
        ar, ac = (tok // GRID).astype(np.float32)[:, None] * inv, (tok % GRID).astype(np.float32)[:, None] * inv
        o = c["cos"].start + tt * 64
        Cc[:, o:o + 64] = np.concatenate([np.cos(ar), np.cos(ar), np.cos(ac), np.cos(ac)], 1)
        o = c["sin"].start + tt * 64
        Cc[:, o:o + 64] = np.concatenate([-np.sin(ar), np.sin(ar), -np.sin(ac), np.sin(ac)], 1)
    qc = (np.arange(P) % GRID)[:, None]
    c0 = np.clip(qc - 8, 0, GRID - 16)
    kc = np.arange(GRID)[None, :]
    Cc[:, c["namask"]] = np.where((kc >= c0) & (kc < c0 + 16), 0, NEG)
    pool = np.zeros((NT, P, 4, T), np.float32)
    for g, w in enumerate(WINDOWS):
        for tq in range(T):
            lo, hi = max(tq - w // 2, 0), min(tq + w // 2 - 1, T - 1)
            col = np.zeros(T, np.float32)
            col[lo:hi + 1] = np.float32(1) / np.float32(hi - lo + 1)
            col[tq] -= 1
            pool[:, :, g, tq] = col.reshape(NT, P)
    return A, B, Cc, np.ascontiguousarray(pool.transpose(1, 0, 2, 3).reshape(P, NT * 4 * T))


def build(nc, W, CA, CB, CC, POOL, VEC, ROW1, NORMF, ROW2, LRW2, POOLW, X, CTX, CTX2, RPB, OUT):
    la, lb, lc, lv, lr1, lr2 = layouts()
    with ExitStack() as ctx:
        def sb(name, shape):
            return ctx.enter_context(nc.sbuf_tensor(name, shape, F32))

        sems = {}

        def S(name):
            if name not in sems:
                sems[name] = ctx.enter_context(nc.semaphore(name))
            return sems[name]

        cA = sb("cA", [P, la.n])
        vec = sb("vec", [P, lv.n])
        x = sb("x", [P, NT, D])
        h2T = sb("h2T", [P, C, T])
        ring_at = nc.sbuf_base
        ring = sb("ring", [P, WSLOTS, WT])
        cond = sb("cond", [P, C, 4])
        condt = sb("condt", [P, C, 4])
        mod1 = sb("mod1", [P, 48, 2])
        mod2 = sb("mod2", [P, 2, 24, 2])
        gain = sb("gain", [P, 5, C])
        rs = sb("rs", [P, 6, 80])
        tiny = sb("tiny", [P, 6, 16])
        AR = 39000
        arena_at = nc.sbuf_base
        arena = sb("arena", [P, AR])
        banks = [ctx.enter_context(nc.psum_tensor(f"bank{i}", [P, 512], F32)) for i in range(8)]
        ident = cA[:, la["ident"]]
        ones = cA[:, la["ones"]]
        zero = cA[:, la["zero"]]
        iota = cA[:, la["iota"]]

        cursor = [0]

        def shaped(ap, shape):
            if len(shape) == 2:
                return ap.rearrange("p (a b) -> p a b", a=shape[0])
            if len(shape) == 3:
                return ap.rearrange("p (a b c) -> p a b c", a=shape[0], b=shape[1])
            if len(shape) == 4:
                return ap.rearrange("p (a b c d) -> p a b c d", a=shape[0], b=shape[1], c=shape[2])
            return ap

        def region(off, *shape):
            n = int(np.prod(shape))
            assert off + n <= AR, (off, n)
            return shaped(arena[:, off:off + n], shape)

        def bump(*shape):
            r = region(cursor[0], *shape)
            cursor[0] += int(np.prod(shape))
            return r

        cB = bump(lb.n)
        row1 = bump(lr1.n)
        cq = bump(HEADS, T)
        ck = bump(HEADS, 2 * T)
        vml = bump(4, HEADS, P + 1)
        og = bump(NT, D)
        gqT = bump(2, T)
        gkT = bump(2, 2 * T)
        gv = bump(4, 512)
        glrT = bump(2, 2 * T)
        lrw2 = bump(2, 256)
        base = cursor[0]
        hT = bump(C, 2 * T)
        EW, PW = region(base, 2, 4, T), region(base + 2048, 2, 4, T)
        xn = bump(4, D)
        es, ogt = region(base + 4096, 3072), region(base + 7168, NT, D)
        cx = bump(NT, D)
        gi = bump(2, 2 * T)
        gf = bump(2, 2 * T)
        gtmp = bump(2, 2 * T)
        gb = bump(2, 2 * T)
        negA = bump(2, 2 * T)
        nM = bump(2, 2 * T)
        em = bump(2, T)
        acol = bump(4, 2, HEADS)
        emcol = bump(NT, 2, HEADS)
        dn = bump(4, NT)
        sqj = bump(D)
        cursor[0] = base
        lt = bump(2, 2, 2 * T)
        lx = bump(2, 2, 2 * T)
        lbm = bump(2, 2, 2 * T)
        qz = bump(2, 2, 2, T)
        kz = bump(2, 2, T)
        qs = bump(2, 2, 2, T)
        kdn = bump(2, 4, 2, 256)
        att = bump(2, HEADS, P)
        Sst = bump(2, NGC, 2, 256)
        Sct = bump(2, 2, 2, 256)
        eend = bump(2, 2, 8)
        hcat = shaped(h2T[:, :, :].rearrange("p c t -> p (c t)"), (NT, D))
        assert cursor[0] <= AR - 1024
        modrow = region(AR - 1024, 2, 512)
        cursor[0] = base
        mix = bump(NT, D)
        mixT = bump(C, T)
        gbc = bump(D)
        sq2 = bump(D)
        ytmp = bump(NT, WC)
        diag = bump(C, P)
        xn2 = bump(NT, D)
        GH = region(0, P, T)
        cursor[0] = 64 * T
        qTp = bump(16, T)
        cand, work = region(64 * T, PH, 256), region(64 * T + 2048, 256)
        sc = bump(NT, 16, PK)
        tops = bump(NT, 16, TOPK)
        topi = bump(NT, 16, TOPK)
        topf = bump(NT, 16, TOPK)
        bests = bump(NT, PH, TOPK)
        bestc = bump(NT, PH, TOPK)
        bhl = bump(2, PH, TOPK)
        onek = bump(PH, TOPK, TOPK)
        smx = bump(4, 16)
        sels = bump(NT, 3, P)
        assert cursor[0] <= P * T
        cursor[0] = P * T
        peT = h2T
        def parts(name, at, *shape):
            return nc.alloc_sbuf_tensor_at(name, [P] + list(shape), F32R, offset=at)

        w_rest = parts("w_rest", ring_at, WSLOTS, WT)
        w_high = parts("w_high", arena_at + 4 * cursor[0], 2, HALF)
        dif = bump(2, 4, P)
        cursor[0] += 2 * HALF - 2 * 4 * P
        h2_high = parts("h2_high", arena_at + 4 * cursor[0], C, T)
        g_high = parts("g_high", arena_at + 4 * cursor[0], 2, 2, T)
        g_rest = parts("g_rest", arena_at + 4 * cursor[0] + 4096, 2, 2, T)
        oh = bump(2, 2, 4, P)
        h2_rest = parts("h2_rest", arena_at + 4 * cursor[0], C, T)
        selT = bump(3, T)
        cursor[0] += C * T - 3 * T
        assert cursor[0] <= AR
        cursor[0] = 0
        hT2, mixT3 = region(0, C, 2 * T), region(0, 2, C, T)
        aqT = bump(8, T)
        akT = bump(2, 2 * T)
        nqT = bump(4, T)
        nkT = bump(4, 2 * T)
        c2 = bump(NT, D)
        z = bump(4, IN2)
        xn3 = bump(4, D)
        mix3 = xn3
        rt = bump(2, 640)
        ytmp2 = shaped(rt[:, 0, 0:512], (NT, WC))
        pw = bump(2, 512)
        pt = bump(2, 4, P)
        diag2 = region(cursor[0] - 2048, C, P)
        plT = bump(4, T)
        braw = bump(NT, HEADS, T)
        bm = bump(NT, HEADS, T)
        poolc = bump(NT, 4, T)
        row2 = bump(lr2.n)
        normf = bump(D)
        plw = bump(2, 4, 64)
        cC = bump(lc.n)
        g2b = bump(2, D)

        units, order, emptied_n = {}, [], {"dve": 0, "act": 0}
        tiles_n, before_peer = [0], {}

        def stored(eng, key):
            u = units[key]
            eng.wait_ge(S("emptied_" + u["by"]), u["idx"] + 1)

        def take(eng, key):
            u = units[key]
            eng.wait_ge(S(u["sem"]), u["val"])
            return banks[u["bank"]]

        freed = {"dve": 0, "act": 0}

        def free(ins, key):
            u = units[key]
            assert freed[u["by"]] == u["idx"], (key, freed, u)
            freed[u["by"]] += 1
            ins.then_inc(S("emptied_" + u["by"]), 1)

        def w3(w):
            return w.rearrange("p (c n) -> p c n", c=C)

        block = ctx.enter_context(nc.Block())

        @block.tensor
        def _(pe):
            opened = [None]

            def qk_transpose(layer, src, n, col):
                bank = open_unit(("qk", layer, src, n), "act" if n % 2 else "dve")
                for k in range(2):
                    for tt in range(NT):
                        last = pe.transpose(bank[0:64, k * T + tt * P:k * T + tt * P + P],
                                            z[:, 2 * src + tt, col + 64 * k:col + 64 * k + 64], ident)
                close_unit(last)

            def open_unit(key, by):
                n = len(order)
                if n >= NB:
                    stored(pe, order[n - NB])
                assert opened[0] is None
                opened[0] = key
                units[key] = dict(bank=n % NB, by=by, idx=emptied_n[by])
                emptied_n[by] += 1
                order.append(key)
                return banks[n % NB]

            filled = [0]

            def close_unit(ins, weights=False):
                u = units[opened[0]]
                opened[0] = None
                if weights:
                    u["sem"], u["val"] = "tile_used", tiles_n[0]
                    ins.then_inc(S("tile_used"), 1)
                else:
                    filled[0] += 1
                    u["sem"], u["val"] = "unit_filled", filled[0]
                    ins.then_inc(S("unit_filled"), 1)

            def weights():
                n = tiles_n[0]
                tiles_n[0] += 1
                pe.wait_ge(S(f"tile_landed{n % WSLOTS}"), 16 * (n // WSLOTS + 1))
                return ring[:, n % WSLOTS, :]

            def mm(out, lhsT, rhs, c=0, n=1):
                return pe.matmul(out, lhsT=lhsT, rhs=rhs, start=(c == 0), stop=(c == n - 1))

            mod_at = [0]

            def modulation(n=1):
                for _ in range(n):
                    u = mod_at[0]
                    if u == MOD_UNITS:
                        return
                    mod_at[0] += 1
                    lo = 0 if u < N_MOD1 // 2 else 2
                    bank = open_unit(("modrow", u), "act")
                    for k in range(2):
                        w = w3(weights())
                        for c in range(C):
                            last = mm(bank[0:2, k * WC:(k + 1) * WC], cond[:, c, lo:lo + 2], w[:, c, :], c, C)
                        if k == 0:
                            last.then_inc(S("tile_used"), 1)
                    close_unit(last, weights=True)
                    if u not in (0, MOD_FIRST):
                        mod_columns(u - 1)
                    if u in (MOD_FIRST - 1, MOD_UNITS - 1):
                        mod_columns(u)

            def mod_columns(u):
                stored(pe, ("modrow", u))
                for k in range(4):
                    o = (4 * u + k) * 2
                    last = pe.transpose(banks[7][:, o:o + 2], modrow[0:2, u % 2, k * P:(k + 1) * P], ident[0:2, 0:2])
                last.then_inc(S("mod_columns"), 1)

            def transposed(key, src_tiles, by):
                for cc in range(4):
                    bank = open_unit(key + (cc,), by)
                    for k in range(2):
                        for tt in range(NT):
                            last = pe.transpose(bank[:, k * T + tt * P:k * T + tt * P + P],
                                                src_tiles[tt][:, (2 * cc + k) * P:(2 * cc + k + 1) * P], ident)
                    close_unit(last)

            def rows_of(key, hsrc, cols, w, by, weights=False):
                bank = open_unit(key, by)
                for tt in range(NT):
                    for c in range(C):
                        last = mm(bank[:, tt * WC:(tt + 1) * WC], hsrc[:, c, cols + tt * P:cols + tt * P + P],
                                  w[:, c, :], c, C)
                close_unit(last, weights)

            pe.wait_ge(S("const_loaded"), 16 * N_CONST)
            pe.wait_ge(S("cond_ready"), 1)
            modulation(MOD_FIRST)

            for src in range(2):
                pe.wait_ge(S("xn_ready"), 2 * src + 2)
                transposed(("hT", src), [xn[:, 2 * src + tt, :] for tt in range(NT)], "dve")
            stored(pe, ("hT", 1, 3))

            w = w3(weights())
            for d in range(2):
                for g in range(2):
                    bank = open_unit(("gate", d, g), "dve")
                    for c in range(C):
                        last = mm(bank[0:HEADS, :], w[:, c, d * 8 + g * 4:d * 8 + g * 4 + 4], hT[:, c, :], c, C)
                    close_unit(last)
            for d in range(2):
                bank = open_unit(("glr", d), "act")
                for c in range(C):
                    last = mm(bank[0:GRANK, :], w[:, c, 16 + d * GRANK:16 + (d + 1) * GRANK], hT[:, c, :], c, C)
                close_unit(last, weights=(d == 1))
            for i in range(2):
                w = w3(weights())
                bank = open_unit(("mq", i), "dve")
                for k in range(2):
                    for c in range(C):
                        last = mm(bank[:, k * T:(k + 1) * T], w[:, c, k * P:(k + 1) * P], hT[:, c, 0:T], c, C)
                close_unit(last, weights=True)
            for i in range(2):
                w = w3(weights())
                for k in range(2):
                    bank = open_unit(("mk", 2 * i + k), "dve")
                    for c in range(C):
                        last = mm(bank[:, :], w[:, c, k * P:(k + 1) * P], hT[:, c, :], c, C)
                    close_unit(last, weights=(k == 1))
            for i in range(2):
                w = w3(weights())
                rows_of(("mv", i, 0), hT, 0, w, "act")
                rows_of(("mv", i, 1), hT, T, w, "act", weights=True)
            for i in range(2):
                rows_of(("mo", i), hT, 0, w3(weights()), "act", weights=True)
            w = w3(weights())
            bank = open_unit(("gq",), "act")
            for k in range(2):
                for c in range(C):
                    last = mm(bank[:, k * T:(k + 1) * T], w[:, c, k * P:(k + 1) * P], hT[:, c, 0:T], c, C)
            close_unit(last, weights=True)
            w = w3(weights())
            for k in range(2):
                bank = open_unit(("gk", k), "act")
                for c in range(C):
                    last = mm(bank[:, :], w[:, c, k * P:(k + 1) * P], hT[:, c, :], c, C)
                close_unit(last, weights=(k == 1))
            for i in range(2):
                w = w3(weights())
                rows_of(("gv", i, 0), hT, 0, w, "act")
                rows_of(("gv", i, 1), hT, T, w, "act", weights=True)
            for i in range(2):
                rows_of(("gr", i), hT, 0, w3(weights()), "act", weights=True)
            modulation(MOD_LATER["gr"])

            pe.wait_ge(S("gate_rows_ready"), 1)
            bank = open_unit(("acol",), "dve")
            for d in range(2):
                for st in range(4):
                    o = (st * 2 + d) * HEADS
                    last = pe.transpose(bank[:, o:o + HEADS], negA[0:HEADS, d, st * P:(st + 1) * P],
                                        ident[0:HEADS, 0:HEADS])
            close_unit(last)
            pe.wait_ge(S("em_ready"), 1)
            bank = open_unit(("emcol",), "dve")
            for d in range(2):
                for tt in range(NT):
                    o = (tt * 2 + d) * HEADS
                    last = pe.transpose(bank[:, o:o + HEADS], em[0:HEADS, d, tt * P:(tt + 1) * P],
                                        ident[0:HEADS, 0:HEADS])
            close_unit(last)
            pe.wait_ge(S("conv_ready"), 1)
            for h in range(HEADS):
                sel_h = cB[0:HEADS, lb["sel"].start + h * P:lb["sel"].start + (h + 1) * P]
                for src in range(2):
                    bank = open_unit(("S", h, src), "dve")
                    for st in range(2):
                        last = mm(bank[:, st * T:(st + 1) * T], ck[:, h, src * T + st * P:src * T + (st + 1) * P],
                                  cq[:, h, :])
                    close_unit(last)
                for d in range(2):
                    bank = open_unit(("E", h, d), "act")
                    mm(bank[:, 0:T], sel_h, nM[0:HEADS, d, 0:T])
                    pe.matmul(bank[:, T:2 * T], lhsT=sel_h, rhs=nM[0:HEADS, d, 0:T], start=True, stop=False)
                    o = lb["tri_ml"].start + d * T
                    close_unit(pe.matmul(bank[:, T:2 * T], lhsT=ident, rhs=cB[:, o:o + T], start=False, stop=True))
                for d in range(2):
                    bank = open_unit(("O", h, d), "dve")
                    pe.wait_ge(S("P_ready"), 2 * h + d + 1)
                    for tt in range(NT):
                        sts = [2, 3] + [s for s in range(2) if (s <= tt if d == 0 else s >= tt)]
                        for n, st in enumerate(sts):
                            last = mm(bank[:, tt * 256:tt * 256 + P + 1], PW[:, d, st, tt * P:(tt + 1) * P],
                                      vml[:, st, h, :], n, len(sts))
                    close_unit(last)
                modulation(MOD_LATER["mlstm"])

            for d in range(2):
                for j in range(2):
                    bank = open_unit(("alpha", d, j), "dve")
                    close_unit(mm(bank[:, :], lrw2[0:GRANK, d, j * P:(j + 1) * P], glrT[0:GRANK, d, :]))
            modulation(MOD_LATER["alpha"])
            pe.wait_ge(S("kdec_ready"), 1)
            for d in range(2):
                for src in range(2):
                    bank = open_unit(("kdn", d, src), "dve")
                    for tt in range(NT):
                        for j in range(2):
                            o = tt * 256 + j * P
                            last = pe.transpose(bank[:, o:o + P],
                                                lx[:, d, j, src * T + tt * P:src * T + (tt + 1) * P], ident)
                    close_unit(last)
            modulation(MOD_LATER["kdn"])
            for step in range(7):
                for d in range(2):
                    c = gla_chunk(step, d)
                    bank = open_unit(("St", step, d), "dve")
                    if step == 0:
                        stored(pe, ("kdn", 1, 1))
                    for j in range(2):
                        last = mm(bank[:, j * 256:(j + 1) * 256], kdn[:, d, c // 2, c % 2, j * P:(j + 1) * P],
                                  gv[:, c // 2, j * 256:(j + 1) * 256])
                    close_unit(last)
                modulation(MOD_LATER["state"])
            pe.wait_ge(S("gla_q_ready"), 1)
            for tt in range(NT):
                for d in range(2):
                    bank = open_unit(("att", tt, d), "dve")
                    for h in range(HEADS):
                        last = mm(bank[:, h * P:(h + 1) * P], kz[:, d, h // 2, tt * P:(tt + 1) * P],
                                  qz[:, d, h % 2, h // 2, tt * P:(tt + 1) * P])
                    close_unit(last)
                bank = open_unit(("gla", tt), "dve")
                stored(pe, ("att", tt, 1))
                for h in range(HEADS):
                    for d in range(2):
                        mm(bank[:, h * P:(h + 1) * P], att[:, d, h, :], gv[:, tt, h * P:(h + 1) * P], d, 99)
                    for d in range(2):
                        for par in range(2):
                            last = mm(bank[:, h * P:(h + 1) * P], qs[:, d, par, h // 2, tt * P:(tt + 1) * P],
                                      Sst[:, d, 2 * tt + par, h // 2, (h % 2) * P:(h % 2 + 1) * P],
                                      3 if d and par else 1, 4)
                close_unit(last)

            modulation(MOD_UNITS)

            pe.wait_ge(S("diag_ready"), 1)
            for half in range(2):
                bank = open_unit(("gbc", half), "act")
                close_unit(mm(bank[:, :], ones, diag[:, 4 * half:4 * half + 4, :]))
            pe.wait_ge(S("mix_ready"), 1)
            transposed(("mixT",), [mix[:, tt, :] for tt in range(NT)], "act")
            stored(pe, ("mixT", 3))
            for i in range(N_OUT):
                rows_of(("y", i), mixT, 0, w3(weights()), "dve", weights=True)

            pe.wait_ge(S("xn_ready"), 6)
            transposed(("h2T",), [xn2[:, tt, :] for tt in range(NT)], "dve")
            stored(pe, ("h2T", 3))
            for i in range(N_WQ):
                w = w3(weights())
                bank = open_unit(("wq", i), "act")
                for k in range(2):
                    for c in range(C):
                        last = mm(bank[:, k * T:(k + 1) * T], w[:, c, k * P:(k + 1) * P], h2T[:, c, :], c, C)
                close_unit(last, weights=True)
            keys = weights().rearrange("p (a b) -> p a b", a=16)
            stored(pe, ("wq", N_WQ - 1))
            for tt in range(NT):
                for q in range(4):
                    bank = open_unit(("sc", tt, q), "act")
                    for k in range(4):
                        last = mm(bank[:, k * P:(k + 1) * P], qTp[:, 4 * q + k, tt * P:(tt + 1) * P],
                                  keys[:, 4 * q + k, :])
                    close_unit(last, weights=(tt == 1 and q == 3))
            assert tiles_n[0] == N_PRE and N_PRE % WSLOTS == 0

            before_peer.update(emptied_n)
            pe.wait_ge(S("emptied_dve"), emptied_n["dve"])
            pe.wait_ge(S("emptied_act"), emptied_n["act"])

            def three(out, highs, rests, wh, wr, idx, first):
                pe.wait_ge(S("w_high_ready"), idx)
                for c in range(C):
                    pe.matmul(out(c), lhsT=wh[:, c, :], rhs=highs(c), start=(first and c == 0), stop=False,
                              skip_group_check=True)
                    last = pe.matmul(out(c), lhsT=wh[:, c, :], rhs=rests(c), start=False, stop=False,
                                     skip_group_check=True)
                last.then_inc(S("w_high_used"), 1)
                pe.wait_ge(S("w_rest_ready"), idx)
                for c in range(C):
                    last = pe.matmul(out(c), lhsT=wr[:, c, :], rhs=highs(c), start=False, stop=(first and c == C - 1),
                                     skip_group_check=True)
                return last

            def experts(first, split, split_before):
                with pe.Fori(0, U_HALF) as it:
                    for k in range(WSLOTS):
                        landed = pe.snap(it * 16 + 16 * ((N_PRE + first) // WSLOTS + 1))
                        free_n = pe.snap(it * WSLOTS + first + k + 1)
                        idx = [pe.snap(it * (2 * len(split)) + split_before + 2 * split.index(k) + a + 1)
                               for a in range(2)] if k in split else None
                        pe.wait_ge(S(f"tile_landed{k}"), landed)
                        pe.wait_ge(S("u_bank_free"), free_n)
                        w = ring[:, k, :].rearrange("p (a c n) -> p a c n", a=2, c=C)
                        wr = w_rest[:, k, :].rearrange("p (a c n) -> p a c n", a=2, c=C)
                        for a in range(2):
                            out = banks[k][:, a * T:(a + 1) * T]
                            if k in split:
                                last = three(lambda c: out, lambda c: h2_high[:, c, :], lambda c: h2_rest[:, c, :],
                                             w_high[:, a, :].rearrange("p (c n) -> p c n", c=C), wr[:, a], idx[a],
                                             True)
                            else:
                                for c in range(C):
                                    last = mm(out, w[:, a, c, :], h2T[:, c, :], c, C)
                        last.then_inc(S("tile_used"), 1)

            pe.wait_ge(S("h2_rest_ready"), 1)
            experts(0, SPLIT1, 0)
            pe.wait_ge(S("topk_done"), 1)
            for f in range(3):
                for tt in range(NT):
                    o = (f % 2) * T + tt * P
                    last = pe.transpose(banks[6 + f // 2][:, o:o + P], sels[:, tt, f, :], ident)
            last.then_inc(S("selT_filled"), 1)
            experts(N_PEER // 2, tuple(range(WSLOTS)), N_SPLIT1)

            with pe.Fori(0, T // 8) as it:
                for b in range(2):
                    n = pe.snap(it * 2 + b + 1)
                    pe.wait_ge(S("oh_ready"), n)
                    pe.wait_ge(S("oh2_ready"), n)
                    pe.wait_ge(S("w_bank_free"), n)
                    for k in range(4):
                        last = mm(banks[4 + b][:, k * P:(k + 1) * P], oh[:, b, 0, k, :], oh[:, b, 1, k, :])
                    last.then_inc(S("w_filled"), 1)

            pe.wait_ge(S("w_bank_free"), 2 + T // 4)
            for k in range(4):
                pe.matmul(banks[k][:, :], lhsT=zero, rhs=h2T[:, 0:2, :], start=True, stop=False,
                          skip_group_check=True)
            with pe.Fori(0, N_PEER // WSLOTS) as it:
                for k in range(WSLOTS):
                    g_n = pe.snap(it * WSLOTS + k + 1)
                    idx = [pe.snap(it * (2 * WSLOTS) + N_SPLIT2 + 2 * k + a + 1) for a in range(2)]
                    wr = w_rest[:, k, :].rearrange("p (a c n) -> p a c n", a=2, c=C)
                    pe.wait_ge(S("g_rest_ready"), g_n)
                    for a in range(2):
                        last = three(lambda c: banks[c // 2][:, (c % 2) * T:(c % 2 + 1) * T],
                                     lambda c: g_high[:, k % 2, a, :], lambda c: g_rest[:, k % 2, a, :],
                                     w_high[:, a, :].rearrange("p (c n) -> p c n", c=C), wr[:, a], idx[a], False)
                    last.then_inc(S("tile_used"), 1)
            tiles_n[0] = N_PRE + 2 * N_PEER
            pe.wait_ge(S("peT_ready"), 1)
            for tt in range(NT):
                for half in range(2):
                    bank = open_unit(("pe", tt, half), "dve")
                    for k in range(4):
                        last = pe.transpose(bank[:, k * P:(k + 1) * P], peT[:, 4 * half + k, tt * P:(tt + 1) * P],
                                            ident)
                    close_unit(last)

            pe.wait_ge(S("const2_loaded"), 16 * N_CONST2)
            n_xn, n_attn, n_gap = 6, 0, 0
            for layer in range(2):
                for src in range(2):
                    n_xn += 2
                    pe.wait_ge(S("xn_ready"), n_xn)
                    transposed(("hT2", layer, src), [xn3[:, 2 * src + tt, :] for tt in range(NT)], "dve")
                stored(pe, ("hT2", layer, 1, 3))
                for i in range(N_IN2):
                    w = w3(weights())
                    two = i in z_tiles(layer, 1)
                    rows_of(("z", layer, i, 0), hT2, 0, w, "act", weights=not two)
                    if two:
                        rows_of(("z", layer, i, 1), hT2, T, w, "dve", weights=True)
                for src in range(2):
                    pe.wait_ge(S("qk_ready"), 2 * layer + src + 1)
                    if src == 1:
                        continue
                    for n, (buf, h, col) in enumerate(qk_pairs(layer, src)):
                        qk_transpose(layer, src, n, col)
                for n, (buf, h, col) in enumerate(qk_pairs(layer, 1)):
                    if buf in ("akT", "nkT"):
                        qk_transpose(layer, 1, n, col)
                todo = attn_list(layer)
                for part in range(1 if layer else 2):
                    mine = [a for a in todo if a[1] == part]
                    if part == 1:
                        for n, (buf, h, col) in enumerate(qk_pairs(layer, 1)):
                            if buf in ("aqT", "nqT"):
                                qk_transpose(layer, 1, n, col)
                    stored(pe, [k for k in order if k[0] == "qk" and units[k]["by"] == "act"][-1])
                    stored(pe, [k for k in order if k[0] == "qk" and units[k]["by"] == "dve"][-1])
                    if part == 0:
                        pe.wait_ge(S("bias_ready"), layer + 1)

                    def scores(a):
                        _, src, kind, tt, h = a
                        lo, n = (0, 512) if src == 0 else (T, T)
                        q, k = (aqT[0:64, h, :], akT[0:64, h // 4, :]) if kind == "a" else \
                               (nqT[0:64, h, :], nkT[0:64, h, :])
                        bank = open_unit(("s",) + a, "act")
                        biased = kind == "n" and src == 0
                        last = pe.matmul(bank[:, 0:n], lhsT=q[:, tt * P:(tt + 1) * P], rhs=k[:, lo:lo + n],
                                         start=True, stop=not biased)
                        if biased:
                            last = pe.matmul(bank[:, 0:T], lhsT=ident, rhs=bm[:, tt, h, :], start=False, stop=True)
                        close_unit(last)

                    scores(mine[0])
                    scores(mine[1])
                    for i, a in enumerate(mine):
                        _, src, kind, tt, h = a
                        nst = 4 if src == 0 else 2
                        bank = open_unit(("t",) + a, "dve")
                        stored(pe, ("s",) + a)
                        for st in range(nst):
                            last = pe.transpose(bank[:, st * P:(st + 1) * P], pw[:, (n_attn + i) % 2,
                                                st * P:(st + 1) * P], ident)
                        close_unit(last)
                        if i + 2 < len(mine):
                            scores(mine[i + 2])
                        stored(pe, ("t",) + a)
                        if h == 0 and n_gap >= 2:
                            pe.wait_ge(S("att_free"), n_gap - 1)
                        v0 = AV + (h // 4) * 64 if kind == "a" else NV + h * 64
                        for st in range(nst):
                            zt = st if src == 0 else 2 + st
                            last = mm(banks[6 + n_gap % 2][:, h * 64:(h + 1) * 64], pt[:, (n_attn + i) % 2, st, :],
                                      z[:, zt, v0:v0 + 64], st, nst)
                        if h == (7 if kind == "a" else 3):
                            last.then_inc(S("att_filled"), 1)
                            n_gap += 1
                    n_attn += len(mine)
                    src = part
                    for gp in range(2):
                        bank = open_unit(("pl", layer, src, gp), "dve")
                        for k in range(2):
                            g = 2 * gp + k
                            for st in range(NT):
                                last = mm(bank[0:64, k * T:(k + 1) * T],
                                          z[:, 2 * src + st, BZ + g * 64:BZ + (g + 1) * 64],
                                          poolc[:, st, g, :], st, NT)
                        close_unit(last)
                    bank = open_unit(("py", layer, src), "dve")
                    stored(pe, ("pl", layer, src, 1))
                    for tt in range(NT):
                        for g in range(4):
                            o = tt * T + g * 64
                            last = mm(bank[:, o:o + 64], plT[0:64, g, tt * P:(tt + 1) * P], plw[0:64, layer, g, :])
                    close_unit(last)
                srcs = (0, 1) if layer == 0 else (0,)
                for src in srcs:
                    pe.wait_ge(S("diag_ready"), 2 + 2 * layer + src)
                    for half in range(2):
                        bank = open_unit(("gb", layer, src, half), "act")
                        close_unit(mm(bank[:, :], ones, diag2[:, 4 * half:4 * half + 4, :]))
                    pe.wait_ge(S("mix_ready"), 2 + 2 * layer + src)
                    transposed(("mT", layer, src), [mix3[:, 2 * src + tt, :] for tt in range(NT)], "act")
                stored(pe, ("mT", layer, srcs[-1], 3))
                for i in range(N_OUT):
                    w = w3(weights())
                    for src in srcs:
                        rows_of(("y2", layer, i, src), mixT3[:, src], 0, w, "dve", weights=(src == srcs[-1]))
            assert tiles_n[0] == N_TILES

        @block.sync
        def _(sp):
            def fetch(row, k):
                sp.dma_start(ring[:, k, :], W[row]).then_inc(S(f"tile_landed{k}"), 16)

            for k in range(WSLOTS):
                fetch(k, k)
            rounds = (N_TILES - WSLOTS) // WSLOTS
            with sp.Fori(0, rounds) as it:
                for k in range(WSLOTS):
                    row = sp.snap(it * WSLOTS + WSLOTS + k)
                    used = sp.snap(it * WSLOTS + k + 1)
                    sp.wait_ge(S("tile_used"), used)
                    fetch(row, k)
            for n in range(WSLOTS * (rounds + 1), N_TILES):
                sp.wait_ge(S("tile_used"), n - WSLOTS + 1)
                fetch(n, n % WSLOTS)
            sp.wait_ge(S("x_final"), 1)
            sp.dma_start(OUT.rearrange("b (t p) d -> p (b t) d", p=P), x[:, :, :]).then_inc(S("out_done"), 16)
            sp.wait_ge(S("out_done"), 16)

        @block.gpsimd
        def _(pool):
            nc.gpsimd.memset(vml[:, :, :, P:P + 1], 1.0).then_inc(S("vml_ones"), 1)
            pool.wait_ge(S("mlstm_done"), 1)
            nc.gpsimd.memset(qz, 0.0).then_inc(S("gla_zero"), 1)
            nc.gpsimd.memset(qs, 0.0).then_inc(S("gla_zero"), 1)
            nc.gpsimd.memset(att, 0.0).then_inc(S("gla_zero"), 1)
            nc.gpsimd.memset(Sst, 0.0).then_inc(S("gla_zero"), 1)
            with pool.Fori(0, U_HALF) as it:
                for j, k in enumerate(SPLIT1):
                    for a in range(2):
                        n = pool.snap(it * (2 * len(SPLIT1)) + 2 * j + a + 1)
                        half = slice(a * HALF, (a + 1) * HALF)
                        pool.wait_ge(S("w_high_ready"), n)
                        nc.gpsimd.tensor_tensor(w_rest[:, k, half], ring[:, k, half], w_high[:, a, :].bitcast(F32),
                                                ALU.subtract).then_inc(S("w_rest_ready"), 1)
            pool.wait_ge(S("selT_stored"), 1)

            def differences(b, col):
                nc.gpsimd.tensor_tensor(dif[:, b], iota.unsqueeze(1).to_broadcast([P, 4, P]),
                                        selT[:, 1, bass.ds(col, 4)].unsqueeze(2).to_broadcast([P, 4, P]),
                                        ALU.subtract).then_inc(S("dif_ready"), 1)

            for b in range(2):
                differences(b, 4 * b)
            with pool.Fori(0, T // 8 - 1) as it:
                for b in range(2):
                    n = pool.snap(it * 2 + b + 1)
                    col = pool.snap(it * 8 + 8 + 4 * b)
                    pool.wait_ge(S("oh2_ready"), n)
                    differences(b, col)
            pool.wait_ge(S("peT_ready"), 1)
            c2n = S("const2_loaded")
            pool.dma_start(normf, NORMF.partition_broadcast(P)).then_inc(c2n, 16)
            pool.dma_start(c2, CTX2.rearrange("b (t p) d -> p (b t) d", p=P)).then_inc(c2n, 16)
            pool.dma_start(poolc.rearrange("p a b c -> p (a b c)"), POOL).then_inc(c2n, 16)
            pool.dma_start(cC, CC).then_inc(c2n, 16)
            pool.dma_start(row2, ROW2.partition_broadcast(P)).then_inc(c2n, 16)
            for layer in range(2):
                pool.dma_start(plw[0:64, layer], POOLW[layer].rearrange("g i o -> i g o")).then_inc(c2n, 16)
            for layer in range(2):
                if layer == 1:
                    pool.wait_ge(S("bias_ready"), 1)
                for qr in range(4):
                    for h in range(HEADS):
                        off = ((layer * HEADS + h) * 15 + 7 - qr) * 31 - 48
                        dst = braw[(qr % 2) * 64:(qr % 2) * 64 + 64, qr // 2, h, :]
                        pool.dma_start(dst.rearrange("p (r c) -> p r c", r=4),
                                       bass.AP(tensor=RPB.tensor, offset=off, ap=[[1, 64], [31, 4], [1, 64]])
                                       ).then_inc(S(f"rpb_loaded{layer}"), 16)

        @block.scalar
        def _(act):
            steps = [0]

            def link(ins):
                steps[0] += 1
                ins.then_inc(S("act_step"), 1)
                act.wait_ge(S("act_step"), steps[0])

            n_rsqrt = [0]

            def rsqrt(n):
                n_rsqrt[0] += 1
                act.wait_ge(S("ms_ready"), n_rsqrt[0])
                link(nc.scalar.activation(rs[:, 2, 0:n], rs[:, 1, 0:n], ACT.Ln))
                nc.scalar.activation(rs[:, 3, 0:n], rs[:, 2, 0:n], ACT.Exp, scale=-0.5).then_inc(S("r0_ready"), 1)

            n_ss = [0]

            def square_sums(tiles, junk):
                for i, t in enumerate(tiles):
                    if n_ss[0]:
                        act.wait_ge(S("ss_ready"), n_ss[0])
                    n_ss[0] += 1
                    nc.scalar.activation(junk, t, ACT.Square, accum_out=rs[:, 0, i:i + 1]
                                         ).then_inc(S("ss_ready"), 1)

            cn = S("const_loaded")
            act.dma_start(vec[:, :], VEC).then_inc(cn, 16)
            act.dma_start(cA[:, :], CA).then_inc(cn, 16)
            act.dma_start(x[:, :, :], X.rearrange("b (t p) d -> p (b t) d", p=P)).then_inc(cn, 16)
            act.dma_start(cx, CTX.rearrange("b (t p) d -> p (b t) d", p=P)).then_inc(cn, 16)
            act.dma_start(cB, CB).then_inc(cn, 16)
            act.dma_start(row1, ROW1.partition_broadcast(P)).then_inc(cn, 16)
            act.dma_start(lrw2[0:GRANK], LRW2.rearrange("d r k -> r d k")).then_inc(cn, 16)
            act.wait_ge(cn, 16 * N_CONST)
            nc.scalar.activation(condt[:, :, :].rearrange("p c v -> p (c v)"), vec[:, lv["cond"]], ACT.Exp,
                                 scale=-1.0).then_inc(S("cond_exp"), 1)
            square_sums([x[:, 0, :], x[:, 1, :], cx[:, 0, :], cx[:, 1, :]], sqj)
            rsqrt(4)

            def copy_out(key, dst, src=None, scale=None):
                bank = take(act, key)
                src = bank[:, :] if src is None else src(bank)
                if scale is None:
                    free(nc.scalar.copy(dst, src), key)
                else:
                    free(nc.scalar.mul(dst, src, scale), key)

            pair = lambda b: b[:, :].rearrange("p (a n) -> p a n", a=2)
            mod_at = [0]

            def modulation(n=1):
                for _ in range(n):
                    u = mod_at[0]
                    if u == MOD_UNITS:
                        return
                    mod_at[0] += 1
                    if u >= 2:
                        act.wait_ge(S("mod_columns"), u - 1)
                    copy_out(("modrow", u), modrow[0:2, u % 2, :], lambda b: b[0:2, :])

            modulation(MOD_FIRST)
            for d in range(2):
                copy_out(("glr", d), glrT[0:GRANK, d, :], lambda b: b[0:GRANK, :])
            act.wait_ge(S("gate_abs"), 1)
            link(nc.scalar.activation(gtmp[0:HEADS], gtmp[0:HEADS], ACT.Exp, scale=-1.0))
            nc.scalar.activation(gtmp[0:HEADS], gtmp[0:HEADS], ACT.Ln, bias=1.0).then_inc(S("gate_ln"), 1)
            for i in range(2):
                for src in range(2):
                    copy_out(("mv", i, src), vml[:, 2 * src:2 * src + 2, 2 * i:2 * i + 2, 0:P],
                             lambda b: b[:, :].rearrange("p (a h n) -> p a h n", a=2, h=2))
            for i in range(2):
                copy_out(("mo", i), og[:, :, i * WC:(i + 1) * WC], pair)
            copy_out(("gq",), gqT, pair, scale=64.0 ** -0.5)
            for j in range(2):
                copy_out(("gk", j), gkT[:, j, :])
            for i in range(2):
                for src in range(2):
                    copy_out(("gv", i, src), gv[:, 2 * src:2 * src + 2, i * WC:(i + 1) * WC], pair)
            for i in range(2):
                copy_out(("gr", i), og[:, :, 512 + i * WC:512 + (i + 1) * WC], pair)
            modulation(MOD_LATER["gr"])
            act.wait_ge(S("conv_done"), 1)
            nc.scalar.activation(es[:, 0:1024], cq.rearrange("p h t -> p (h t)"), ACT.Exp, scale=-1.0
                                 ).then_inc(S("conv_exp"), 1)
            nc.scalar.activation(es[:, 1024:3072], ck.rearrange("p h t -> p (h t)"), ACT.Exp, scale=-1.0
                                 ).then_inc(S("conv_exp"), 1)
            act.wait_ge(S("m_ready"), 1)
            nc.scalar.activation(em[0:HEADS], em[0:HEADS], ACT.Exp, scale=-1.0).then_inc(S("em_ready"), 1)
            stored(act, ("gr", 1))
            nc.scalar.activation(ogt, og, ACT.Exp, scale=-1.0).then_inc(S("og_exp"), 1)
            stored(act, ("acol",))
            for h in range(HEADS):
                for d in range(2):
                    if h >= 1:
                        act.wait_ge(S("P_ready"), 2 * (h - 1) + d + 1)
                    bank = take(act, ("E", h, d))

                    def weight(st, dst, src):
                        return nc.scalar.activation(EW[:, d, st, dst:dst + src.shape[1]], src, ACT.Exp,
                                                    bias=acol[:, st, d, h:h + 1])

                    weight(2, 0, bank[:, 0:T])
                    weight(3, 0, bank[:, 0:T])
                    weight(0, 0, bank[:, T:T + P])
                    if d == 0:
                        weight(0, P, bank[:, P:T])
                    else:
                        weight(1, 0, bank[:, 0:P])
                    free(weight(1, P, bank[:, T + P:2 * T]), ("E", h, d))
                modulation(MOD_LATER["mlstm"])
            modulation(MOD_LATER["alpha"])
            act.wait_ge(S("alpha_abs"), 1)
            link(nc.scalar.activation(lt, lt, ACT.Exp, scale=-1.0))
            nc.scalar.activation(lt, lt, ACT.Ln, bias=1.0).then_inc(S("alpha_ln"), 1)
            act.wait_ge(S("kdec_log"), 1)
            nc.scalar.activation(lt, lt, ACT.Exp).then_inc(S("kdec_exp"), 1)
            nc.scalar.activation(eend, eend, ACT.Exp).then_inc(S("kdec_exp"), 1)
            modulation(MOD_LATER["kdn"])
            act.wait_ge(S("q_log"), 1)
            nc.scalar.activation(lt[:, :, :, T:2 * T], lt[:, :, :, 0:T], ACT.Exp, scale=-1.0).then_inc(S("q_exp"), 1)
            nc.scalar.activation(lt[:, :, :, 0:T], lt[:, :, :, 0:T], ACT.Exp).then_inc(S("q_exp"), 1)
            nc.scalar.activation(lbm[:, :, :, 0:T], lbm[:, :, :, 0:T], ACT.Exp).then_inc(S("q_exp"), 1)
            for step in range(7):
                modulation(MOD_LATER["state"])
            modulation(MOD_UNITS)
            act.wait_ge(S("hcat_ready"), 1)
            for tt in range(NT):
                if tt:
                    act.wait_ge(S("sq_used"), tt)
                nc.scalar.activation(sq2, hcat[:, tt, :], ACT.Square).then_inc(S("sq_ready"), 1)
            rsqrt(16)
            for half in range(2):
                copy_out(("gbc", half), gbc[:, half * 512:(half + 1) * 512])
            for cc in range(4):
                copy_out(("mixT", cc), mixT[:, 2 * cc:2 * cc + 2, :], pair)
            act.wait_ge(S("x_ready"), 1)
            square_sums([x[:, 0, :], x[:, 1, :]], sq2)
            rsqrt(2)
            stored(act, ("h2T", 3))
            nc.scalar.activation(h2_high[:, :, :], h2T[:, :, :], ACT.Copy).then_inc(S("h2_high_ready"), 1)
            for i in range(N_WQ):
                copy_out(("wq", i), qTp[:, 2 * i:2 * i + 2, :], pair)
            for tt in range(NT):
                for q in range(4):
                    copy_out(("sc", tt, q), sc[:, tt, 4 * q:4 * q + 4, :],
                             lambda b: b[:, :].rearrange("p (a n) -> p a n", a=4))
            act.wait_ge(S("emptied_dve"), before_peer["dve"])
            act.sem_inc(S("u_bank_free"), WSLOTS)

            def val(e):
                return e if isinstance(e, int) else act.snap(e)

            def high(k, landed, idx):
                act.wait_ge(S(f"tile_landed{k}"), landed)
                for a in range(2):
                    if not (isinstance(idx[a], int) and idx[a] < 0):
                        act.wait_ge(S("w_high_used"), idx[a])
                        act.wait_ge(S("w_rest_ready"), idx[a])
                    nc.scalar.activation(w_high[:, a, :], ring[:, k, a * HALF:(a + 1) * HALF], ACT.Copy
                                         ).then_inc(S("w_high_ready"), 1)

            def gelu(k, used, col):
                act.wait_ge(S("tile_used"), used)
                nc.scalar.activation(GH[:, bass.ds(col, 2), :], banks[k][:, :].rearrange("p (a t) -> p a t", a=2),
                                     ACT.Gelu).then_inc(S("u_bank_free"), 1)

            def expert_tiles(it, tile, split, split_before):
                for k in range(WSLOTS):
                    landed = val(it * 16 + 16 * ((N_PRE + tile) // WSLOTS + 1))
                    if k in split:
                        idx = [val(it * (2 * len(split)) + split_before + 2 * split.index(k) + a - 1)
                               for a in range(2)]
                        high(k, landed, idx)
                    if not (isinstance(it, int) and tile + k == 0):
                        gelu((k - 1) % WSLOTS, val(it * WSLOTS + N_PRE + tile + k),
                             val(it * (2 * WSLOTS) + 2 * (tile + k - 1)))

            expert_tiles(0, 0, SPLIT1, 0)
            with act.Fori(0, U_HALF - 1) as it:
                expert_tiles(it, WSLOTS, SPLIT1, 2 * len(SPLIT1))
            act.wait_ge(S("smax_log"), 1)
            for tt in range(NT):
                nc.scalar.activation(bests[:, tt], bests[:, tt], ACT.Exp).then_inc(S("smax_exp"), 1)
            act.wait_ge(S("selT_filled"), 1)
            with act.Fori(0, U_HALF) as it:
                expert_tiles(it, N_PEER // 2, tuple(range(WSLOTS)), N_SPLIT1)
            gelu(WSLOTS - 1, N_PRE + N_PEER, P - 2)
            def onehots(b, n):
                act.wait_ge(S("dif_ready"), n)
                nc.scalar.activation(dif[:, b], dif[:, b], ACT.Square).then_inc(S("dif_squared"), 1)
                act.wait_ge(S("dif_squared"), n)
                nc.scalar.activation(oh[:, b, 1], dif[:, b], ACT.Relu, bias=ones[:, 0:1], scale=-1.0
                                     ).then_inc(S("oh2_ready"), 1)

            for b in range(2):
                onehots(b, b + 1)
            with act.Fori(0, T // 8 - 1) as it:
                for b in range(2):
                    n = act.snap(it * 2 + b + 3)
                    used = act.snap(it * 2 + b + 1)
                    act.wait_ge(S("w_filled"), used)
                    onehots(b, n)

            act.wait_ge(S("w_bank_free"), 2 + T // 4)
            with act.Fori(0, N_PEER // WSLOTS) as it:
                for k in range(WSLOTS):
                    used = act.snap(it * WSLOTS + N_PRE + N_PEER + k - 1)
                    col = act.snap(it * (2 * WSLOTS) + 2 * k)
                    landed = act.snap(it * 16 + 16 * ((N_PRE + N_PEER) // WSLOTS + 1))
                    idx = [act.snap(it * (2 * WSLOTS) + N_SPLIT2 + 2 * k + a - 1) for a in range(2)]
                    act.wait_ge(S("tile_used"), used)
                    nc.scalar.activation(g_high[:, k % 2], GH[:, bass.ds(col, 2), :], ACT.Copy
                                         ).then_inc(S("g_high_ready"), 1)
                    high(k, landed, idx)
            act.wait_ge(S("x_ready"), 2)
            square_sums([x[:, 0, :], x[:, 1, :]], z[:, 0, 0:D])
            rsqrt(2)
            n_attn, n_x = 0, 2
            act.wait_ge(S("const2_loaded"), 16 * N_CONST2)
            for layer in range(2):
                n_x += 1
                act.wait_ge(S("x_ready"), n_x)
                square_sums([x[:, 0, :], x[:, 1, :], c2[:, 0, :], c2[:, 1, :]], z[:, 0, 0:D])
                rsqrt(4)
                for i in range(N_IN2):
                    copy_out(("z", layer, i, 0), z[:, 0:2, i * WC:(i + 1) * WC], pair)
                for src in ((0, 1) if layer == 0 else (0,)):
                    stored(act, ("z", layer, N_IN2 - 1, src))
                    for tt in range(NT):
                        zt = 2 * src + tt
                        for o, (col, n) in zip((0, 512, 768), ((AG, 512), (BG, 256), (NG, 256))):
                            last = nc.scalar.activation(xn3[:, zt, o:o + n], z[:, zt, col:col + n], ACT.Exp, scale=-1.0)
                    last.then_inc(S("gate2_exp"), 1)
                for src in range(2):
                    rsqrt(n_norms(layer, src))
                bufs = dict(aqT=aqT, akT=akT, nqT=nqT, nkT=nkT)

                def qk_out(src, n, buf, h):
                    if n % 2:
                        lo = src * T if buf in ("akT", "nkT") else 0
                        copy_out(("qk", layer, src, n), bufs[buf][0:64, h:h + 2, lo:lo + T],
                                 lambda b: b[0:64, :].rearrange("p (a t) -> p a t", a=2))

                for n, (buf, h, col) in enumerate(qk_pairs(layer, 0)):
                    qk_out(0, n, buf, h)
                for n, (buf, h, col) in enumerate(qk_pairs(layer, 1)):
                    if buf in ("akT", "nkT"):
                        qk_out(1, n, buf, h)
                todo = attn_list(layer)
                for part in range(1 if layer else 2):
                    mine = [a for a in todo if a[1] == part]
                    if part == 1:
                        for n, (buf, h, col) in enumerate(qk_pairs(layer, 1)):
                            if buf in ("aqT", "nqT"):
                                qk_out(1, n, buf, h)
                    for i, a in enumerate(mine):
                        _, src, kind, tt, h = a
                        n = 512 if src == 0 else T
                        act.wait_ge(S("negmax_ready"), n_attn + i + 1)
                        if i >= 2:
                            take(act, ("t",) + mine[i - 2])
                        bank = take(act, ("s",) + a)
                        u = n_attn + i
                        g = attn_group(layer, src, kind, tt)
                        if h == 0 and g >= 2:
                            act.wait_ge(S("att_free"), g - 1)
                        free(nc.scalar.activation(pw[:, u % 2, 0:n], bank[:, 0:n], ACT.Exp,
                                                  bias=tiny[:, 1, u % 16:u % 16 + 1],
                                                  accum_out=tiny[:, 2 + g % 2, h:h + 1]), ("s",) + a)
                    n_attn += len(mine)
                srcs = (0, 1) if layer == 0 else (0,)
                for src in srcs:
                    for half in range(2):
                        copy_out(("gb", layer, src, half), g2b[:, src, half * 512:(half + 1) * 512])
                    for cc in range(4):
                        copy_out(("mT", layer, src, cc), mixT3[:, src, 2 * cc:2 * cc + 2, :], pair)

        @block.vector
        def _(dve):
            steps = [0]

            def link(ins):
                steps[0] += 1
                ins.then_inc(S("dve_step"), 1)
                dve.wait_ge(S("dve_step"), steps[0])

            tt_, ts_, stt = nc.vector.tensor_tensor, nc.vector.tensor_scalar, nc.vector.scalar_tensor_tensor
            n_rsqrt = [0]

            def rsqrt(n, width):
                n_rsqrt[0] += 1
                ms, r, a = rs[:, 1, 0:n], rs[:, 3, 0:n], rs[:, 4, 0:n]
                ts_(ms, rs[:, 0, 0:n], 1.0 / width, EPS, ALU.mult, ALU.add).then_inc(S("ms_ready"), 1)
                dve.wait_ge(S("r0_ready"), n_rsqrt[0])
                link(tt_(a, r, r, ALU.mult))
                link(tt_(a, a, ms, ALU.mult))
                link(ts_(a, a, -0.5, 1.5, ALU.mult, ALU.add))
                link(tt_(r, r, a, ALU.mult))

            n_ss = [0]

            def norm_rows(tiles, outs):
                n_ss[0] += len(tiles)
                dve.wait_ge(S("ss_ready"), n_ss[0])
                rsqrt(len(tiles), D)
                for i, (t, o) in enumerate(zip(tiles, outs)):
                    ts_(o, t, rs[:, 3, i:i + 1], None, ALU.mult).then_inc(S("xn_ready"), 1)

            def bc(ap, shape, axis):
                return ap.unsqueeze(axis).to_broadcast(shape)

            def vcol(name, i=0):
                return vec[:, lv[name].start + i:lv[name].start + i + 1]

            def modulated(key, dst, g, sh):
                for cc in range(4):
                    bank = take(dve, key + (cc,))
                    for k in range(2):
                        c = 2 * cc + k
                        ins = ts_(dst(c), bank[:, k * T:(k + 1) * T], gain[:, g, c:c + 1], sh(c), ALU.mult, ALU.add)
                    free(ins, key + (cc,))

            dve.wait_ge(S("const_loaded"), 16 * N_CONST)
            dve.wait_ge(S("cond_exp"), 1)
            cv = vec[:, lv["cond"]].rearrange("p (c v) -> p c v", v=4)
            link(ts_(condt[:, :, :], condt[:, :, :], 1.0, None, ALU.add))
            link(nc.vector.reciprocal(condt[:, :, :], condt[:, :, :]))
            tt_(cond[:, :, :], condt[:, :, :], cv, ALU.mult).then_inc(S("cond_ready"), 1)
            norm_rows([x[:, 0, :], x[:, 1, :], cx[:, 0, :], cx[:, 1, :]], [xn[:, i, :] for i in range(4)])

            def mod_bias(dst, name, lo, n, col):
                o = lv[name].start + lo
                link(tt_(dst, banks[7][:, 2 * col:2 * (col + n)].rearrange("p (j v) -> p j v", v=2),
                         bc(vec[:, o:o + n], [P, n, 2], 2), ALU.add))

            dve.wait_ge(S("mod_columns"), MOD_FIRST)
            mod_bias(mod1[:, 0:16, :], "bmod1", 0, 16, 0)
            for v in range(2):
                link(stt(out=gain[:, v, :], in0=mod1[:, 8:16, v], scalar=1.0, in1=vec[:, lv["norm1"]],
                         op0=ALU.add, op1=ALU.mult))
            for src in range(2):
                modulated(("hT", src), lambda c: hT[:, c, src * T:(src + 1) * T], src,
                          lambda c: mod1[:, c, src:src + 1])

            for d in range(2):
                for g in range(2):
                    bank = take(dve, ("gate", d, g))
                    o = lv["gate_b"].start + d * 2 + g
                    dst = (gi, gf)[g]
                    free(ts_(dst[0:HEADS, d, :], bank[0:HEADS, :], vec[0:HEADS, o:o + 1], None, ALU.add),
                         ("gate", d, g))
            stored(dve, ("gate", 1, 1))
            stt(out=gtmp[0:HEADS], in0=gf[0:HEADS], scalar=-1.0, in1=gf[0:HEADS], op0=ALU.mult, op1=ALU.max
                ).then_inc(S("gate_abs"), 1)
            cw = vec[:, lv["conv"]].rearrange("p (k c) -> p k c", k=3)

            def conv(u, dst, feat, width, ready):
                u = u.rearrange("p (r c) -> p r c", c=width)
                y = dst.rearrange("p (r c) -> p r c", c=width)
                link(ts_(y, u, cw[:, 1, feat:feat + 1], None, ALU.mult))
                link(stt(out=y[:, :, 1:width], in0=u[:, :, 0:width - 1], scalar=cw[:, 0, feat:feat + 1],
                         in1=y[:, :, 1:width], op0=ALU.mult, op1=ALU.add))
                return stt(out=y[:, :, 0:width - 1], in0=u[:, :, 1:width], scalar=cw[:, 2, feat:feat + 1],
                           in1=y[:, :, 0:width - 1], op0=ALU.mult, op1=ALU.add)

            for i in range(2):
                bank = take(dve, ("mq", i))
                for k in range(2):
                    ins = conv(bank[:, k * T:(k + 1) * T], cq[:, 2 * i + k, :], 2 * i + k, GRID, None)
                free(ins, ("mq", i))
            for h in range(HEADS):
                bank = take(dve, ("mk", h))
                conv(bank[:, 0:T], ck[:, h, 0:T], 4 + h, GRID, None)
                free(conv(bank[:, T:2 * T], ck[:, h, T:2 * T], 4 + h, T, None), ("mk", h))
            stored(dve, ("mk", HEADS - 1))
            dve.sem_inc(S("conv_done"), 1)
            dve.wait_ge(S("gate_ln"), 1)
            link(stt(out=gf[0:HEADS], in0=gf[0:HEADS], scalar=0.0, in1=gtmp[0:HEADS], op0=ALU.min,
                     op1=ALU.subtract))
            scan = nc.vector.tensor_tensor_scan
            one_row = ones[0:HEADS, 0:1].to_broadcast([HEADS, T])
            for part in range(2):
                for d in range(2):
                    lo = T if part == 0 else 0
                    v = slice(lo, lo + T)
                    rev = (lambda ap: ap) if d == 0 else (lambda ap: ap[:, ::-1])
                    last_ctx = 2 * T - 1 if d == 0 else T
                    init = 0.0 if part == 0 else gb[0:HEADS, d, last_ctx:last_ctx + 1]
                    link(scan(rev(gb[0:HEADS, d, v]), one_row, rev(gf[0:HEADS, d, v]), init, ALU.mult, ALU.add))
            link(tt_(negA[0:HEADS], gb[0:HEADS], gi[0:HEADS], ALU.subtract))
            for part in range(2):
                for d in range(2):
                    lo = T if part == 0 else 0
                    v = slice(lo, lo + T)
                    rev = (lambda ap: ap) if d == 0 else (lambda ap: ap[:, ::-1])
                    last_ctx = 2 * T - 1 if d == 0 else T
                    init = 0.0 if part == 0 else nM[0:HEADS, d, last_ctx:last_ctx + 1]
                    link(scan(rev(nM[0:HEADS, d, v]), rev(negA[0:HEADS, d, v]), rev(negA[0:HEADS, d, v]), init,
                              ALU.min, ALU.min))
            dve.sem_inc(S("gate_rows_ready"), 1)
            tt_(em[0:HEADS], gb[0:HEADS, :, 0:T], nM[0:HEADS, :, 0:T], ALU.subtract).then_inc(S("m_ready"), 1)
            dve.wait_ge(S("conv_exp"), 2)
            link(ts_(es, es, 1.0, None, ALU.add))
            link(nc.vector.reciprocal(es, es))
            fl = lambda a: a.rearrange("p h t -> p (h t)")
            link(tt_(fl(cq), fl(cq), es[:, 0:1024], ALU.mult))
            stt(out=fl(ck), in0=fl(ck), scalar=float(P) ** -0.5, in1=es[:, 1024:3072], op0=ALU.mult, op1=ALU.mult
                ).then_inc(S("conv_ready"), 1)
            bank = take(dve, ("acol",))
            free(ts_(acol.rearrange("p a b c -> p (a b c)"), bank[:, 0:32], -1.0, None, ALU.mult), ("acol",))
            bank = take(dve, ("emcol",))
            free(nc.vector.tensor_copy(emcol.rearrange("p a b c -> p (a b c)"), bank[:, 0:16]), ("emcol",))
            dve.wait_ge(S("og_exp"), 1)
            link(ts_(ogt, ogt, 1.0, None, ALU.add))
            link(nc.vector.reciprocal(ogt, ogt))
            link(tt_(og[:, :, 512:D], og[:, :, 512:D], ogt[:, :, 512:D], ALU.mult))
            link(nc.vector.tensor_copy(og[:, :, 0:512], ogt[:, :, 0:512]))
            link(tt_(og, og, bc(row1, [P, NT, D], 1), ALU.mult))
            dve.wait_ge(S("vml_ones"), 1)
            for h in range(HEADS):
                bl, bx = take(dve, ("S", h, 0)), take(dve, ("S", h, 1))
                bl = bl[:, :].rearrange("p (s t) -> p s t", s=2)
                bx = bx[:, :].rearrange("p (s t) -> p s t", s=2)
                for d in range(2):
                    stored(dve, ("E", h, d))
                    if d == 0:
                        tt_(PW[:, d, 0, :], bl[:, 0, :], EW[:, d, 0, :], ALU.mult)
                        tt_(PW[:, d, 1, P:T], bl[:, 1, P:T], EW[:, d, 1, P:T], ALU.mult)
                        tt_(PW[:, d, 2:4, :], bx, EW[:, d, 2:4, :], ALU.mult).then_inc(S("P_ready"), 1)
                    else:
                        tt_(PW[:, d, 0, 0:P], bl[:, 0, 0:P], EW[:, d, 0, 0:P], ALU.mult)
                        free(tt_(PW[:, d, 1, :], bl[:, 1, :], EW[:, d, 1, :], ALU.mult), ("S", h, 0))
                        free(tt_(PW[:, d, 2:4, :], bx, EW[:, d, 2:4, :], ALU.mult), ("S", h, 1))
                        dve.wait_ge(S("emptied_dve"), units[("S", h, 1)]["idx"] + 1)
                        dve.sem_inc(S("P_ready"), 1)
                for d in range(2):
                    bank = take(dve, ("O", h, d))
                    b3 = bank[:, :].rearrange("p (t n) -> p t n", t=NT)
                    den = b3[:, :, P]
                    link(nc.vector.tensor_copy(dn[:, 0, :], den))
                    link(stt(out=dn[:, 1, :], in0=dn[:, 0, :], scalar=-1.0, in1=dn[:, 0, :], op0=ALU.mult,
                             op1=ALU.max))
                    link(tt_(dn[:, 2, :], dn[:, 1, :], emcol[:, :, d, h], ALU.max))
                    link(nc.vector.reciprocal(dn[:, 3, :], dn[:, 2, :]))
                    for tt in range(NT):
                        dst = hcat[:, tt, h * P:(h + 1) * P]
                        if d == 0:
                            ins = ts_(dst, b3[:, tt, 0:P], dn[:, 3, tt:tt + 1], None, ALU.mult)
                        else:
                            ins = stt(out=dst, in0=b3[:, tt, 0:P], scalar=dn[:, 3, tt:tt + 1], in1=dst,
                                      op0=ALU.mult, op1=ALU.add)
                    free(ins, ("O", h, d))
                    stored(dve, ("O", h, d))
            dve.sem_inc(S("mlstm_done"), 1)

            for d in range(2):
                for j in range(2):
                    bank = take(dve, ("alpha", d, j))
                    free(ts_(lx[:, d, j, :], bank[:, :], vcol("alpha_b", d * 2 + j), None, ALU.add),
                         ("alpha", d, j))
            stored(dve, ("alpha", 1, 1))
            stt(out=lt, in0=lx, scalar=-1.0, in1=lx, op0=ALU.mult, op1=ALU.max).then_inc(S("alpha_abs"), 1)
            dve.wait_ge(S("alpha_ln"), 1)
            link(stt(out=lx, in0=lx, scalar=0.0, in1=lt, op0=ALU.min, op1=ALU.subtract))
            link(ts_(lx, lx, 1.0 / 16, None, ALU.mult))
            reset = cB[:, lb["reset"]]
            for d in range(2):
                for j in range(2):
                    rev = (lambda ap: ap) if d == 0 else (lambda ap: ap[:, ::-1])
                    link(scan(rev(lbm[:, d, j, :]), reset, rev(lx[:, d, j, :]), 0.0, ALU.mult, ALU.add))
            chunks = lambda ap: ap.rearrange("p j (c s) -> p j c s", s=GC)
            for d in range(2):
                end = GC - 1 if d == 0 else 0
                b4 = chunks(lbm[:, d])
                link(nc.vector.tensor_copy(eend[:, d], b4[:, :, :, end]))
                link(tt_(chunks(lt[:, d]), b4[:, :, :, end:end + 1].to_broadcast([P, 2, 8, GC]), b4, ALU.subtract))
            dve.sem_inc(S("kdec_log"), 1)
            dve.wait_ge(S("kdec_exp"), 2)
            for d in range(2):
                ins = tt_(lx[:, d], lt[:, d], gkT, ALU.mult)
                if d == 0:
                    link(ins)
            ins.then_inc(S("kdec_ready"), 1)
            dve.wait_ge(S("kdec_ready"), 1)
            for d in range(2):
                refc = GC // 2 if d == 0 else GC // 2 - 1
                b4 = chunks(lbm[:, d, :, 0:T])
                link(tt_(chunks(lt[:, d, :, 0:T]), b4, b4[:, :, :, refc:refc + 1].to_broadcast([P, 2, NGC, GC]),
                         ALU.subtract))
            dve.sem_inc(S("q_log"), 1)
            for d in range(2):
                for src in range(2):
                    bank = take(dve, ("kdn", d, src))
                    v = bank[:, :].rearrange("p (t n) -> p t n", t=NT)
                    for par in range(2):
                        hc = cB[:, lb["half"].start + par:lb["half"].start + par + 1]
                        ins = ts_(kdn[:, d, 2 * src:2 * src + 2, par, :], v, hc, None, ALU.mult)
                    free(ins, ("kdn", d, src))
            dve.wait_ge(S("q_exp"), 3)
            dve.wait_ge(S("gla_zero"), 4)
            for d in range(2):
                tt_(kz[:, d], lt[:, d, :, T:2 * T], gkT[:, :, 0:T], ALU.mult)
                for par in range(2):
                    pr = slice(par * 64, par * 64 + 64)
                    tt_(qz[pr, d, par], lt[pr, d, :, 0:T], gqT[pr], ALU.mult)
                    for j in range(2):
                        v = lambda ap: ap.rearrange("p (a b s) -> p a b s", a=2, b=2)[:, :, par, :]
                        ins = tt_(v(qs[:, d, par, j, :]), v(lbm[:, d, j, 0:T]), v(gqT[:, j, :]), ALU.mult)
                        link(ins)
            dve.sem_inc(S("gla_q_ready"), 1)
            for step in range(7):
                for d in range(2):
                    c = gla_chunk(step, d)
                    bank = take(dve, ("St", step, d))

                    def state(n):
                        if n < NGC:
                            return Sct[:, d, n % 2]
                        return Sst[:, d, gla_chunk(n, d)]

                    new, old = state(step + 1), state(step)
                    for j in range(2):
                        for par in range(2):
                            pr, cols = slice(par * 64, par * 64 + 64), slice(par * P, par * P + P)
                            b = bank[pr, j * 256 + par * P:j * 256 + par * P + P]
                            if step == 0:
                                ins = nc.vector.tensor_copy(new[pr, j, cols], b)
                            else:
                                ins = stt(out=new[pr, j, cols], in0=old[pr, j, cols], scalar=eend[pr, d, j, c:c + 1],
                                          in1=b, op0=ALU.mult, op1=ALU.add)
                    free(ins, ("St", step, d))
                    stored(dve, ("St", step, d))
            for tt in range(NT):
                for d in range(2):
                    bank = take(dve, ("att", tt, d))
                    o = lb["tri_gla"].start + d * P
                    m = bc(cB[:, o:o + P].bitcast(U32), [P, HEADS, P], 1)
                    free(nc.vector.copy_predicated(att[:, d], m, bank[:, :].rearrange("p (h t) -> p h t", h=HEADS)),
                         ("att", tt, d))
                bank = take(dve, ("gla", tt))
                free(nc.vector.tensor_copy(hcat[:, tt, 512:D], bank[:, :]), ("gla", tt))
            stored(dve, ("gla", 1))
            dve.sem_inc(S("hcat_ready"), 1)
            dve.wait_ge(S("mod_columns"), MOD_UNITS)
            mod_bias(mod1[:, 16:48, :], "bmod1", 16, 32, 16)
            for layer in range(2):
                mod_bias(mod2[:, layer], "bmod2", 24 * layer, 24, 48 + 24 * layer)
            link(stt(out=gain[:, 2, :], in0=mod1[:, 32:40, 0], scalar=1.0, in1=vec[:, lv["norm2"]],
                     op0=ALU.add, op1=ALU.mult))
            id8 = bc(ident, [P, C, P], 1)
            link(tt_(diag, id8, bc(mod1[:, 16:24, 0], [P, C, P], 2), ALU.mult))
            dve.sem_inc(S("diag_ready"), 1)
            for tt in range(NT):
                dve.wait_ge(S("sq_ready"), tt + 1)
                link(nc.vector.tensor_reduce(rs[:, 0, tt * 8:tt * 8 + 8], sq2.rearrange("p (h n) -> p h n", n=P),
                                             AX, ALU.add))
                dve.sem_inc(S("sq_used"), 1)
            rsqrt(16, P)
            for tt in range(NT):
                m = mix[:, tt, :].rearrange("p (h n) -> p h n", n=P)
                r = rs[:, 3, tt * 8:tt * 8 + 8]
                link(tt_(m, hcat[:, tt, :].rearrange("p (h n) -> p h n", n=P), bc(r, [P, 8, P], 2), ALU.mult))
                link(tt_(mix[:, tt, :], mix[:, tt, :], og[:, tt, :], ALU.mult))
            dve.sem_inc(S("mix_ready"), 1)
            stored(dve, ("gbc", 1))

            def residual(key, dst, gate, i, tmp):
                bank = take(dve, key)
                cols = slice(i * WC, (i + 1) * WC)
                free(tt_(tmp, bank[:, :].rearrange("p (t n) -> p t n", t=NT), bc(gate[:, cols], [P, NT, WC], 1),
                         ALU.mult), key)
                stored(dve, key)
                link(tt_(dst[:, :, cols], dst[:, :, cols], tmp, ALU.add))

            for i in range(N_OUT):
                residual(("y", i), x, gbc, i, ytmp)
            dve.sem_inc(S("x_ready"), 1)
            norm_rows([x[:, 0, :], x[:, 1, :]], [xn2[:, 0, :], xn2[:, 1, :]])
            modulated(("h2T",), lambda c: h2T[:, c, :], 2, lambda c: mod1[:, 24 + c, 0:1])
            dve.wait_ge(S("h2_high_ready"), 1)
            tt_(h2_rest[:, :, :], h2T[:, :, :], h2_high[:, :, :].bitcast(F32), ALU.subtract).then_inc(S("h2_rest_ready"), 1)

            def top16(vals, scratch, out_v, out_i, n):
                link(nc.vector.max(out_v[:, 0:8], vals))
                nc.vector.max_index(out_i[:, 0:8].bitcast(U32), out_v[:, 0:8], vals)
                link(nc.vector.match_replace(scratch[:, 0:n], out_v[:, 0:8], vals, BIG))
                link(nc.vector.max(out_v[:, 8:16], scratch[:, 0:n]))
                link(nc.vector.max_index(out_i[:, 8:16].bitcast(U32), out_v[:, 8:16], scratch[:, 0:n]))

            for tt in range(NT):
                stored(dve, ("sc", NT - 1, 3))
                for hp in range(16):
                    top16(sc[:, tt, hp, :], work, tops[:, tt, hp, :], topi[:, tt, hp, :], PK)
                link(nc.vector.tensor_copy(topf[:, tt], topi[:, tt].bitcast(U32)))
                pairs = tops[:, tt].rearrange("p (h s) k -> p h s k", s=2)
                for h in range(PH):
                    link(tt_(cand[:, h, :].rearrange("p (a b) -> p a b", a=TOPK), bc(pairs[:, h, 0, :], [P, 16, 16], 2),
                             bc(pairs[:, h, 1, :], [P, 16, 16], 1), ALU.add))
                    top16(cand[:, h, :], work, bests[:, tt, h, :], bestc[:, tt, h, :], 256)
                bc_u = bestc[:, tt].bitcast(U32)
                link(nc.vector.tensor_single_scalar(bhl[:, 0].bitcast(U32), bc_u, 4, ALU.logical_shift_right))
                link(nc.vector.tensor_single_scalar(bhl[:, 1].bitcast(U32), bc_u, 15, ALU.bitwise_and))
                io16 = iota[:, 0:TOPK]
                fi = topf[:, tt].rearrange("p (h s) k -> p h s k", s=2)
                for s in range(2):
                    link(nc.vector.tensor_copy(bhl[:, s], bhl[:, s].bitcast(U32)))
                    link(tt_(onek.rearrange("p h k j -> p (h k) j"), bc(fl(bhl[:, s]), [P, P, TOPK], 2),
                             bc(io16, [P, P, TOPK], 1), ALU.is_equal))
                    link(tt_(onek, onek, bc(fi[:, :, s, :], [P, PH, TOPK, TOPK], 2), ALU.mult))
                    link(nc.vector.tensor_reduce(sels[:, tt, s, :], onek.rearrange("p h k j -> p (h k) j"), AX,
                                                 ALU.add))
                link(nc.vector.tensor_copy(smx[:, tt, 0:8], bests[:, tt, :, 0]))
                link(tt_(bests[:, tt], bests[:, tt], bc(smx[:, tt, 0:8], [P, PH, TOPK], 2), ALU.subtract))
            dve.sem_inc(S("smax_log"), 1)
            dve.wait_ge(S("smax_exp"), NT)
            for tt in range(NT):
                link(nc.vector.tensor_reduce(smx[:, 2 + tt, 0:8], bests[:, tt], AX, ALU.add))
                link(nc.vector.reciprocal(smx[:, 2 + tt, 8:16], smx[:, 2 + tt, 0:8]))
                link(tt_(sels[:, tt, 2, :].rearrange("p (h k) -> p h k", k=TOPK), bests[:, tt],
                         bc(smx[:, 2 + tt, 8:16], [P, PH, TOPK], 2), ALU.mult))
            dve.sem_inc(S("topk_done"), 1)

            def rests(k, n):
                for a in range(2):
                    half = slice(a * HALF, (a + 1) * HALF)
                    dve.wait_ge(S("w_high_ready"), n[a])
                    tt_(w_rest[:, k, half], ring[:, k, half], w_high[:, a, :].bitcast(F32), ALU.subtract
                        ).then_inc(S("w_rest_ready"), 1)

            dve.wait_ge(S("w_rest_ready"), N_SPLIT1)
            with dve.Fori(0, U_HALF) as it:
                for k in range(WSLOTS):
                    rests(k, [dve.snap(it * (2 * WSLOTS) + N_SPLIT1 + 2 * k + a + 1) for a in range(2)])
            dve.wait_ge(S("tile_used"), N_PRE + N_PEER)
            link(nc.vector.tensor_copy(selT[:, 0:2, :].rearrange("p a t -> p (a t)"), banks[6][:, :]))
            link(nc.vector.tensor_copy(selT[:, 2, :], banks[7][:, 0:T]))
            dve.sem_inc(S("selT_stored"), 1)
            dve.wait_ge(S("u_bank_free"), WSLOTS + N_PEER)
            dve.sem_inc(S("w_bank_free"), 2)

            def weighted_onehots(b, first):
                for k in range(4):
                    one = bass.ds(first[k], 1)
                    ins = ts_(oh[:, b, 0, k, :], iota, selT[:, 0, one], selT[:, 2, one], ALU.is_equal, ALU.mult)
                ins.then_inc(S("oh_ready"), 1)

            def weigh(b, col, n):
                dve.wait_ge(S("w_filled"), n)
                g = GH[:, :, bass.ds(col, 4)]
                tt_(g, g, banks[4 + b][:, :].rearrange("p (t i) -> p i t", t=4), ALU.mult
                    ).then_inc(S("w_bank_free"), 1)

            for b in range(2):
                weighted_onehots(b, [4 * b + k for k in range(4)])
            with dve.Fori(0, T // 8 - 1) as it:
                for b in range(2):
                    n = dve.snap(it * 2 + b + 1)
                    col = dve.snap(it * 8 + 4 * b)
                    weigh(b, col, n)
                    weighted_onehots(b, [dve.snap(it * 8 + 8 + 4 * b + k) for k in range(4)])
            for b in range(2):
                weigh(b, T - 8 + 4 * b, T // 4 - 1 + b)
            with dve.Fori(0, N_PEER // WSLOTS) as it:
                for k in range(WSLOTS):
                    n = dve.snap(it * WSLOTS + k + 1)
                    col = dve.snap(it * (2 * WSLOTS) + 2 * k)
                    idx = [dve.snap(it * (2 * WSLOTS) + N_SPLIT2 + 2 * k + a + 1) for a in range(2)]
                    dve.wait_ge(S("g_high_ready"), n)
                    tt_(g_rest[:, k % 2], GH[:, bass.ds(col, 2), :], g_high[:, k % 2].bitcast(F32), ALU.subtract
                        ).then_inc(S("g_rest_ready"), 1)
                    rests(k, idx)
            dve.wait_ge(S("tile_used"), N_PRE + 2 * N_PEER)
            for c in range(C):
                link(ts_(peT[:, c, :], banks[c // 2][:, (c % 2) * T:(c % 2 + 1) * T], mod1[:, 40 + c, 0:1], None,
                         ALU.mult))
            dve.sem_inc(S("peT_ready"), 1)
            for tt in range(NT):
                for half in range(2):
                    bank = take(dve, ("pe", tt, half))
                    cols = slice(half * 512, (half + 1) * 512)
                    free(tt_(x[:, tt, cols], x[:, tt, cols], bank[:, :], ALU.add), ("pe", tt, half))
            stored(dve, ("pe", 1, 1))
            dve.sem_inc(S("x_ready"), 1)
            dve.wait_ge(S("ss_ready"), n_ss[0] + 2)
            n_ss[0] += 2
            rsqrt(2, D)
            dve.wait_ge(S("const2_loaded"), 16 * N_CONST2)
            for tt in range(NT):
                link(stt(out=x[:, tt, :], in0=x[:, tt, :], scalar=rs[:, 3, tt:tt + 1], in1=normf, op0=ALU.mult,
                         op1=ALU.mult))
            dve.sem_inc(S("x_ready"), 1)
            for layer in range(2):
                for g in (0, 1):
                    o = lv["normg2"].start + C * layer
                    link(stt(out=gain[:, 3 + g, :], in0=mod2[:, layer, 8:16, g], scalar=1.0, in1=vec[:, o:o + C],
                             op0=ALU.add, op1=ALU.mult))
                norm_rows([x[:, 0, :], x[:, 1, :], c2[:, 0, :], c2[:, 1, :]], [xn3[:, i, :] for i in range(4)])
                for src in range(2):
                    modulated(("hT2", layer, src), lambda c: hT2[:, c, src * T:(src + 1) * T], 3 + src,
                              lambda c: mod2[:, layer, c, src:src + 1])
                for i in z_tiles(layer, 1):
                    bank = take(dve, ("z", layer, i, 1))
                    free(nc.vector.tensor_copy(z[:, 2:4, i * WC:(i + 1) * WC],
                                               bank[:, :].rearrange("p (t n) -> p t n", t=NT)), ("z", layer, i, 1))
                stored(dve, ("z", layer, z_tiles(layer, 1)[-1], 1))
                stored(dve, ("z", layer, N_IN2 - 1, 0))
                if layer == 0:
                    for l2 in range(2):
                        for nm in ("aq", "nq"):
                            g = row2[:, lr2[f"{nm}{l2}"]]
                            link(ts_(g, g, 64.0 ** -0.5, None, ALU.mult))
                for src in range(2):
                    groups = norm_groups(layer, src)
                    n = 0
                    for tt in range(NT):
                        for col, heads, name in groups:
                            zz = z[:, 2 * src + tt, col:col + heads * 64]
                            link(tt_(rt[:, 0, 0:heads * 64], zz, zz, ALU.mult))
                            link(nc.vector.tensor_reduce(rs[:, 0, n:n + heads],
                                                         rt[:, 0, 0:heads * 64].rearrange("p (h n) -> p h n", n=64),
                                                         AX, ALU.add))
                            n += heads
                    rsqrt(n, 64)
                    n = 0
                    for tt in range(NT):
                        for col, heads, name in groups:
                            zz = z[:, 2 * src + tt, col:col + heads * 64].rearrange("p (h n) -> p h n", n=64)
                            link(tt_(zz, zz, bc(rs[:, 3, n:n + heads], [P, heads, 64], 2), ALU.mult))
                            link(tt_(zz, zz, bc(row2[:, lr2[f"{name}{layer}"]], [P, heads, 64], 1), ALU.mult))
                            n += heads
                        if src == 0:
                            q = z[:, tt, 0:640].rearrange("p (h n) -> p h n", n=64)
                            cs = cC[:, lc["cos"].start + tt * 64:lc["cos"].start + tt * 64 + 64]
                            sn = cC[:, lc["sin"].start + tt * 64:lc["sin"].start + tt * 64 + 64]
                            r0 = rt[:, 0, :].rearrange("p (h n) -> p h n", n=64)
                            link(tt_(r0, q, bc(cs, [P, 10, 64], 1), ALU.mult))
                            for hf in range(2):
                                for a in range(2):
                                    o, s = a * 32 + hf * 16, a * 32 + (1 - hf) * 16
                                    r1 = rt[:, 1, :].rearrange("p (h n) -> p h n", n=64)
                                    link(tt_(r1[:, :, o:o + 16], q[:, :, s:s + 16], bc(sn[:, o:o + 16], [P, 10, 16], 1),
                                             ALU.mult))
                            link(tt_(z[:, tt, 0:640], rt[:, 0, :], rt[:, 1, :], ALU.add))
                    dve.sem_inc(S("qk_ready"), 1)
                dve.wait_ge(S(f"rpb_loaded{layer}"), 16 * 16)
                for tt in range(NT):
                    for h in range(HEADS):
                        link(tt_(bm[:, tt, h, :].rearrange("p (r c) -> p r c", r=4),
                                 braw[:, tt, h, :].rearrange("p (r c) -> p r c", r=4)[:, :, ::-1],
                                 bc(cC[:, lc["namask"]], [P, 4, GRID], 1), ALU.add))
                dve.sem_inc(S("bias_ready"), 1)
                srcs = (0, 1) if layer == 0 else (0,)
                for src in srcs:
                    dve.wait_ge(S("gate2_exp"), 2 * layer + src + 1)
                    for tt in range(NT):
                        zt = 2 * src + tt
                        link(ts_(xn3[:, zt, :], xn3[:, zt, :], 1.0, None, ALU.add))
                        link(nc.vector.reciprocal(xn3[:, zt, :], xn3[:, zt, :]))
                        for o, (col, n) in zip((0, 512, 768), ((AG, 512), (BG, 256), (NG, 256))):
                            link(tt_(z[:, zt, col:col + n], z[:, zt, col:col + n], xn3[:, zt, o:o + n], ALU.mult))
                bufs = dict(aqT=aqT, akT=akT, nqT=nqT, nkT=nkT)

                def qk_out(src, n, buf, h):
                    if n % 2 == 0:
                        lo = src * T if buf in ("akT", "nkT") else 0
                        key = ("qk", layer, src, n)
                        bank = take(dve, key)
                        free(nc.vector.tensor_copy(bufs[buf][0:64, h:h + 2, lo:lo + T],
                                                   bank[0:64, :].rearrange("p (a t) -> p a t", a=2)), key)

                for n, (buf, h, col) in enumerate(qk_pairs(layer, 0)):
                    qk_out(0, n, buf, h)
                for n, (buf, h, col) in enumerate(qk_pairs(layer, 1)):
                    if buf in ("akT", "nkT"):
                        qk_out(1, n, buf, h)
                todo = attn_list(layer)
                for part in range(1 if layer else 2):
                    mine = [a for a in todo if a[1] == part]
                    if part == 1:
                        for n, (buf, h, col) in enumerate(qk_pairs(layer, 1)):
                            if buf in ("aqT", "nqT"):
                                qk_out(1, n, buf, h)

                    def negmax(a):
                        u = attn_index(a)
                        n = 512 if a[1] == 0 else T
                        bank = take(dve, ("s",) + a)
                        i = u % 16
                        link(nc.vector.tensor_reduce(tiny[:, 0, i:i + 1], bank[:, 0:n], AX, ALU.max))
                        ts_(tiny[:, 1, i:i + 1], tiny[:, 0, i:i + 1], -1.0, None, ALU.mult
                            ).then_inc(S("negmax_ready"), 1)

                    negmax(mine[0])
                    negmax(mine[1])
                    for i, a in enumerate(mine):
                        _, src, kind, tt, h = a
                        nst = 4 if src == 0 else 2
                        bank = take(dve, ("t",) + a)
                        free(nc.vector.tensor_copy(pt[:, attn_index(a) % 2, 0:nst, :],
                                                   bank[:, 0:nst * P].rearrange("p (s t) -> p s t", s=nst)),
                             ("t",) + a)
                        if i + 2 < len(mine):
                            negmax(mine[i + 2])
                        if h == (7 if kind == "a" else 3):
                            g = attn_group(layer, src, kind, tt)
                            dve.wait_ge(S("att_filled"), g + 1)
                            hs = h + 1
                            zt, mo, gc = 2 * src + tt, (0 if kind == "a" else 768), (AG if kind == "a" else NG)
                            link(nc.vector.reciprocal(tiny[:, 4, 0:hs], tiny[:, 2 + g % 2, 0:hs]))
                            m = mix3[:, zt, mo:mo + hs * 64]
                            link(tt_(m.rearrange("p (h n) -> p h n", n=64),
                                     banks[6 + g % 2][:, 0:hs * 64].rearrange("p (h n) -> p h n", n=64),
                                     bc(tiny[:, 4, 0:hs], [P, hs, 64], 2), ALU.mult))
                            dve.sem_inc(S("att_free"), 1)
                            link(tt_(m, m, z[:, zt, gc:gc + hs * 64], ALU.mult))
                    src = part
                    for gp in range(2):
                        key = ("pl", layer, src, gp)
                        bank = take(dve, key)
                        free(nc.vector.tensor_copy(plT[0:64, 2 * gp:2 * gp + 2, :],
                                                   bank[0:64, :].rearrange("p (a t) -> p a t", a=2)), key)
                    bank = take(dve, ("py", layer, src))
                    m = mix3[:, 2 * src:2 * src + 2, 512:768]
                    free(tt_(m, bank[:, :].rearrange("p (t n) -> p t n", t=NT),
                             bc(row2[:, lr2[f"pool{layer}"]], [P, NT, 256], 1), ALU.mult), ("py", layer, src))
                    stored(dve, ("py", layer, src))
                    link(tt_(m, m, z[:, 2 * src:2 * src + 2, BG:BG + 256], ALU.mult))
                for src in srcs:
                    if src == 1:
                        stored(dve, ("gb", layer, 0, 1))
                    link(tt_(diag2, id8, bc(mod2[:, layer, 16:24, src], [P, C, P], 2), ALU.mult))
                    dve.sem_inc(S("diag_ready"), 1)
                    dve.sem_inc(S("mix_ready"), 1)
                stored(dve, ("gb", layer, srcs[-1], 1))
                for i in range(N_OUT):
                    for src in srcs:
                        residual(("y2", layer, i, src), (x, c2)[src], g2b[:, src], i, ytmp2)
                if layer == 0:
                    dve.sem_inc(S("x_ready"), 1)
                else:
                    dve.sem_inc(S("x_final"), 1)


def weight_stream(i):
    def cols(w, starts):
        out = []
        for a in starts:
            t = w[:, a:a + WC]
            out.append(t.reshape(C, P, WC).transpose(1, 0, 2).reshape(P, WT))
        return out

    w_in = i["w_in"][0]
    small = np.concatenate([w_in[:, MG:MG + 16], w_in[:, GLR:GLR + 32], np.zeros((D, WC - 48), np.float32)], 1)
    mods = cols(i["w_mod"][0], range(0, 6 * D, WC))
    for l in range(2):
        mods += cols(i["w_mod_2"][l], range(0, 3 * D, WC))
    tiles = mods[:2 * MOD_FIRST] + cols(small, [0]) + cols(w_in, [a for a, _ in IN_TILES[1:]])
    tiles += mods[2 * MOD_FIRST:] + cols(i["w_out"][0], range(0, D, WC))
    tiles += cols(i["peer_wq"][0], range(0, 2048, WC))
    tiles.append(i["peer_keys"][0].transpose(3, 0, 1, 2).reshape(P, WT))
    u = i["peer_u"][0].reshape(P, N_PEER, 2, C, P).transpose(1, 4, 2, 3, 0).reshape(N_PEER, P, WT)
    v = i["peer_v"][0].reshape(P, N_PEER, 2, D).transpose(1, 0, 2, 3).reshape(N_PEER, P, WT)
    rest = []
    for l in range(2):
        rest += cols(i["w_in_2"][l], range(0, IN2, WC)) + cols(i["w_out_2"][l], range(0, D, WC))
    return np.concatenate([np.stack(tiles), u, v, np.stack(rest)])


def small_inputs(i):
    _, _, _, lv, _, _ = layouts()
    col = lambda a: np.asarray(a).reshape(-1, P).T
    v = np.zeros((P, lv.n), np.float32)
    cs = [i["c"], i["c_ctx"], i["c_2"], i["c_ctx_2"]]
    v[:, lv["cond"]] = np.stack([col(c) for c in cs], 2).reshape(P, 4 * C)
    v[:, lv["bmod1"]] = col(i["b_mod"])
    v[:, lv["bmod2"]] = col(i["b_mod_2"])
    v[:, lv["norm1"]] = col(i["norm1_g"])
    v[:, lv["norm2"]] = col(i["norm2_g"])
    v[:, lv["normg2"]] = col(i["norm_gain_2"])
    v[:, lv["conv"]] = col(i["ml_conv_w"])
    v[:, lv["alpha_b"]] = col(i["gla_alpha_b"])
    v[0:HEADS, lv["gate_b"]] = i["ml_gate_b"].reshape(4, HEADS).T
    r1 = np.concatenate([i["ml_norm_g"].ravel(), i["gla_norm_g"].ravel()])[None]
    r2 = np.concatenate([i[n][l].ravel() for l in range(2) for n in
                         ("att_q_gain_2", "att_k_gain_2", "na_q_gain_2", "na_k_gain_2", "pool_scale_2")])[None]
    return v, r1, r2


def kernel(**inputs):
    import concourse.bacc as bacc
    from concourse.bass_utils import run_bass_kernel_spmd

    i = {k: np.asarray(v) for k, v in inputs.items()}
    a, b, c, pool = constants()
    vec, row1, row2 = small_inputs(i)
    arrays = dict(W=weight_stream(i), CA=a, CB=b, CC=c, POOL=pool, VEC=vec, ROW1=row1,
                  NORMF=i["norm_f_g"][None], ROW2=row2, LRW2=i["gla_lr_w2"][0], POOLW=i["pool_w_2"],
                  X=i["x"], CTX=i["ctx"], CTX2=i["ctx_2"], RPB=i["na_rpb_2"][..., ::-1])
    arrays = {k: np.ascontiguousarray(v) for k, v in arrays.items()}
    nc = bacc.Bacc("TRN2", target_bir_lowering=False, num_devices=1)
    aps = {k: nc.dram_tensor(k, v.shape, F32, kind="ExternalInput").ap() for k, v in arrays.items()}
    out = nc.dram_tensor("OUT", (1, T, D), F32, kind="ExternalOutput").ap()
    build(nc, OUT=out, **aps)
    r = run_bass_kernel_spmd(nc, [arrays], core_ids=[0])
    return r.results[0]["OUT"]
```

```python
from contextlib import ExitStack
import numpy as np
import concourse.bass as bass
from concourse import mybir

F32 = mybir.dt.float32
F32R = mybir.dt.float32r
U32 = mybir.dt.uint32
ACT = mybir.ActivationFunctionType
ALU = mybir.AluOpType
AX = mybir.AxisListType.X

P = 128
D = 1024
C = D // P
T = 256
NT = T // P
GRID = 64
EPS = 1e-6
WT = 2048
WC = WT // C
WSLOTS = 4
HALF = WT // 2
NB = 6
HEADS = 4
GRANK = 16
GC = 64
NGC = T // GC
PH, PK, TOPK = 8, 128, 16
NEG = -1e30
BIG = -3e38

MQ, MK, MV, MO, MG = 0, 512, 1024, 1536, 2048
GQ, GK, GV, GR, GLR = 2064, 2320, 2576, 3088, 3600
IN_TILES = ([(None, 48)] + [(MQ + i * WC, WC) for i in range(2)] + [(MK + i * WC, WC) for i in range(2)]
            + [(MV + i * WC, WC) for i in range(2)] + [(MO + i * WC, WC) for i in range(2)]
            + [(GQ, WC), (GK, WC)] + [(GV + i * WC, WC) for i in range(2)] + [(GR + i * WC, WC) for i in range(2)])
N_MOD1, N_IN, N_OUT, N_WQ = 6 * D // WC, len(IN_TILES), D // WC, 2048 // WC
N_MOD2 = 3 * D // WC
MOD_UNITS = (N_MOD1 + 2 * N_MOD2) // 2
MOD_FIRST = 4
MOD_LATER = {"gr": 1, "mlstm": 2, "alpha": 1, "kdn": 2, "state": 1}
N_PRE = N_MOD1 + 2 * N_MOD2 + N_IN + N_OUT + N_WQ + 1
N_PEER = 64
U_HALF = N_PEER // 2 // WSLOTS
N_SPLIT1 = 2 * WSLOTS * U_HALF
N_SPLIT2 = 2 * N_SPLIT1
IN2 = 2816
N_IN2 = IN2 // WC
N_TILES = N_PRE + 2 * N_PEER + 2 * (N_IN2 + N_OUT)
AQ, AK, AV, AG, BZ, BG, NQ, NK, NV, NG = 0, 512, 640, 768, 1280, 1536, 1792, 2048, 2304, 2560
WINDOWS = (2, 4, 8, 16)


N_CONST, N_CONST2 = 7, 5


def gla_chunk(n, d):
    if n < NGC:
        return NGC + n if d == 0 else 2 * NGC - 1 - n
    return n - NGC if d == 0 else 2 * NGC - 1 - n


def attn_list(layer):
    return [(layer, src, kind, tt, h) for src in ((0, 1) if layer == 0 else (0,))
            for kind, heads in (("a", 8), ("n", 4)) for tt in range(NT) for h in range(heads)]


ATTN_ALL = attn_list(0) + attn_list(1)
ATTN_GROUPS = list(dict.fromkeys(a[:4] for a in ATTN_ALL))


def attn_index(a):
    return ATTN_ALL.index(a)


def attn_group(*g):
    return ATTN_GROUPS.index(g)


def qk_pairs(layer, src):
    ps = [("aqT", h, AQ + 64 * h) for h in range(0, 8, 2)] + [("akT", 0, AK)]
    ps += [("nqT", h, NQ + 64 * h) for h in (0, 2)] + [("nkT", h, NK + 64 * h) for h in (0, 2)]
    if layer == 1 and src == 1:
        ps = [q for q in ps if q[0] in ("akT", "nkT")]
    return ps


def norm_groups(layer, src):
    gs = [(AQ, 8, "aq"), (AK, 2, "ak"), (NQ, 4, "nq"), (NK, 4, "nk")]
    if layer == 1 and src == 1:
        gs = [g for g in gs if g[2] in ("ak", "nk")]
    return gs


def norm_spans(layer, src):
    gs = norm_groups(layer, src)
    if len(gs) == 2:
        return [(c, h, [(0, h, n)]) for c, h, n in gs]
    return [(a[0], a[1] + b[1], [(0, a[1], a[2]), (a[1], b[1], b[2])]) for a, b in (gs[0:2], gs[2:4])]


def n_norms(layer, src):
    return NT * sum(g[1] for g in norm_groups(layer, src))


Z_ORDER = tuple(c // WC for c in (AQ, AQ + WC, AK, NQ, NK, NV, BZ, AG, AG + WC, BG, NG))
Z_GATES = tuple(c // WC for c in (AG, AG + WC, BG, NG))
Z_QK = 5


def z_tiles(layer, src):
    return tuple(i for i in Z_ORDER if layer == 0 or src == 0 or i in (AK // WC, NK // WC, NV // WC))


class Layout:
    def __init__(self):
        self.at, self.n = {}, 0

    def add(self, name, n):
        self.at[name] = (self.n, n)
        self.n += n

    def __getitem__(self, name):
        o, n = self.at[name]
        return slice(o, o + n)


def layouts():
    a, b, c, v, r1, r2 = (Layout() for _ in range(6))
    for n, w in (("ident", P), ("ones", P), ("zero", P), ("iota", P)):
        a.add(n, w)
    for n, w in (("tri_ml", 2 * 256), ("tri_gla", 2 * P), ("sel", HEADS * P), ("reset", 2 * T), ("half", 2)):
        b.add(n, w)
    for n, w in (("cos", NT * 64), ("sin", NT * 64), ("namask", GRID)):
        c.add(n, w)
    for n, w in (("cond", 4 * C), ("bmod1", 48), ("bmod2", 48), ("norm1", C), ("norm2", C), ("normg2", 2 * C),
                 ("conv", 3 * C), ("alpha_b", 4), ("gate_b", 4)):
        v.add(n, w)
    for n, w in (("ml_g", 512), ("gla_g", 512)):
        r1.add(n, w)
    for layer in range(2):
        for n, w in ((f"aq{layer}", 64), (f"ak{layer}", 64), (f"nq{layer}", 64), (f"nk{layer}", 64),
                     (f"pool{layer}", 256)):
            r2.add(n, w)
    return a, b, c, v, r1, r2


def constants():
    a, b, c, _, _, _ = layouts()
    A = np.zeros((P, a.n), np.float32)
    A[:, a["ident"]] = np.eye(P)
    A[:, a["ones"]] = 1
    A[:, a["iota"]] = np.arange(P)
    B = np.zeros((P, b.n), np.float32)
    s, t = np.arange(P)[:, None], np.arange(P)[None, :]
    fwd = np.where(t >= s, 0, NEG)
    bwd = np.where(t <= s, 0, NEG)
    B[:, b["tri_ml"]] = np.concatenate([fwd, fwd, bwd, bwd], 1)
    same = s // GC == t // GC
    B[:, b["tri_gla"]] = np.concatenate([(same & (t >= s)), (same & (t <= s))], 1)
    for h in range(HEADS):
        B[h, b["sel"].start + h * P:b["sel"].start + (h + 1) * P] = 1
    B[:, b["reset"]] = (np.arange(2 * T) % GC != 0)
    B[:, b["half"]] = np.concatenate([s < GC, s >= GC], 1)
    Cc = np.zeros((P, c.n), np.float32)
    inv = (10000.0 ** (-np.arange(16, dtype=np.float32) / np.float32(16))).astype(np.float32)
    for tt in range(NT):
        tok = tt * P + np.arange(P)
        ar, ac = (tok // GRID).astype(np.float32)[:, None] * inv, (tok % GRID).astype(np.float32)[:, None] * inv
        o = c["cos"].start + tt * 64
        Cc[:, o:o + 64] = np.concatenate([np.cos(ar), np.cos(ar), np.cos(ac), np.cos(ac)], 1)
        o = c["sin"].start + tt * 64
        Cc[:, o:o + 64] = np.concatenate([-np.sin(ar), np.sin(ar), -np.sin(ac), np.sin(ac)], 1)
    qc = (np.arange(P) % GRID)[:, None]
    c0 = np.clip(qc - 8, 0, GRID - 16)
    kc = np.arange(GRID)[None, :]
    Cc[:, c["namask"]] = np.where((kc >= c0) & (kc < c0 + 16), 0, NEG)
    pool = np.zeros((NT, P, 4, T), np.float32)
    for g, w in enumerate(WINDOWS):
        for tq in range(T):
            lo, hi = max(tq - w // 2, 0), min(tq + w // 2 - 1, T - 1)
            col = np.zeros(T, np.float32)
            col[lo:hi + 1] = np.float32(1) / np.float32(hi - lo + 1)
            col[tq] -= 1
            pool[:, :, g, tq] = col.reshape(NT, P)
    return A, B, Cc, np.ascontiguousarray(pool.transpose(1, 0, 2, 3).reshape(P, NT * 4 * T))


def build(nc, W, CA, CB, CC, POOL, VEC, ROW1, NORMF, ROW2, LRW2, POOLW, X, CTX, CTX2, RPB, OUT):
    la, lb, lc, lv, lr1, lr2 = layouts()
    with ExitStack() as ctx:
        def sb(name, shape):
            return ctx.enter_context(nc.sbuf_tensor(name, shape, F32))

        sems = {}

        def S(name):
            if name not in sems:
                sems[name] = ctx.enter_context(nc.semaphore(name))
            return sems[name]

        cA = sb("cA", [P, la.n])
        vec = sb("vec", [P, lv.n])
        x = sb("x", [P, NT, D])
        h2T = sb("h2T", [P, C, T])
        ring_at = nc.sbuf_base
        ring = sb("ring", [P, WSLOTS, WT])
        cond = sb("cond", [P, C, 4])
        condt = sb("condt", [P, C, 4])
        mod1 = sb("mod1", [P, 48, 2])
        mod2 = sb("mod2", [P, 2, 24, 2])
        gain = sb("gain", [P, 5, C])
        rs = sb("rs", [P, 6, 80])
        tiny = sb("tiny", [P, 6, 16])
        AR = 39000
        arena_at = nc.sbuf_base
        arena = sb("arena", [P, AR])
        banks = [ctx.enter_context(nc.psum_tensor(f"bank{i}", [P, 512], F32)) for i in range(8)]
        ident = cA[:, la["ident"]]
        ones = cA[:, la["ones"]]
        zero = cA[:, la["zero"]]
        iota = cA[:, la["iota"]]

        w_rest = nc.alloc_sbuf_tensor_at("w_rest", [P, WSLOTS, WT], F32R, offset=ring_at)
        cursor = [0]

        def shaped(ap, shape):
            if len(shape) == 2:
                return ap.rearrange("p (a b) -> p a b", a=shape[0])
            if len(shape) == 3:
                return ap.rearrange("p (a b c) -> p a b c", a=shape[0], b=shape[1])
            if len(shape) == 4:
                return ap.rearrange("p (a b c d) -> p a b c d", a=shape[0], b=shape[1], c=shape[2])
            return ap

        def region(off, *shape):
            n = int(np.prod(shape))
            assert off + n <= AR, (off, n)
            return shaped(arena[:, off:off + n], shape)

        def bump(*shape):
            r = region(cursor[0], *shape)
            cursor[0] += int(np.prod(shape))
            return r

        def parts(name, at, *shape):
            return nc.alloc_sbuf_tensor_at(name, [P] + list(shape), F32R, offset=at)

        cB = bump(lb.n)
        row1 = bump(lr1.n)
        cq = bump(HEADS, T)
        ck = bump(HEADS, 2 * T)
        vml = bump(4, HEADS, P + 1)
        og = bump(NT, D)
        gqT = bump(2, T)
        gkT = bump(2, 2 * T)
        gv = bump(4, 512)
        glrT = bump(2, 2 * T)
        lrw2 = bump(2, 256)
        cursor[0] += -cursor[0] % 8
        base = cursor[0]
        hT = bump(C, 2 * T)
        EW, PW = region(base, 2, 4, T), region(base + 2048, 2, 4, T)
        h1_rest = parts("h1_rest", arena_at + 4 * base, C, 2 * T)
        h1_high = parts("h1_high", arena_at + 4 * cursor[0], 2, C, T)
        xn = bump(4, D)
        wx_high = parts("wx_high", arena_at + 4 * cursor[0], WT)
        cx = bump(NT, D)
        gi = bump(2, 2 * T)
        gf = bump(2, 2 * T)
        gtmp = bump(2, 2 * T)
        gb = bump(2, 2 * T)
        negA = bump(2, 2 * T)
        nM = bump(2, 2 * T)
        em = bump(2, T)
        acol = bump(4, 2, HEADS)
        emcol = bump(NT, 2, HEADS)
        dn = bump(4, NT)
        sqj = bump(D)
        cursor[0] += -cursor[0] % 8
        wy_high = parts("wy_high", arena_at + 4 * cursor[0], WT)
        assert cursor[0] + WT <= AR - 1024
        cursor[0] = base
        lt = bump(2, 2, 2 * T)
        lx = bump(2, 2, 2 * T)
        lbm = bump(2, 2, 2 * T)
        qz = bump(2, 2, 2, T)
        kz = bump(2, 2, T)
        qs = bump(2, 2, 2, T)
        kdn = bump(2, 4, 2, 256)
        att = bump(2, HEADS, P)
        Sst = bump(2, NGC, 2, 256)
        Sct = bump(2, 2, 2, 256)
        eend = bump(2, 2, 8)
        hcat = shaped(h2T[:, :, :].rearrange("p c t -> p (c t)"), (NT, D))
        assert cursor[0] <= AR - 1024
        modrow = region(AR - 1024, 2, 512)
        cursor[0] = base
        mix = bump(NT, D)
        mixT = bump(C, T)
        gbc = bump(D)
        sq2 = bump(D)
        ytmp = bump(NT, WC)
        diag = bump(C, P)
        xn2 = bump(NT, D)
        GH = region(0, P, T)
        cursor[0] = 64 * T
        qTp = bump(16, T)
        cand, work = region(64 * T, PH, 256), region(64 * T + 2048, 256)
        sc = bump(NT, 16, PK)
        tops = bump(NT, 16, TOPK)
        topi = bump(NT, 16, TOPK)
        topf = bump(NT, 16, TOPK)
        bests = bump(NT, PH, TOPK)
        bestc = bump(NT, PH, TOPK)
        bhl = bump(2, PH, TOPK)
        onek = bump(PH, TOPK, TOPK)
        smx = bump(4, 16)
        sels = bump(NT, 3, P)
        assert cursor[0] <= P * T
        cursor[0] = P * T
        peT = h2T
        w_high = parts("w_high", arena_at + 4 * cursor[0], 2, HALF)
        dif = bump(2, 4, P)
        cursor[0] += 2 * HALF - 2 * 4 * P
        h2_high = parts("h2_high", arena_at + 4 * cursor[0], C, T)
        g_high = parts("g_high", arena_at + 4 * cursor[0], 2, 2, T)
        g_rest = parts("g_rest", arena_at + 4 * cursor[0] + 4096, 2, 2, T)
        oh = bump(2, 2, 4, P)
        h2_rest = parts("h2_rest", arena_at + 4 * cursor[0], C, T)
        selT = bump(3, T)
        cursor[0] += C * T - 3 * T
        assert cursor[0] <= AR
        cursor[0] = 0
        hT2, mixT3 = region(0, C, 2 * T), region(0, 2, C, T)
        in_rest = parts("in_rest", arena_at, 2 * C * T)
        in_high = parts("in_high", arena_at + 4 * 2 * C * T, 2 * C * T)
        aqT = bump(8, T)
        akT = bump(2, 2 * T)
        nqT = bump(4, T)
        assert cursor[0] == 2 * C * T
        nkT = bump(4, 2 * T)
        bm = bump(NT, HEADS, T)
        wq_high = parts("wq_high", arena_at + 4 * cursor[0], 4, IN2)
        z = bump(4, IN2)
        wb_high = parts("wb_high", arena_at + 4 * cursor[0], WT)
        xn3 = bump(4, D)
        mix3 = xn3
        rt = bump(2, 640)
        wa_high = parts("wa_high", arena_at + 4 * cursor[0], WT)
        ytmp2 = shaped(rt[:, 0, 0:512], (NT, WC))
        pw = bump(2, 512)
        pt = bump(2, 4, P)
        diag2 = region(cursor[0] - 2048, C, P)
        plT = bump(4, T)
        braw = bump(NT, HEADS, T)
        poolc = bump(NT, 4, T)
        row2 = bump(lr2.n)
        normf = bump(D)
        plw = bump(2, 4, 64)
        cC = bump(lc.n)
        g2b = bump(2, D)
        c2 = bump(NT, D)
        assert cursor[0] - NT * D >= P * T + 4096

        def high_of(m):
            i = m % (N_IN2 + N_OUT)
            if i < N_IN2:
                return (wb_high if i % 2 else wa_high)[:, :].rearrange("p (a n) -> p a n", a=4)
            return (wb_high[:, :].rearrange("p (a n) -> p a n", a=4) if (i - N_IN2) % 2
                    else wq_high[:, :, 0:2 * WC])

        units, order, emptied_n = {}, [], {"dve": 0, "act": 0}
        tiles_n, before_peer = [0], {}

        def stored(eng, key):
            u = units[key]
            eng.wait_ge(S("emptied_" + u["by"]), u["idx"] + 1)

        def take(eng, key):
            u = units[key]
            eng.wait_ge(S(u["sem"]), u["val"])
            return banks[u["bank"]]

        freed = {"dve": 0, "act": 0}

        def free(ins, key):
            u = units[key]
            assert freed[u["by"]] == u["idx"], (key, freed, u)
            freed[u["by"]] += 1
            ins.then_inc(S("emptied_" + u["by"]), 1)

        def w3(w):
            return w.rearrange("p (c n) -> p c n", c=C)

        block = ctx.enter_context(nc.Block())

        @block.tensor
        def _(pe):
            opened = [None]

            def qk_transpose(layer, src, n, col):
                bank = open_unit(("qk", layer, src, n), "act" if n % 2 else "dve")
                for k in range(2):
                    for tt in range(NT):
                        last = pe.transpose(bank[0:64, k * T + tt * P:k * T + tt * P + P],
                                            z[:, 2 * src + tt, col + 64 * k:col + 64 * k + 64], ident)
                close_unit(last)

            def open_unit(key, by):
                n = len(order)
                if n >= NB:
                    stored(pe, order[n - NB])
                assert opened[0] is None
                opened[0] = key
                units[key] = dict(bank=n % NB, by=by, idx=emptied_n[by])
                emptied_n[by] += 1
                order.append(key)
                return banks[n % NB]

            filled = [0]

            def close_unit(ins, weights=False):
                u = units[opened[0]]
                opened[0] = None
                if weights:
                    u["sem"], u["val"] = "tile_used", tiles_n[0]
                    ins.then_inc(S("tile_used"), 1)
                else:
                    filled[0] += 1
                    u["sem"], u["val"] = "unit_filled", filled[0]
                    ins.then_inc(S("unit_filled"), 1)

            def weights():
                n = tiles_n[0]
                tiles_n[0] += 1
                pe.wait_ge(S(f"tile_landed{n % WSLOTS}"), 16 * (n // WSLOTS + 1))
                return ring[:, n % WSLOTS, :]

            def mm(out, lhsT, rhs, c=0, n=1):
                return pe.matmul(out, lhsT=lhsT, rhs=rhs, start=(c == 0), stop=(c == n - 1))

            mod_at = [0]

            def modulation(n=1):
                for _ in range(n):
                    u = mod_at[0]
                    if u == MOD_UNITS:
                        return
                    mod_at[0] += 1
                    lo = 0 if u < N_MOD1 // 2 else 2
                    bank = open_unit(("modrow", u), "act")
                    for k in range(2):
                        w = w3(weights())
                        for c in range(C):
                            last = mm(bank[0:2, k * WC:(k + 1) * WC], cond[:, c, lo:lo + 2], w[:, c, :], c, C)
                        if k == 0:
                            last.then_inc(S("tile_used"), 1)
                    close_unit(last, weights=True)
                    if u not in (0, MOD_FIRST):
                        mod_columns(u - 1)
                    if u in (MOD_FIRST - 1, MOD_UNITS - 1):
                        mod_columns(u)

            def mod_columns(u):
                stored(pe, ("modrow", u))
                for k in range(4):
                    o = (4 * u + k) * 2
                    last = pe.transpose(banks[7][:, o:o + 2], modrow[0:2, u % 2, k * P:(k + 1) * P], ident[0:2, 0:2])
                last.then_inc(S("mod_columns"), 1)

            def transposed(key, src_tiles, by):
                for cc in range(4):
                    bank = open_unit(key + (cc,), by)
                    for k in range(2):
                        for tt in range(NT):
                            last = pe.transpose(bank[:, k * T + tt * P:k * T + tt * P + P],
                                                src_tiles[tt][:, (2 * cc + k) * P:(2 * cc + k + 1) * P], ident)
                    close_unit(last)

            def rows_of(key, hsrc, cols, w, by, weights=False):
                bank = open_unit(key, by)
                for tt in range(NT):
                    for c in range(C):
                        last = mm(bank[:, tt * WC:(tt + 1) * WC], hsrc[:, c, cols + tt * P:cols + tt * P + P],
                                  w[:, c, :], c, C)
                close_unit(last, weights)

            pe.wait_ge(S("const_loaded"), 16 * N_CONST)
            pe.wait_ge(S("cond_ready"), 1)
            modulation(MOD_FIRST)

            for src in range(2):
                pe.wait_ge(S("xn_ready"), 2 * src + 2)
                transposed(("hT", src), [xn[:, 2 * src + tt, :] for tt in range(NT)], "dve")
            pe.wait_ge(S("in_rest_ready"), 8)

            def w1():
                j, n = tiles_n[0] - 2 * MOD_FIRST, tiles_n[0]
                tiles_n[0] += 1
                pe.wait_ge(S("w1_high_ready"), j + 1)
                pe.wait_ge(S("w1_rest_ready"), j + 1)
                return w3((wy_high if j % 2 else wx_high)[:, :]), w3(w_rest[:, n % WSLOTS, :])

            hb = h1_high[:, :, :, :], h1_rest[:, :, :].rearrange("p c (s t) -> p s c t", s=2)

            def in_parts(out, terms):
                for n, (lhsT, rhs) in enumerate(terms):
                    last = pe.matmul(out, lhsT=lhsT, rhs=rhs, start=(n == 0), stop=(n == len(terms) - 1))
                return last

            def features(out, w, cols, srcs):
                return in_parts(out, [(w[i][:, c, cols], hb[j][:, srcs, c, :])
                                      for i, j in ((0, 0), (0, 1), (1, 0)) for c in range(C)])

            def rows1(key, src, w, weights=False):
                bank = open_unit(key, "act")
                for tt in range(NT):
                    last = in_parts(bank[:, tt * WC:(tt + 1) * WC],
                                    [(hb[j][:, src, c, tt * P:(tt + 1) * P], w[i][:, c, :])
                                     for i, j in ((0, 0), (0, 1), (1, 0)) for c in range(C)])
                close_unit(last, weights)

            both = slice(0, 2)
            w = w1()
            for d in range(2):
                for g in range(2):
                    bank = open_unit(("gate", d, g), "dve")
                    close_unit(features(bank[0:HEADS, :], w, slice(d * 8 + g * 4, d * 8 + g * 4 + 4), both))
            for d in range(2):
                bank = open_unit(("glr", d), "act")
                close_unit(features(bank[0:GRANK, :], w, slice(16 + d * GRANK, 16 + (d + 1) * GRANK), both),
                           weights=(d == 1))
            for i in range(2):
                w = w1()
                bank = open_unit(("mq", i), "dve")
                for k in range(2):
                    last = features(bank[:, k * T:(k + 1) * T], w, slice(k * P, (k + 1) * P), 0)
                close_unit(last, weights=True)
            for i in range(2):
                w = w1()
                for k in range(2):
                    bank = open_unit(("mk", 2 * i + k), "dve")
                    close_unit(features(bank[:, :], w, slice(k * P, (k + 1) * P), both), weights=(k == 1))
            for i in range(2):
                w = w1()
                rows1(("mv", i, 0), 0, w)
                rows1(("mv", i, 1), 1, w, weights=True)
            for i in range(2):
                rows1(("mo", i), 0, w1(), weights=True)
            w = w1()
            bank = open_unit(("gq",), "act")
            for k in range(2):
                last = features(bank[:, k * T:(k + 1) * T], w, slice(k * P, (k + 1) * P), 0)
            close_unit(last, weights=True)
            w = w1()
            for k in range(2):
                bank = open_unit(("gk", k), "act")
                close_unit(features(bank[:, :], w, slice(k * P, (k + 1) * P), both), weights=(k == 1))
            for i in range(2):
                w = w1()
                rows1(("gv", i, 0), 0, w)
                rows1(("gv", i, 1), 1, w, weights=True)
            for i in range(2):
                rows1(("gr", i), 0, w1(), weights=True)
            modulation(MOD_LATER["gr"])

            pe.wait_ge(S("gate_rows_ready"), 1)
            bank = open_unit(("acol",), "dve")
            for d in range(2):
                for st in range(4):
                    o = (st * 2 + d) * HEADS
                    last = pe.transpose(bank[:, o:o + HEADS], negA[0:HEADS, d, st * P:(st + 1) * P],
                                        ident[0:HEADS, 0:HEADS])
            close_unit(last)
            pe.wait_ge(S("em_ready"), 1)
            bank = open_unit(("emcol",), "dve")
            for d in range(2):
                for tt in range(NT):
                    o = (tt * 2 + d) * HEADS
                    last = pe.transpose(bank[:, o:o + HEADS], em[0:HEADS, d, tt * P:(tt + 1) * P],
                                        ident[0:HEADS, 0:HEADS])
            close_unit(last)
            pe.wait_ge(S("conv_ready"), 1)
            for h in range(HEADS):
                sel_h = cB[0:HEADS, lb["sel"].start + h * P:lb["sel"].start + (h + 1) * P]
                for src in range(2):
                    bank = open_unit(("S", h, src), "dve")
                    for st in range(2):
                        last = mm(bank[:, st * T:(st + 1) * T], ck[:, h, src * T + st * P:src * T + (st + 1) * P],
                                  cq[:, h, :])
                    close_unit(last)
                for d in range(2):
                    bank = open_unit(("E", h, d), "act")
                    mm(bank[:, 0:T], sel_h, nM[0:HEADS, d, 0:T])
                    pe.matmul(bank[:, T:2 * T], lhsT=sel_h, rhs=nM[0:HEADS, d, 0:T], start=True, stop=False)
                    o = lb["tri_ml"].start + d * T
                    close_unit(pe.matmul(bank[:, T:2 * T], lhsT=ident, rhs=cB[:, o:o + T], start=False, stop=True))
                for d in range(2):
                    bank = open_unit(("O", h, d), "dve")
                    pe.wait_ge(S("P_ready"), 2 * h + d + 1)
                    for tt in range(NT):
                        sts = [2, 3] + [s for s in range(2) if (s <= tt if d == 0 else s >= tt)]
                        for n, st in enumerate(sts):
                            last = mm(bank[:, tt * 256:tt * 256 + P + 1], PW[:, d, st, tt * P:(tt + 1) * P],
                                      vml[:, st, h, :], n, len(sts))
                    close_unit(last)
                modulation(MOD_LATER["mlstm"])

            for d in range(2):
                for j in range(2):
                    bank = open_unit(("alpha", d, j), "dve")
                    close_unit(mm(bank[:, :], lrw2[0:GRANK, d, j * P:(j + 1) * P], glrT[0:GRANK, d, :]))
            modulation(MOD_LATER["alpha"])
            pe.wait_ge(S("kdec_ready"), 1)
            for d in range(2):
                for src in range(2):
                    bank = open_unit(("kdn", d, src), "dve")
                    for tt in range(NT):
                        for j in range(2):
                            o = tt * 256 + j * P
                            last = pe.transpose(bank[:, o:o + P],
                                                lx[:, d, j, src * T + tt * P:src * T + (tt + 1) * P], ident)
                    close_unit(last)
            modulation(MOD_LATER["kdn"])
            for step in range(7):
                for d in range(2):
                    c = gla_chunk(step, d)
                    bank = open_unit(("St", step, d), "dve")
                    if step == 0:
                        stored(pe, ("kdn", 1, 1))
                    for j in range(2):
                        last = mm(bank[:, j * 256:(j + 1) * 256], kdn[:, d, c // 2, c % 2, j * P:(j + 1) * P],
                                  gv[:, c // 2, j * 256:(j + 1) * 256])
                    close_unit(last)
                modulation(MOD_LATER["state"])
            pe.wait_ge(S("gla_q_ready"), 1)
            for tt in range(NT):
                for d in range(2):
                    bank = open_unit(("att", tt, d), "dve")
                    for h in range(HEADS):
                        last = mm(bank[:, h * P:(h + 1) * P], kz[:, d, h // 2, tt * P:(tt + 1) * P],
                                  qz[:, d, h % 2, h // 2, tt * P:(tt + 1) * P])
                    close_unit(last)
                bank = open_unit(("gla", tt), "dve")
                stored(pe, ("att", tt, 1))
                for h in range(HEADS):
                    for d in range(2):
                        mm(bank[:, h * P:(h + 1) * P], att[:, d, h, :], gv[:, tt, h * P:(h + 1) * P], d, 99)
                    for d in range(2):
                        for par in range(2):
                            last = mm(bank[:, h * P:(h + 1) * P], qs[:, d, par, h // 2, tt * P:(tt + 1) * P],
                                      Sst[:, d, 2 * tt + par, h // 2, (h % 2) * P:(h % 2 + 1) * P],
                                      3 if d and par else 1, 4)
                close_unit(last)

            modulation(MOD_UNITS)

            pe.wait_ge(S("diag_ready"), 1)
            for half in range(2):
                bank = open_unit(("gbc", half), "act")
                close_unit(mm(bank[:, :], ones, diag[:, 4 * half:4 * half + 4, :]))
            pe.wait_ge(S("mix_ready"), 1)
            transposed(("mixT",), [mix[:, tt, :] for tt in range(NT)], "act")
            stored(pe, ("mixT", 3))
            for i in range(N_OUT):
                rows_of(("y", i), mixT, 0, w3(weights()), "dve", weights=True)

            pe.wait_ge(S("xn_ready"), 6)
            transposed(("h2T",), [xn2[:, tt, :] for tt in range(NT)], "dve")
            stored(pe, ("h2T", 3))
            for i in range(N_WQ):
                w = w3(weights())
                bank = open_unit(("wq", i), "act")
                for k in range(2):
                    for c in range(C):
                        last = mm(bank[:, k * T:(k + 1) * T], w[:, c, k * P:(k + 1) * P], h2T[:, c, :], c, C)
                close_unit(last, weights=True)
            keys = weights().rearrange("p (a b) -> p a b", a=16)
            stored(pe, ("wq", N_WQ - 1))
            for tt in range(NT):
                for q in range(4):
                    bank = open_unit(("sc", tt, q), "act")
                    for k in range(4):
                        last = mm(bank[:, k * P:(k + 1) * P], qTp[:, 4 * q + k, tt * P:(tt + 1) * P],
                                  keys[:, 4 * q + k, :])
                    close_unit(last, weights=(tt == 1 and q == 3))
            assert tiles_n[0] == N_PRE and N_PRE % WSLOTS == 0

            before_peer.update(emptied_n)
            pe.wait_ge(S("emptied_dve"), emptied_n["dve"])
            pe.wait_ge(S("emptied_act"), emptied_n["act"])

            def three(out, highs, rests, wh, wr, idx, first):
                pe.wait_ge(S("w_high_ready"), idx)
                for c in range(C):
                    pe.matmul(out(c), lhsT=wh[:, c, :], rhs=highs(c), start=(first and c == 0), stop=False,
                              skip_group_check=True)
                    last = pe.matmul(out(c), lhsT=wh[:, c, :], rhs=rests(c), start=False, stop=False,
                                     skip_group_check=True)
                last.then_inc(S("w_high_used"), 1)
                pe.wait_ge(S("w_rest_ready"), idx)
                for c in range(C):
                    last = pe.matmul(out(c), lhsT=wr[:, c, :], rhs=highs(c), start=False, stop=(first and c == C - 1),
                                     skip_group_check=True)
                return last

            def experts(first, split_before):
                with pe.Fori(0, U_HALF) as it:
                    for k in range(WSLOTS):
                        landed = pe.snap(it * 16 + 16 * ((N_PRE + first) // WSLOTS + 1))
                        free_n = pe.snap(it * WSLOTS + first + k + 1)
                        idx = [pe.snap(it * (2 * WSLOTS) + split_before + 2 * k + a + 1) for a in range(2)]
                        pe.wait_ge(S(f"tile_landed{k}"), landed)
                        pe.wait_ge(S("u_bank_free"), free_n)
                        wr = w_rest[:, k, :].rearrange("p (a c n) -> p a c n", a=2, c=C)
                        for a in range(2):
                            out = banks[k][:, a * T:(a + 1) * T]
                            last = three(lambda c: out, lambda c: h2_high[:, c, :], lambda c: h2_rest[:, c, :],
                                         w_high[:, a, :].rearrange("p (c n) -> p c n", c=C), wr[:, a], idx[a], True)
                        last.then_inc(S("tile_used"), 1)

            pe.wait_ge(S("h2_rest_ready"), 1)
            experts(0, 0)
            pe.wait_ge(S("topk_done"), 1)
            for f in range(3):
                for tt in range(NT):
                    o = (f % 2) * T + tt * P
                    last = pe.transpose(banks[6 + f // 2][:, o:o + P], sels[:, tt, f, :], ident)
            last.then_inc(S("selT_filled"), 1)
            experts(N_PEER // 2, N_SPLIT1)

            with pe.Fori(0, T // 8) as it:
                for b in range(2):
                    n = pe.snap(it * 2 + b + 1)
                    pe.wait_ge(S("oh_ready"), n)
                    pe.wait_ge(S("oh2_ready"), n)
                    pe.wait_ge(S("w_bank_free"), n)
                    for k in range(4):
                        last = mm(banks[4 + b][:, k * P:(k + 1) * P], oh[:, b, 0, k, :], oh[:, b, 1, k, :])
                    last.then_inc(S("w_filled"), 1)

            pe.wait_ge(S("w_bank_free"), 2 + T // 4)
            for k in range(4):
                pe.matmul(banks[k][:, :], lhsT=zero, rhs=h2T[:, 0:2, :], start=True, stop=False,
                          skip_group_check=True)
            with pe.Fori(0, N_PEER // WSLOTS) as it:
                for k in range(WSLOTS):
                    g_n = pe.snap(it * WSLOTS + k + 1)
                    idx = [pe.snap(it * (2 * WSLOTS) + N_SPLIT2 + 2 * k + a + 1) for a in range(2)]
                    wr = w_rest[:, k, :].rearrange("p (a c n) -> p a c n", a=2, c=C)
                    pe.wait_ge(S("g_rest_ready"), g_n)
                    for a in range(2):
                        last = three(lambda c: banks[c // 2][:, (c % 2) * T:(c % 2 + 1) * T],
                                     lambda c: g_high[:, k % 2, a, :], lambda c: g_rest[:, k % 2, a, :],
                                     w_high[:, a, :].rearrange("p (c n) -> p c n", c=C), wr[:, a], idx[a], False)
                    last.then_inc(S("tile_used"), 1)
            tiles_n[0] = N_PRE + 2 * N_PEER
            pe.wait_ge(S("peT_ready"), 1)
            for tt in range(NT):
                for half in range(2):
                    bank = open_unit(("pe", tt, half), "dve")
                    for k in range(4):
                        last = pe.transpose(bank[:, k * P:(k + 1) * P], peT[:, 4 * half + k, tt * P:(tt + 1) * P],
                                            ident)
                    close_unit(last)

            n_xn, n_attn, n_gap, parts_n = 6, 0, 0, 8
            hT_parts = [p.rearrange("p (c t) -> p c t", c=C) for p in (in_high[:, :], in_rest[:, :])]
            mT_parts = [[p.rearrange("p (s c t) -> p s c t", s=2, c=C)[:, src] for p in (in_high[:, :], in_rest[:, :])]
                        for src in range(2)]

            def weights_in_parts():
                n = tiles_n[0]
                m = n - N_PRE - 2 * N_PEER
                tiles_n[0] += 1
                pe.wait_ge(S("w2_high_ready"), m + 1)
                pe.wait_ge(S("w2_rest_ready"), m + 1)
                return high_of(m), w3(w_rest[:, n % WSLOTS, :])

            def rows_in_parts(key, h, cols, w, by, weights):
                bank = open_unit(key, by)
                for tt in range(NT):
                    at = slice(cols + tt * P, cols + tt * P + P)
                    for i, (hp, wp) in enumerate(((h[0], w[0]), (h[1], w[0]), (h[0], w[1]))):
                        for c in range(C):
                            wc = wp[:, c, :] if i == 2 else wp[:, c // 2, c % 2 * WC:(c % 2 + 1) * WC]
                            last = pe.matmul(bank[:, tt * WC:(tt + 1) * WC], lhsT=hp[:, c, at], rhs=wc,
                                             start=(i == 0 and c == 0), stop=(i == 2 and c == C - 1))
                close_unit(last, weights)

            for layer in range(2):
                n_xn += 2
                pe.wait_ge(S("xn_ready"), n_xn)
                transposed(("hT2", layer, 0), [xn3[:, tt, :] for tt in range(NT)], "dve")
                pe.wait_ge(S("in_rest_ready"), parts_n + 4)
                for pos, i in enumerate(Z_ORDER):
                    w = weights_in_parts()
                    two = i in z_tiles(layer, 1)
                    rows_in_parts(("z", layer, i, 0), hT_parts, 0, w, "act", weights=not two)
                    if pos == 0:
                        n_xn += 2
                        pe.wait_ge(S("xn_ready"), n_xn)
                        transposed(("hT2", layer, 1), [xn3[:, 2 + tt, :] for tt in range(NT)], "dve")
                        parts_n += 8
                        pe.wait_ge(S("in_rest_ready"), parts_n)
                    if two:
                        rows_in_parts(("z", layer, i, 1), hT_parts, T, w, "act", weights=True)
                stored(pe, ("z", layer, Z_ORDER[-1], 0 if layer else 1))
                pe.wait_ge(S("const2_loaded"), 16 * N_CONST2)
                for src in range(2):
                    pe.wait_ge(S("qk_ready"), 2 * layer + src + 1)
                    if src == 1:
                        continue
                    for n, (buf, h, col) in enumerate(qk_pairs(layer, src)):
                        qk_transpose(layer, src, n, col)
                for n, (buf, h, col) in enumerate(qk_pairs(layer, 1)):
                    if buf in ("akT", "nkT"):
                        qk_transpose(layer, 1, n, col)
                todo = attn_list(layer)
                for part in range(1 if layer else 2):
                    mine = [a for a in todo if a[1] == part]
                    if part == 1:
                        for n, (buf, h, col) in enumerate(qk_pairs(layer, 1)):
                            if buf in ("aqT", "nqT"):
                                qk_transpose(layer, 1, n, col)
                    stored(pe, [k for k in order if k[0] == "qk" and units[k]["by"] == "act"][-1])
                    stored(pe, [k for k in order if k[0] == "qk" and units[k]["by"] == "dve"][-1])

                    def scores(a):
                        _, src, kind, tt, h = a
                        lo, n = (0, 512) if src == 0 else (T, T)
                        q, k = (aqT[0:64, h, :], akT[0:64, h // 4, :]) if kind == "a" else \
                               (nqT[0:64, h, :], nkT[0:64, h, :])
                        bank = open_unit(("s",) + a, "act")
                        biased = kind == "n" and src == 0
                        last = pe.matmul(bank[:, 0:n], lhsT=q[:, tt * P:(tt + 1) * P], rhs=k[:, lo:lo + n],
                                         start=True, stop=not biased)
                        if biased:
                            if (tt, h) == (0, 0):
                                pe.wait_ge(S("bias_ready"), layer + 1)
                            last = pe.matmul(bank[:, 0:T], lhsT=ident, rhs=bm[:, tt, h, :], start=False, stop=True)
                        close_unit(last)

                    def weighted_values(i):
                        nonlocal n_gap
                        a = mine[i]
                        _, src, kind, tt, h = a
                        nst = 4 if src == 0 else 2
                        stored(pe, ("t",) + a)
                        if h == 0 and n_gap >= 2:
                            pe.wait_ge(S("att_free"), n_gap - 1)
                        v0 = AV + (h // 4) * 64 if kind == "a" else NV + h * 64
                        wide = 64 if h == (7 if kind == "a" else 3) else 128
                        for st in range(nst):
                            zt = st if src == 0 else 2 + st
                            last = mm(banks[6 + n_gap % 2][:, h * 64:h * 64 + wide], pt[:, (n_attn + i) % 2, st, :],
                                      z[:, zt, v0:v0 + wide], st, nst)
                        if h == (7 if kind == "a" else 3):
                            last.then_inc(S("att_filled"), 1)
                            n_gap += 1

                    scores(mine[0])
                    scores(mine[1])
                    for i, a in enumerate(mine):
                        _, src, kind, tt, h = a
                        nst = 4 if src == 0 else 2
                        bank = open_unit(("t",) + a, "dve")
                        stored(pe, ("s",) + a)
                        for st in range(nst):
                            last = pe.transpose(bank[:, st * P:(st + 1) * P], pw[:, (n_attn + i) % 2,
                                                st * P:(st + 1) * P], ident)
                        close_unit(last)
                        if i + 2 < len(mine):
                            scores(mine[i + 2])
                        if i >= 1:
                            weighted_values(i - 1)
                    weighted_values(len(mine) - 1)
                    n_attn += len(mine)
                    src = part
                    for gp in range(2):
                        bank = open_unit(("pl", layer, src, gp), "dve")
                        for k in range(2):
                            g = 2 * gp + k
                            for st in range(NT):
                                last = mm(bank[0:64, k * T:(k + 1) * T],
                                          z[:, 2 * src + st, BZ + g * 64:BZ + (g + 1) * 64],
                                          poolc[:, st, g, :], st, NT)
                        close_unit(last)
                    bank = open_unit(("py", layer, src), "dve")
                    stored(pe, ("pl", layer, src, 1))
                    for tt in range(NT):
                        for g in range(4):
                            o = tt * T + g * 64
                            last = mm(bank[:, o:o + 64], plT[0:64, g, tt * P:(tt + 1) * P], plw[0:64, layer, g, :])
                    close_unit(last)
                srcs = (0, 1) if layer == 0 else (0,)
                for src in srcs:
                    pe.wait_ge(S("diag_ready"), 2 + 2 * layer + src)
                    for half in range(2):
                        bank = open_unit(("gb", layer, src, half), "act")
                        close_unit(mm(bank[:, :], ones, diag2[:, 4 * half:4 * half + 4, :]))
                    pe.wait_ge(S("mix_ready"), 2 + 2 * layer + src)
                    transposed(("mT", layer, src), [mix3[:, 2 * src + tt, :] for tt in range(NT)], "act")
                for i in range(N_OUT):
                    w = weights_in_parts()
                    for src in srcs:
                        if i == 0:
                            parts_n += 4
                            pe.wait_ge(S("in_rest_ready"), parts_n)
                        rows_in_parts(("y2", layer, i, src), mT_parts[src], 0, w, "dve", weights=(src == srcs[-1]))
            assert tiles_n[0] == N_TILES

        @block.sync
        def _(sp):
            def fetch(row, k):
                sp.dma_start(ring[:, k, :], W[row]).then_inc(S(f"tile_landed{k}"), 16)

            for k in range(WSLOTS):
                fetch(k, k)
            rounds = (N_TILES - WSLOTS) // WSLOTS
            with sp.Fori(0, rounds) as it:
                for k in range(WSLOTS):
                    row = sp.snap(it * WSLOTS + WSLOTS + k)
                    used = sp.snap(it * WSLOTS + k + 1)
                    sp.wait_ge(S("tile_used"), used)
                    fetch(row, k)
            for n in range(WSLOTS * (rounds + 1), N_TILES):
                sp.wait_ge(S("tile_used"), n - WSLOTS + 1)
                fetch(n, n % WSLOTS)
            sp.wait_ge(S("x_final"), 1)
            sp.dma_start(OUT.rearrange("b (t p) d -> p (b t) d", p=P), x[:, :, :]).then_inc(S("out_done"), 16)
            sp.wait_ge(S("out_done"), 16)

        @block.gpsimd
        def _(pool):
            nc.gpsimd.memset(vml[:, :, :, P:P + 1], 1.0).then_inc(S("vml_ones"), 1)
            for j in range(N_IN):
                k = (2 * MOD_FIRST + j) % WSLOTS
                pool.wait_ge(S("w1_high_ready"), j + 1)
                nc.gpsimd.tensor_tensor(w_rest[:, k, :], ring[:, k, :],
                                        (wy_high if j % 2 else wx_high)[:, :].bitcast(F32), ALU.subtract
                                        ).then_inc(S("w1_rest_ready"), 1)
            pool.wait_ge(S("mlstm_done"), 1)
            nc.gpsimd.memset(qz, 0.0).then_inc(S("gla_zero"), 1)
            nc.gpsimd.memset(qs, 0.0).then_inc(S("gla_zero"), 1)
            nc.gpsimd.memset(att, 0.0).then_inc(S("gla_zero"), 1)
            nc.gpsimd.memset(Sst, 0.0).then_inc(S("gla_zero"), 1)
            with pool.Fori(0, U_HALF) as it:
                for k in range(WSLOTS):
                    for a in range(2):
                        n = pool.snap(it * (2 * WSLOTS) + 2 * k + a + 1)
                        half = slice(a * HALF, (a + 1) * HALF)
                        pool.wait_ge(S("w_high_ready"), n)
                        nc.gpsimd.tensor_tensor(w_rest[:, k, half], ring[:, k, half], w_high[:, a, :].bitcast(F32),
                                                ALU.subtract).then_inc(S("w_rest_ready"), 1)
            pool.wait_ge(S("selT_stored"), 1)

            def differences(b, col):
                nc.gpsimd.tensor_tensor(dif[:, b], iota.unsqueeze(1).to_broadcast([P, 4, P]),
                                        selT[:, 1, bass.ds(col, 4)].unsqueeze(2).to_broadcast([P, 4, P]),
                                        ALU.subtract).then_inc(S("dif_ready"), 1)

            for b in range(2):
                differences(b, 4 * b)
            with pool.Fori(0, T // 8 - 1) as it:
                for b in range(2):
                    n = pool.snap(it * 2 + b + 1)
                    col = pool.snap(it * 8 + 8 + 4 * b)
                    pool.wait_ge(S("oh2_ready"), n)
                    differences(b, col)
            pool.wait_ge(S("w_bank_free"), 2 + T // 4)
            pool.dma_start(c2, CTX2.rearrange("b (t p) d -> p (b t) d", p=P)).then_inc(S("c2_loaded"), 16)
            pool.wait_ge(S("tile_used"), N_PRE + 2 * N_PEER)
            pool.dma_start(normf, NORMF.partition_broadcast(P)).then_inc(S("normf_loaded"), 16)

            def weight_rest(m):
                k = (N_PRE + 2 * N_PEER + m) % WSLOTS
                pool.wait_ge(S("w2_high_ready"), m + 1)
                four = lambda t: t.rearrange("p (a n) -> p a n", a=4)
                nc.gpsimd.tensor_tensor(four(w_rest[:, k, :]), four(ring[:, k, :]), high_of(m).bitcast(F32),
                                        ALU.subtract).then_inc(S("w2_rest_ready"), 1)

            def position_biases(layer, qr):
                for h in range(HEADS):
                    off = ((layer * HEADS + h) * 15 + 7 - qr) * 31 - 48
                    dst = braw[(qr % 2) * 64:(qr % 2) * 64 + 64, qr // 2, h, :]
                    pool.dma_start(dst.rearrange("p (r c) -> p r c", r=4),
                                   bass.AP(tensor=RPB.tensor, offset=off, ap=[[1, 64], [31, 4], [1, 64]])
                                   ).then_inc(S(f"rpb_loaded{layer}"), 16)

            weight_rest(0)
            c2n = S("const2_loaded")
            pool.dma_start(row2, ROW2.partition_broadcast(P)).then_inc(c2n, 16)
            pool.dma_start(cC, CC).then_inc(c2n, 16)
            weight_rest(1)
            pool.dma_start(poolc.rearrange("p a b c -> p (a b c)"), POOL).then_inc(c2n, 16)
            for layer in range(2):
                pool.dma_start(plw[0:64, layer], POOLW[layer].rearrange("g i o -> i g o")).then_inc(c2n, 16)
            for tile in range(2, N_IN2):
                weight_rest(tile)
                if tile < 6:
                    position_biases(0, tile - 2)
            pool.wait_ge(S("bias_ready"), 1)
            for qr in range(4):
                position_biases(1, qr)
            for tile in range(N_IN2, 2 * (N_IN2 + N_OUT)):
                weight_rest(tile)

        @block.scalar
        def _(act):
            steps = [0]

            def link(ins):
                steps[0] += 1
                ins.then_inc(S("act_step"), 1)
                act.wait_ge(S("act_step"), steps[0])

            n_rsqrt = [0]

            def rsqrt(n):
                n_rsqrt[0] += 1
                act.wait_ge(S("ms_ready"), n_rsqrt[0])
                link(nc.scalar.activation(rs[:, 2, 0:n], rs[:, 1, 0:n], ACT.Ln))
                nc.scalar.activation(rs[:, 3, 0:n], rs[:, 2, 0:n], ACT.Exp, scale=-0.5).then_inc(S("r0_ready"), 1)

            n_ss = [0]

            def square_sums(tiles, junk):
                for i, t in enumerate(tiles):
                    if n_ss[0]:
                        act.wait_ge(S("ss_ready"), n_ss[0])
                    n_ss[0] += 1
                    nc.scalar.activation(junk, t, ACT.Square, accum_out=rs[:, 0, i:i + 1]
                                         ).then_inc(S("ss_ready"), 1)

            cn = S("const_loaded")
            act.dma_start(vec[:, :], VEC).then_inc(cn, 16)
            act.dma_start(cA[:, :], CA).then_inc(cn, 16)
            act.dma_start(x[:, :, :], X.rearrange("b (t p) d -> p (b t) d", p=P)).then_inc(cn, 16)
            act.dma_start(cx, CTX.rearrange("b (t p) d -> p (b t) d", p=P)).then_inc(cn, 16)
            act.dma_start(cB, CB).then_inc(cn, 16)
            act.dma_start(row1, ROW1.partition_broadcast(P)).then_inc(cn, 16)
            act.dma_start(lrw2[0:GRANK], LRW2.rearrange("d r k -> r d k")).then_inc(cn, 16)
            act.wait_ge(cn, 16 * N_CONST)
            nc.scalar.activation(condt[:, :, :].rearrange("p c v -> p (c v)"), vec[:, lv["cond"]], ACT.Exp,
                                 scale=-1.0).then_inc(S("cond_exp"), 1)
            square_sums([x[:, 0, :], x[:, 1, :], cx[:, 0, :], cx[:, 1, :]], sqj)
            rsqrt(4)

            def copy_out(key, dst, src=None, scale=None):
                bank = take(act, key)
                src = bank[:, :] if src is None else src(bank)
                if scale is None:
                    free(nc.scalar.copy(dst, src), key)
                else:
                    free(nc.scalar.mul(dst, src, scale), key)

            pair = lambda b: b[:, :].rearrange("p (a n) -> p a n", a=2)
            mod_at = [0]

            def modulation(n=1):
                for _ in range(n):
                    u = mod_at[0]
                    if u == MOD_UNITS:
                        return
                    mod_at[0] += 1
                    if u >= 2:
                        act.wait_ge(S("mod_columns"), u - 1)
                    copy_out(("modrow", u), modrow[0:2, u % 2, :], lambda b: b[0:2, :])

            modulation(MOD_FIRST)

            def in_part(src, high):
                nc.scalar.activation(high, src, ACT.Copy).then_inc(S("in_high_ready"), 1)

            high_n = [0]

            def w1_high():
                j = high_n[0]
                high_n[0] += 1
                n = 2 * MOD_FIRST + j
                act.wait_ge(S(f"tile_landed{n % WSLOTS}"), 16 * (n // WSLOTS + 1))
                if j >= 2:
                    act.wait_ge(S("tile_used"), n - 1)
                nc.scalar.activation((wy_high if j % 2 else wx_high)[:, :], ring[:, n % WSLOTS, :], ACT.Copy
                                     ).then_inc(S("w1_high_ready"), 1)

            act.wait_ge(S("xn_ready"), 4)
            for j in range(2):
                w1_high()
            for src in range(2):
                stored(act, ("hT", src, 3))
                for cc in range(4):
                    in_part(hT[:, 2 * cc:2 * cc + 2, src * T:(src + 1) * T], h1_high[:, src, 2 * cc:2 * cc + 2, :])
            for d in range(2):
                copy_out(("glr", d), glrT[0:GRANK, d, :], lambda b: b[0:GRANK, :])
            w1_high()
            act.wait_ge(S("gate_abs"), 1)
            link(nc.scalar.activation(gtmp[0:HEADS], gtmp[0:HEADS], ACT.Exp, scale=-1.0))
            nc.scalar.activation(gtmp[0:HEADS], gtmp[0:HEADS], ACT.Ln, bias=1.0).then_inc(S("gate_ln"), 1)
            for j in range(3):
                w1_high()
            for i in range(2):
                w1_high()
                for src in range(2):
                    copy_out(("mv", i, src), vml[:, 2 * src:2 * src + 2, 2 * i:2 * i + 2, 0:P],
                             lambda b: b[:, :].rearrange("p (a h n) -> p a h n", a=2, h=2))
            for i in range(2):
                w1_high()
                key = ("mo", i)
                free(nc.scalar.activation(og[:, :, i * WC:(i + 1) * WC], pair(take(act, key)), ACT.Sigmoid), key)
            w1_high()
            copy_out(("gq",), gqT, pair, scale=64.0 ** -0.5)
            w1_high()
            for j in range(2):
                copy_out(("gk", j), gkT[:, j, :])
            for i in range(2):
                w1_high()
                for src in range(2):
                    copy_out(("gv", i, src), gv[:, 2 * src:2 * src + 2, i * WC:(i + 1) * WC], pair)
                if i == 0:
                    act.wait_ge(S("conv_done"), 1)
                    nc.scalar.activation(cq, cq, ACT.Silu).then_inc(S("cq_silu"), 1)
                    nc.scalar.activation(ck, ck, ACT.Silu)
                    act.wait_ge(S("cq_silu"), 1)
                    nc.scalar.mul(cq, cq, float(P) ** -0.5).then_inc(S("conv_ready"), 1)
            for i in range(2):
                if high_n[0] < N_IN:
                    w1_high()
                key = ("gr", i)
                free(nc.scalar.activation(og[:, :, 512 + i * WC:512 + (i + 1) * WC], pair(take(act, key)), ACT.Silu),
                     key)
            assert high_n[0] == N_IN
            modulation(MOD_LATER["gr"])
            act.wait_ge(S("m_ready"), 1)
            nc.scalar.activation(em[0:HEADS], em[0:HEADS], ACT.Exp, scale=-1.0).then_inc(S("em_ready"), 1)
            stored(act, ("acol",))
            for h in range(HEADS):
                for d in range(2):
                    if h >= 1:
                        act.wait_ge(S("P_ready"), 2 * (h - 1) + d + 1)
                    bank = take(act, ("E", h, d))

                    def weight(st, dst, src):
                        return nc.scalar.activation(EW[:, d, st, dst:dst + src.shape[1]], src, ACT.Exp,
                                                    bias=acol[:, st, d, h:h + 1])

                    weight(2, 0, bank[:, 0:T])
                    weight(3, 0, bank[:, 0:T])
                    weight(0, 0, bank[:, T:T + P])
                    if d == 0:
                        weight(0, P, bank[:, P:T])
                    else:
                        weight(1, 0, bank[:, 0:P])
                    free(weight(1, P, bank[:, T + P:2 * T]), ("E", h, d))
                modulation(MOD_LATER["mlstm"])
            modulation(MOD_LATER["alpha"])
            act.wait_ge(S("alpha_abs"), 1)
            link(nc.scalar.activation(lt, lt, ACT.Exp, scale=-1.0))
            nc.scalar.activation(lt, lt, ACT.Ln, bias=1.0).then_inc(S("alpha_ln"), 1)
            act.wait_ge(S("kdec_log"), 1)
            nc.scalar.activation(lt, lt, ACT.Exp).then_inc(S("kdec_exp"), 1)
            nc.scalar.activation(eend, eend, ACT.Exp).then_inc(S("kdec_exp"), 1)
            modulation(MOD_LATER["kdn"])
            act.wait_ge(S("q_log"), 1)
            nc.scalar.activation(lt[:, :, :, T:2 * T], lt[:, :, :, 0:T], ACT.Exp, scale=-1.0).then_inc(S("q_exp"), 1)
            nc.scalar.activation(lt[:, :, :, 0:T], lt[:, :, :, 0:T], ACT.Exp).then_inc(S("q_exp"), 1)
            nc.scalar.activation(lbm[:, :, :, 0:T], lbm[:, :, :, 0:T], ACT.Exp).then_inc(S("q_exp"), 1)
            for step in range(7):
                modulation(MOD_LATER["state"])
            modulation(MOD_UNITS)
            act.wait_ge(S("hcat_ready"), 1)
            for tt in range(NT):
                if tt:
                    act.wait_ge(S("sq_used"), tt)
                nc.scalar.activation(sq2, hcat[:, tt, :], ACT.Square).then_inc(S("sq_ready"), 1)
            rsqrt(16)
            for half in range(2):
                copy_out(("gbc", half), gbc[:, half * 512:(half + 1) * 512])
            for cc in range(4):
                copy_out(("mixT", cc), mixT[:, 2 * cc:2 * cc + 2, :], pair)
            act.wait_ge(S("x_ready"), 1)
            square_sums([x[:, 0, :], x[:, 1, :]], sq2)
            rsqrt(2)
            stored(act, ("h2T", 3))
            nc.scalar.activation(h2_high[:, :, :], h2T[:, :, :], ACT.Copy).then_inc(S("h2_high_ready"), 1)
            for i in range(N_WQ):
                copy_out(("wq", i), qTp[:, 2 * i:2 * i + 2, :], pair)
            for tt in range(NT):
                for q in range(4):
                    copy_out(("sc", tt, q), sc[:, tt, 4 * q:4 * q + 4, :],
                             lambda b: b[:, :].rearrange("p (a n) -> p a n", a=4))
            act.wait_ge(S("emptied_dve"), before_peer["dve"])
            act.sem_inc(S("u_bank_free"), WSLOTS)

            def val(e):
                return e if isinstance(e, int) else act.snap(e)

            def high(k, landed, idx):
                act.wait_ge(S(f"tile_landed{k}"), landed)
                for a in range(2):
                    if not (isinstance(idx[a], int) and idx[a] < 0):
                        act.wait_ge(S("w_high_used"), idx[a])
                        act.wait_ge(S("w_rest_ready"), idx[a])
                    nc.scalar.activation(w_high[:, a, :], ring[:, k, a * HALF:(a + 1) * HALF], ACT.Copy
                                         ).then_inc(S("w_high_ready"), 1)

            def gelu(k, used, col):
                act.wait_ge(S("tile_used"), used)
                nc.scalar.activation(GH[:, bass.ds(col, 2), :], banks[k][:, :].rearrange("p (a t) -> p a t", a=2),
                                     ACT.Gelu).then_inc(S("u_bank_free"), 1)

            def expert_tiles(it, tile, split_before):
                for k in range(WSLOTS):
                    landed = val(it * 16 + 16 * ((N_PRE + tile) // WSLOTS + 1))
                    idx = [val(it * (2 * WSLOTS) + split_before + 2 * k + a - 1) for a in range(2)]
                    high(k, landed, idx)
                    if not (isinstance(it, int) and tile + k == 0):
                        gelu((k - 1) % WSLOTS, val(it * WSLOTS + N_PRE + tile + k),
                             val(it * (2 * WSLOTS) + 2 * (tile + k - 1)))

            expert_tiles(0, 0, 0)
            with act.Fori(0, U_HALF - 1) as it:
                expert_tiles(it, WSLOTS, 2 * WSLOTS)
            act.wait_ge(S("smax_log"), 1)
            for tt in range(NT):
                nc.scalar.activation(bests[:, tt], bests[:, tt], ACT.Exp).then_inc(S("smax_exp"), 1)
            act.wait_ge(S("selT_filled"), 1)
            with act.Fori(0, U_HALF) as it:
                expert_tiles(it, N_PEER // 2, N_SPLIT1)
            gelu(WSLOTS - 1, N_PRE + N_PEER, P - 2)
            def onehots(b, n):
                act.wait_ge(S("dif_ready"), n)
                nc.scalar.activation(dif[:, b], dif[:, b], ACT.Square).then_inc(S("dif_squared"), 1)
                act.wait_ge(S("dif_squared"), n)
                nc.scalar.activation(oh[:, b, 1], dif[:, b], ACT.Relu, bias=ones[:, 0:1], scale=-1.0
                                     ).then_inc(S("oh2_ready"), 1)

            for b in range(2):
                onehots(b, b + 1)
            with act.Fori(0, T // 8 - 1) as it:
                for b in range(2):
                    n = act.snap(it * 2 + b + 3)
                    used = act.snap(it * 2 + b + 1)
                    act.wait_ge(S("w_filled"), used)
                    onehots(b, n)

            act.wait_ge(S("w_bank_free"), 2 + T // 4)
            with act.Fori(0, N_PEER // WSLOTS) as it:
                for k in range(WSLOTS):
                    used = act.snap(it * WSLOTS + N_PRE + N_PEER + k - 1)
                    col = act.snap(it * (2 * WSLOTS) + 2 * k)
                    landed = act.snap(it * 16 + 16 * ((N_PRE + N_PEER) // WSLOTS + 1))
                    idx = [act.snap(it * (2 * WSLOTS) + N_SPLIT2 + 2 * k + a - 1) for a in range(2)]
                    act.wait_ge(S("tile_used"), used)
                    nc.scalar.activation(g_high[:, k % 2], GH[:, bass.ds(col, 2), :], ACT.Copy
                                         ).then_inc(S("g_high_ready"), 1)
                    high(k, landed, idx)
            act.wait_ge(S("x_ready"), 2)
            square_sums([x[:, 0, :], x[:, 1, :]], z[:, 0, 0:D])
            rsqrt(2)
            n_attn, n_x = 0, 2

            def weight_high(m):
                n = N_PRE + 2 * N_PEER + m
                act.wait_ge(S(f"tile_landed{n % WSLOTS}"), 16 * (n // WSLOTS + 1))
                act.wait_ge(S("tile_used"), n - 1)
                nc.scalar.activation(high_of(m), ring[:, n % WSLOTS, :].rearrange("p (a n) -> p a n", a=4), ACT.Copy
                                     ).then_inc(S("w2_high_ready"), 1)

            act.wait_ge(S("c2_loaded"), 16)
            for layer in range(2):
                n_x += 1
                act.wait_ge(S("x_ready"), n_x)
                square_sums([x[:, 0, :], x[:, 1, :]], z[:, 0, 0:D])
                rsqrt(2)
                square_sums([c2[:, 0, :], c2[:, 1, :]], z[:, 0, 0:D])
                first = layer * (N_IN2 + N_OUT)

                def h_parts(src):
                    for cc in range(4):
                        stored(act, ("hT2", layer, src, cc))
                        in_part(hT2[:, 2 * cc:2 * cc + 2, src * T:(src + 1) * T],
                                in_high[:, :].rearrange("p (c t) -> p c t", c=C)[:, 2 * cc:2 * cc + 2,
                                                                                 src * T:(src + 1) * T])

                weight_high(first)
                h_parts(0)
                weight_high(first + 1)
                rsqrt(2)
                for pos, i in enumerate(Z_ORDER):
                    if 1 <= pos < N_IN2 - 1:
                        weight_high(first + pos + 1)
                    for src in range(2):
                        if i in z_tiles(layer, src):
                            dst, key = z[:, 2 * src:2 * src + 2, i * WC:(i + 1) * WC], ("z", layer, i, src)
                            if i in Z_GATES:
                                free(nc.scalar.activation(dst, pair(take(act, key)), ACT.Silu), key)
                            else:
                                copy_out(key, dst, pair)
                        if pos == 0 and src == 0:
                            h_parts(1)
                    if pos == Z_QK:
                        rsqrt(n_norms(layer, 0) + n_norms(layer, 1))
                bufs = dict(aqT=aqT, akT=akT, nqT=nqT, nkT=nkT)

                def qk_out(src, n, buf, h):
                    if n % 2:
                        lo = src * T if buf in ("akT", "nkT") else 0
                        copy_out(("qk", layer, src, n), bufs[buf][0:64, h:h + 2, lo:lo + T],
                                 lambda b: b[0:64, :].rearrange("p (a t) -> p a t", a=2))

                for n, (buf, h, col) in enumerate(qk_pairs(layer, 0)):
                    qk_out(0, n, buf, h)
                for n, (buf, h, col) in enumerate(qk_pairs(layer, 1)):
                    if buf in ("akT", "nkT"):
                        qk_out(1, n, buf, h)
                todo = attn_list(layer)
                for part in range(1 if layer else 2):
                    mine = [a for a in todo if a[1] == part]
                    if part == 1:
                        for n, (buf, h, col) in enumerate(qk_pairs(layer, 1)):
                            if buf in ("aqT", "nqT"):
                                qk_out(1, n, buf, h)
                    for i, a in enumerate(mine):
                        _, src, kind, tt, h = a
                        n = 512 if src == 0 else T
                        act.wait_ge(S("negmax_ready"), n_attn + i + 1)
                        if i >= 2:
                            take(act, ("t",) + mine[i - 2])
                        bank = take(act, ("s",) + a)
                        u = n_attn + i
                        g = attn_group(layer, src, kind, tt)
                        if h == 0 and g >= 2:
                            act.wait_ge(S("att_free"), g - 1)
                        free(nc.scalar.activation(pw[:, u % 2, 0:n], bank[:, 0:n], ACT.Exp,
                                                  bias=tiny[:, 1, u % 16:u % 16 + 1],
                                                  accum_out=tiny[:, 2 + g % 2, h:h + 1]), ("s",) + a)
                    n_attn += len(mine)
                weight_high(first + N_IN2)
                srcs = (0, 1) if layer == 0 else (0,)
                for src in srcs:
                    for half in range(2):
                        copy_out(("gb", layer, src, half), g2b[:, src, half * 512:(half + 1) * 512])
                    for cc in range(4):
                        copy_out(("mT", layer, src, cc), mixT3[:, src, 2 * cc:2 * cc + 2, :], pair)
                        stored(act, ("mT", layer, src, cc))
                        in_part(mixT3[:, src, 2 * cc:2 * cc + 2, :],
                                in_high[:, :].rearrange("p (s c t) -> p s c t", s=2, c=C)[:, src, 2 * cc:2 * cc + 2])
                for i in range(1, N_OUT):
                    weight_high(first + N_IN2 + i)

        @block.vector
        def _(dve):
            steps = [0]

            def link(ins):
                steps[0] += 1
                ins.then_inc(S("dve_step"), 1)
                dve.wait_ge(S("dve_step"), steps[0])

            tt_, ts_, stt = nc.vector.tensor_tensor, nc.vector.tensor_scalar, nc.vector.scalar_tensor_tensor
            n_rsqrt = [0]

            def rsqrt(n, width):
                n_rsqrt[0] += 1
                ms, r, a = rs[:, 1, 0:n], rs[:, 3, 0:n], rs[:, 4, 0:n]
                ts_(ms, rs[:, 0, 0:n], 1.0 / width, EPS, ALU.mult, ALU.add).then_inc(S("ms_ready"), 1)
                dve.wait_ge(S("r0_ready"), n_rsqrt[0])
                link(tt_(a, r, r, ALU.mult))
                link(tt_(a, a, ms, ALU.mult))
                link(ts_(a, a, -0.5, 1.5, ALU.mult, ALU.add))
                link(tt_(r, r, a, ALU.mult))

            n_ss = [0]

            def norm_rows(tiles, outs):
                n_ss[0] += len(tiles)
                dve.wait_ge(S("ss_ready"), n_ss[0])
                rsqrt(len(tiles), D)
                for i, (t, o) in enumerate(zip(tiles, outs)):
                    ts_(o, t, rs[:, 3, i:i + 1], None, ALU.mult).then_inc(S("xn_ready"), 1)

            def bc(ap, shape, axis):
                return ap.unsqueeze(axis).to_broadcast(shape)

            def vcol(name, i=0):
                return vec[:, lv[name].start + i:lv[name].start + i + 1]

            def modulated(key, dst, g, sh):
                for cc in range(4):
                    bank = take(dve, key + (cc,))
                    for k in range(2):
                        c = 2 * cc + k
                        ins = ts_(dst(c), bank[:, k * T:(k + 1) * T], gain[:, g, c:c + 1], sh(c), ALU.mult, ALU.add)
                    free(ins, key + (cc,))

            dve.wait_ge(S("const_loaded"), 16 * N_CONST)
            dve.wait_ge(S("cond_exp"), 1)
            cv = vec[:, lv["cond"]].rearrange("p (c v) -> p c v", v=4)
            link(ts_(condt[:, :, :], condt[:, :, :], 1.0, None, ALU.add))
            link(nc.vector.reciprocal(condt[:, :, :], condt[:, :, :]))
            tt_(cond[:, :, :], condt[:, :, :], cv, ALU.mult).then_inc(S("cond_ready"), 1)
            norm_rows([x[:, 0, :], x[:, 1, :], cx[:, 0, :], cx[:, 1, :]], [xn[:, i, :] for i in range(4)])

            def mod_bias(dst, name, lo, n, col):
                o = lv[name].start + lo
                link(tt_(dst, banks[7][:, 2 * col:2 * (col + n)].rearrange("p (j v) -> p j v", v=2),
                         bc(vec[:, o:o + n], [P, n, 2], 2), ALU.add))

            dve.wait_ge(S("mod_columns"), MOD_FIRST)
            mod_bias(mod1[:, 0:16, :], "bmod1", 0, 16, 0)
            for v in range(2):
                link(stt(out=gain[:, v, :], in0=mod1[:, 8:16, v], scalar=1.0, in1=vec[:, lv["norm1"]],
                         op0=ALU.add, op1=ALU.mult))
            in_n = [0]

            def in_rests(whole, high, rest):
                in_n[0] += 1
                dve.wait_ge(S("in_high_ready"), in_n[0])
                tt_(rest, whole, high.bitcast(F32), ALU.subtract).then_inc(S("in_rest_ready"), 1)

            for src in range(2):
                modulated(("hT", src), lambda c: hT[:, c, src * T:(src + 1) * T], src,
                          lambda c: mod1[:, c, src:src + 1])
            for src in range(2):
                for cc in range(4):
                    at = (slice(None), slice(2 * cc, 2 * cc + 2), slice(src * T, (src + 1) * T))
                    in_rests(hT[at], h1_high[:, src, 2 * cc:2 * cc + 2, :], h1_rest[at])

            for d in range(2):
                for g in range(2):
                    bank = take(dve, ("gate", d, g))
                    o = lv["gate_b"].start + d * 2 + g
                    dst = (gi, gf)[g]
                    free(ts_(dst[0:HEADS, d, :], bank[0:HEADS, :], vec[0:HEADS, o:o + 1], None, ALU.add),
                         ("gate", d, g))
            stored(dve, ("gate", 1, 1))
            stt(out=gtmp[0:HEADS], in0=gf[0:HEADS], scalar=-1.0, in1=gf[0:HEADS], op0=ALU.mult, op1=ALU.max
                ).then_inc(S("gate_abs"), 1)
            cw = vec[:, lv["conv"]].rearrange("p (k c) -> p k c", k=3)

            def conv(u, dst, feat, width, ready):
                u = u.rearrange("p (r c) -> p r c", c=width)
                y = dst.rearrange("p (r c) -> p r c", c=width)
                link(ts_(y, u, cw[:, 1, feat:feat + 1], None, ALU.mult))
                link(stt(out=y[:, :, 1:width], in0=u[:, :, 0:width - 1], scalar=cw[:, 0, feat:feat + 1],
                         in1=y[:, :, 1:width], op0=ALU.mult, op1=ALU.add))
                return stt(out=y[:, :, 0:width - 1], in0=u[:, :, 1:width], scalar=cw[:, 2, feat:feat + 1],
                           in1=y[:, :, 0:width - 1], op0=ALU.mult, op1=ALU.add)

            for i in range(2):
                bank = take(dve, ("mq", i))
                for k in range(2):
                    ins = conv(bank[:, k * T:(k + 1) * T], cq[:, 2 * i + k, :], 2 * i + k, GRID, None)
                free(ins, ("mq", i))
            for h in range(HEADS):
                bank = take(dve, ("mk", h))
                conv(bank[:, 0:T], ck[:, h, 0:T], 4 + h, GRID, None)
                free(conv(bank[:, T:2 * T], ck[:, h, T:2 * T], 4 + h, T, None), ("mk", h))
            stored(dve, ("mk", HEADS - 1))
            dve.sem_inc(S("conv_done"), 1)
            dve.wait_ge(S("gate_ln"), 1)
            link(stt(out=gf[0:HEADS], in0=gf[0:HEADS], scalar=0.0, in1=gtmp[0:HEADS], op0=ALU.min,
                     op1=ALU.subtract))
            scan = nc.vector.tensor_tensor_scan
            one_row = ones[0:HEADS, 0:1].to_broadcast([HEADS, T])
            for part in range(2):
                for d in range(2):
                    lo = T if part == 0 else 0
                    v = slice(lo, lo + T)
                    rev = (lambda ap: ap) if d == 0 else (lambda ap: ap[:, ::-1])
                    last_ctx = 2 * T - 1 if d == 0 else T
                    init = 0.0 if part == 0 else gb[0:HEADS, d, last_ctx:last_ctx + 1]
                    link(scan(rev(gb[0:HEADS, d, v]), one_row, rev(gf[0:HEADS, d, v]), init, ALU.mult, ALU.add))
            link(tt_(negA[0:HEADS], gb[0:HEADS], gi[0:HEADS], ALU.subtract))
            for part in range(2):
                for d in range(2):
                    lo = T if part == 0 else 0
                    v = slice(lo, lo + T)
                    rev = (lambda ap: ap) if d == 0 else (lambda ap: ap[:, ::-1])
                    last_ctx = 2 * T - 1 if d == 0 else T
                    init = 0.0 if part == 0 else nM[0:HEADS, d, last_ctx:last_ctx + 1]
                    link(scan(rev(nM[0:HEADS, d, v]), rev(negA[0:HEADS, d, v]), rev(negA[0:HEADS, d, v]), init,
                              ALU.min, ALU.min))
            dve.sem_inc(S("gate_rows_ready"), 1)
            tt_(em[0:HEADS], gb[0:HEADS, :, 0:T], nM[0:HEADS, :, 0:T], ALU.subtract).then_inc(S("m_ready"), 1)
            bank = take(dve, ("acol",))
            free(ts_(acol.rearrange("p a b c -> p (a b c)"), bank[:, 0:32], -1.0, None, ALU.mult), ("acol",))
            bank = take(dve, ("emcol",))
            free(nc.vector.tensor_copy(emcol.rearrange("p a b c -> p (a b c)"), bank[:, 0:16]), ("emcol",))
            stored(dve, ("gr", 1))
            link(tt_(og, og, bc(row1, [P, NT, D], 1), ALU.mult))
            dve.wait_ge(S("vml_ones"), 1)
            for h in range(HEADS):
                bl, bx = take(dve, ("S", h, 0)), take(dve, ("S", h, 1))
                bl = bl[:, :].rearrange("p (s t) -> p s t", s=2)
                bx = bx[:, :].rearrange("p (s t) -> p s t", s=2)
                for d in range(2):
                    stored(dve, ("E", h, d))
                    if d == 0:
                        tt_(PW[:, d, 0, :], bl[:, 0, :], EW[:, d, 0, :], ALU.mult)
                        tt_(PW[:, d, 1, P:T], bl[:, 1, P:T], EW[:, d, 1, P:T], ALU.mult)
                        tt_(PW[:, d, 2:4, :], bx, EW[:, d, 2:4, :], ALU.mult).then_inc(S("P_ready"), 1)
                    else:
                        tt_(PW[:, d, 0, 0:P], bl[:, 0, 0:P], EW[:, d, 0, 0:P], ALU.mult)
                        free(tt_(PW[:, d, 1, :], bl[:, 1, :], EW[:, d, 1, :], ALU.mult), ("S", h, 0))
                        free(tt_(PW[:, d, 2:4, :], bx, EW[:, d, 2:4, :], ALU.mult), ("S", h, 1))
                        dve.wait_ge(S("emptied_dve"), units[("S", h, 1)]["idx"] + 1)
                        dve.sem_inc(S("P_ready"), 1)
                for d in range(2):
                    bank = take(dve, ("O", h, d))
                    b3 = bank[:, :].rearrange("p (t n) -> p t n", t=NT)
                    den = b3[:, :, P]
                    link(nc.vector.tensor_copy(dn[:, 0, :], den))
                    link(stt(out=dn[:, 1, :], in0=dn[:, 0, :], scalar=-1.0, in1=dn[:, 0, :], op0=ALU.mult,
                             op1=ALU.max))
                    link(tt_(dn[:, 2, :], dn[:, 1, :], emcol[:, :, d, h], ALU.max))
                    link(nc.vector.reciprocal(dn[:, 3, :], dn[:, 2, :]))
                    for tt in range(NT):
                        dst = hcat[:, tt, h * P:(h + 1) * P]
                        if d == 0:
                            ins = ts_(dst, b3[:, tt, 0:P], dn[:, 3, tt:tt + 1], None, ALU.mult)
                        else:
                            ins = stt(out=dst, in0=b3[:, tt, 0:P], scalar=dn[:, 3, tt:tt + 1], in1=dst,
                                      op0=ALU.mult, op1=ALU.add)
                    free(ins, ("O", h, d))
                    stored(dve, ("O", h, d))
            dve.sem_inc(S("mlstm_done"), 1)

            for d in range(2):
                for j in range(2):
                    bank = take(dve, ("alpha", d, j))
                    free(ts_(lx[:, d, j, :], bank[:, :], vcol("alpha_b", d * 2 + j), None, ALU.add),
                         ("alpha", d, j))
            stored(dve, ("alpha", 1, 1))
            stt(out=lt, in0=lx, scalar=-1.0, in1=lx, op0=ALU.mult, op1=ALU.max).then_inc(S("alpha_abs"), 1)
            dve.wait_ge(S("alpha_ln"), 1)
            link(stt(out=lx, in0=lx, scalar=0.0, in1=lt, op0=ALU.min, op1=ALU.subtract))
            link(ts_(lx, lx, 1.0 / 16, None, ALU.mult))
            reset = cB[:, lb["reset"]]
            for d in range(2):
                for j in range(2):
                    rev = (lambda ap: ap) if d == 0 else (lambda ap: ap[:, ::-1])
                    link(scan(rev(lbm[:, d, j, :]), reset, rev(lx[:, d, j, :]), 0.0, ALU.mult, ALU.add))
            chunks = lambda ap: ap.rearrange("p j (c s) -> p j c s", s=GC)
            for d in range(2):
                end = GC - 1 if d == 0 else 0
                b4 = chunks(lbm[:, d])
                link(nc.vector.tensor_copy(eend[:, d], b4[:, :, :, end]))
                link(tt_(chunks(lt[:, d]), b4[:, :, :, end:end + 1].to_broadcast([P, 2, 8, GC]), b4, ALU.subtract))
            dve.sem_inc(S("kdec_log"), 1)
            dve.wait_ge(S("kdec_exp"), 2)
            for d in range(2):
                ins = tt_(lx[:, d], lt[:, d], gkT, ALU.mult)
                if d == 0:
                    link(ins)
            ins.then_inc(S("kdec_ready"), 1)
            dve.wait_ge(S("kdec_ready"), 1)
            for d in range(2):
                refc = GC // 2 if d == 0 else GC // 2 - 1
                b4 = chunks(lbm[:, d, :, 0:T])
                link(tt_(chunks(lt[:, d, :, 0:T]), b4, b4[:, :, :, refc:refc + 1].to_broadcast([P, 2, NGC, GC]),
                         ALU.subtract))
            dve.sem_inc(S("q_log"), 1)
            for d in range(2):
                for src in range(2):
                    bank = take(dve, ("kdn", d, src))
                    v = bank[:, :].rearrange("p (t n) -> p t n", t=NT)
                    for par in range(2):
                        hc = cB[:, lb["half"].start + par:lb["half"].start + par + 1]
                        ins = ts_(kdn[:, d, 2 * src:2 * src + 2, par, :], v, hc, None, ALU.mult)
                    free(ins, ("kdn", d, src))
            dve.wait_ge(S("q_exp"), 3)
            dve.wait_ge(S("gla_zero"), 4)
            for d in range(2):
                tt_(kz[:, d], lt[:, d, :, T:2 * T], gkT[:, :, 0:T], ALU.mult)
                for par in range(2):
                    pr = slice(par * 64, par * 64 + 64)
                    tt_(qz[pr, d, par], lt[pr, d, :, 0:T], gqT[pr], ALU.mult)
                    for j in range(2):
                        v = lambda ap: ap.rearrange("p (a b s) -> p a b s", a=2, b=2)[:, :, par, :]
                        ins = tt_(v(qs[:, d, par, j, :]), v(lbm[:, d, j, 0:T]), v(gqT[:, j, :]), ALU.mult)
                        link(ins)
            dve.sem_inc(S("gla_q_ready"), 1)
            for step in range(7):
                for d in range(2):
                    c = gla_chunk(step, d)
                    bank = take(dve, ("St", step, d))

                    def state(n):
                        if n < NGC:
                            return Sct[:, d, n % 2]
                        return Sst[:, d, gla_chunk(n, d)]

                    new, old = state(step + 1), state(step)
                    for j in range(2):
                        for par in range(2):
                            pr, cols = slice(par * 64, par * 64 + 64), slice(par * P, par * P + P)
                            b = bank[pr, j * 256 + par * P:j * 256 + par * P + P]
                            if step == 0:
                                ins = nc.vector.tensor_copy(new[pr, j, cols], b)
                            else:
                                ins = stt(out=new[pr, j, cols], in0=old[pr, j, cols], scalar=eend[pr, d, j, c:c + 1],
                                          in1=b, op0=ALU.mult, op1=ALU.add)
                    free(ins, ("St", step, d))
                    stored(dve, ("St", step, d))
            for tt in range(NT):
                for d in range(2):
                    bank = take(dve, ("att", tt, d))
                    o = lb["tri_gla"].start + d * P
                    m = bc(cB[:, o:o + P].bitcast(U32), [P, HEADS, P], 1)
                    free(nc.vector.copy_predicated(att[:, d], m, bank[:, :].rearrange("p (h t) -> p h t", h=HEADS)),
                         ("att", tt, d))
                bank = take(dve, ("gla", tt))
                free(nc.vector.tensor_copy(hcat[:, tt, 512:D], bank[:, :]), ("gla", tt))
            stored(dve, ("gla", 1))
            dve.sem_inc(S("hcat_ready"), 1)
            dve.wait_ge(S("mod_columns"), MOD_UNITS)
            mod_bias(mod1[:, 16:48, :], "bmod1", 16, 32, 16)
            for layer in range(2):
                mod_bias(mod2[:, layer], "bmod2", 24 * layer, 24, 48 + 24 * layer)
            link(stt(out=gain[:, 2, :], in0=mod1[:, 32:40, 0], scalar=1.0, in1=vec[:, lv["norm2"]],
                     op0=ALU.add, op1=ALU.mult))
            id8 = bc(ident, [P, C, P], 1)
            link(tt_(diag, id8, bc(mod1[:, 16:24, 0], [P, C, P], 2), ALU.mult))
            dve.sem_inc(S("diag_ready"), 1)
            for tt in range(NT):
                dve.wait_ge(S("sq_ready"), tt + 1)
                link(nc.vector.tensor_reduce(rs[:, 0, tt * 8:tt * 8 + 8], sq2.rearrange("p (h n) -> p h n", n=P),
                                             AX, ALU.add))
                dve.sem_inc(S("sq_used"), 1)
            rsqrt(16, P)
            for tt in range(NT):
                m = mix[:, tt, :].rearrange("p (h n) -> p h n", n=P)
                r = rs[:, 3, tt * 8:tt * 8 + 8]
                link(tt_(m, hcat[:, tt, :].rearrange("p (h n) -> p h n", n=P), bc(r, [P, 8, P], 2), ALU.mult))
                link(tt_(mix[:, tt, :], mix[:, tt, :], og[:, tt, :], ALU.mult))
            dve.sem_inc(S("mix_ready"), 1)
            stored(dve, ("gbc", 1))

            def residual(key, dst, gate, i, tmp):
                bank = take(dve, key)
                cols = slice(i * WC, (i + 1) * WC)
                free(tt_(tmp, bank[:, :].rearrange("p (t n) -> p t n", t=NT), bc(gate[:, cols], [P, NT, WC], 1),
                         ALU.mult), key)
                stored(dve, key)
                link(tt_(dst[:, :, cols], dst[:, :, cols], tmp, ALU.add))

            for i in range(N_OUT):
                residual(("y", i), x, gbc, i, ytmp)
            dve.sem_inc(S("x_ready"), 1)
            norm_rows([x[:, 0, :], x[:, 1, :]], [xn2[:, 0, :], xn2[:, 1, :]])
            modulated(("h2T",), lambda c: h2T[:, c, :], 2, lambda c: mod1[:, 24 + c, 0:1])
            dve.wait_ge(S("h2_high_ready"), 1)
            tt_(h2_rest[:, :, :], h2T[:, :, :], h2_high[:, :, :].bitcast(F32), ALU.subtract).then_inc(S("h2_rest_ready"), 1)

            def top16(vals, scratch, out_v, out_i, n):
                link(nc.vector.max(out_v[:, 0:8], vals))
                nc.vector.max_index(out_i[:, 0:8].bitcast(U32), out_v[:, 0:8], vals)
                link(nc.vector.match_replace(scratch[:, 0:n], out_v[:, 0:8], vals, BIG))
                link(nc.vector.max(out_v[:, 8:16], scratch[:, 0:n]))
                link(nc.vector.max_index(out_i[:, 8:16].bitcast(U32), out_v[:, 8:16], scratch[:, 0:n]))

            for tt in range(NT):
                stored(dve, ("sc", NT - 1, 3))
                for hp in range(16):
                    top16(sc[:, tt, hp, :], work, tops[:, tt, hp, :], topi[:, tt, hp, :], PK)
                link(nc.vector.tensor_copy(topf[:, tt], topi[:, tt].bitcast(U32)))
                pairs = tops[:, tt].rearrange("p (h s) k -> p h s k", s=2)
                for h in range(PH):
                    link(tt_(cand[:, h, :].rearrange("p (a b) -> p a b", a=TOPK), bc(pairs[:, h, 0, :], [P, 16, 16], 2),
                             bc(pairs[:, h, 1, :], [P, 16, 16], 1), ALU.add))
                    top16(cand[:, h, :], work, bests[:, tt, h, :], bestc[:, tt, h, :], 256)
                bc_u = bestc[:, tt].bitcast(U32)
                link(nc.vector.tensor_single_scalar(bhl[:, 0].bitcast(U32), bc_u, 4, ALU.logical_shift_right))
                link(nc.vector.tensor_single_scalar(bhl[:, 1].bitcast(U32), bc_u, 15, ALU.bitwise_and))
                io16 = iota[:, 0:TOPK]
                fi = topf[:, tt].rearrange("p (h s) k -> p h s k", s=2)
                for s in range(2):
                    link(nc.vector.tensor_copy(bhl[:, s], bhl[:, s].bitcast(U32)))
                    link(tt_(onek.rearrange("p h k j -> p (h k) j"), bc(bhl[:, s].rearrange("p h k -> p (h k)"), [P, P, TOPK], 2),
                             bc(io16, [P, P, TOPK], 1), ALU.is_equal))
                    link(tt_(onek, onek, bc(fi[:, :, s, :], [P, PH, TOPK, TOPK], 2), ALU.mult))
                    link(nc.vector.tensor_reduce(sels[:, tt, s, :], onek.rearrange("p h k j -> p (h k) j"), AX,
                                                 ALU.add))
                link(nc.vector.tensor_copy(smx[:, tt, 0:8], bests[:, tt, :, 0]))
                link(tt_(bests[:, tt], bests[:, tt], bc(smx[:, tt, 0:8], [P, PH, TOPK], 2), ALU.subtract))
            dve.sem_inc(S("smax_log"), 1)
            dve.wait_ge(S("smax_exp"), NT)
            for tt in range(NT):
                link(nc.vector.tensor_reduce(smx[:, 2 + tt, 0:8], bests[:, tt], AX, ALU.add))
                link(nc.vector.reciprocal(smx[:, 2 + tt, 8:16], smx[:, 2 + tt, 0:8]))
                link(tt_(sels[:, tt, 2, :].rearrange("p (h k) -> p h k", k=TOPK), bests[:, tt],
                         bc(smx[:, 2 + tt, 8:16], [P, PH, TOPK], 2), ALU.mult))
            dve.sem_inc(S("topk_done"), 1)

            def rests(k, n):
                for a in range(2):
                    half = slice(a * HALF, (a + 1) * HALF)
                    dve.wait_ge(S("w_high_ready"), n[a])
                    tt_(w_rest[:, k, half], ring[:, k, half], w_high[:, a, :].bitcast(F32), ALU.subtract
                        ).then_inc(S("w_rest_ready"), 1)

            dve.wait_ge(S("w_rest_ready"), N_SPLIT1)
            with dve.Fori(0, U_HALF) as it:
                for k in range(WSLOTS):
                    rests(k, [dve.snap(it * (2 * WSLOTS) + N_SPLIT1 + 2 * k + a + 1) for a in range(2)])
            dve.wait_ge(S("tile_used"), N_PRE + N_PEER)
            link(nc.vector.tensor_copy(selT[:, 0:2, :].rearrange("p a t -> p (a t)"), banks[6][:, :]))
            link(nc.vector.tensor_copy(selT[:, 2, :], banks[7][:, 0:T]))
            dve.sem_inc(S("selT_stored"), 1)
            dve.wait_ge(S("u_bank_free"), WSLOTS + N_PEER)
            dve.sem_inc(S("w_bank_free"), 2)

            def weighted_onehots(b, first):
                for k in range(4):
                    one = bass.ds(first[k], 1)
                    ins = ts_(oh[:, b, 0, k, :], iota, selT[:, 0, one], selT[:, 2, one], ALU.is_equal, ALU.mult)
                ins.then_inc(S("oh_ready"), 1)

            def weigh(b, col, n):
                dve.wait_ge(S("w_filled"), n)
                g = GH[:, :, bass.ds(col, 4)]
                tt_(g, g, banks[4 + b][:, :].rearrange("p (t i) -> p i t", t=4), ALU.mult
                    ).then_inc(S("w_bank_free"), 1)

            for b in range(2):
                weighted_onehots(b, [4 * b + k for k in range(4)])
            with dve.Fori(0, T // 8 - 1) as it:
                for b in range(2):
                    n = dve.snap(it * 2 + b + 1)
                    col = dve.snap(it * 8 + 4 * b)
                    weigh(b, col, n)
                    weighted_onehots(b, [dve.snap(it * 8 + 8 + 4 * b + k) for k in range(4)])
            for b in range(2):
                weigh(b, T - 8 + 4 * b, T // 4 - 1 + b)
            with dve.Fori(0, N_PEER // WSLOTS) as it:
                for k in range(WSLOTS):
                    n = dve.snap(it * WSLOTS + k + 1)
                    col = dve.snap(it * (2 * WSLOTS) + 2 * k)
                    idx = [dve.snap(it * (2 * WSLOTS) + N_SPLIT2 + 2 * k + a + 1) for a in range(2)]
                    dve.wait_ge(S("g_high_ready"), n)
                    tt_(g_rest[:, k % 2], GH[:, bass.ds(col, 2), :], g_high[:, k % 2].bitcast(F32), ALU.subtract
                        ).then_inc(S("g_rest_ready"), 1)
                    rests(k, idx)
            dve.wait_ge(S("tile_used"), N_PRE + 2 * N_PEER)
            for c in range(C):
                link(ts_(peT[:, c, :], banks[c // 2][:, (c % 2) * T:(c % 2 + 1) * T], mod1[:, 40 + c, 0:1], None,
                         ALU.mult))
            dve.sem_inc(S("peT_ready"), 1)
            for tt in range(NT):
                for half in range(2):
                    bank = take(dve, ("pe", tt, half))
                    cols = slice(half * 512, (half + 1) * 512)
                    free(tt_(x[:, tt, cols], x[:, tt, cols], bank[:, :], ALU.add), ("pe", tt, half))
            stored(dve, ("pe", 1, 1))
            dve.sem_inc(S("x_ready"), 1)
            dve.wait_ge(S("ss_ready"), n_ss[0] + 2)
            n_ss[0] += 2
            rsqrt(2, D)
            dve.wait_ge(S("normf_loaded"), 16)
            for tt in range(NT):
                link(stt(out=x[:, tt, :], in0=x[:, tt, :], scalar=rs[:, 3, tt:tt + 1], in1=normf, op0=ALU.mult,
                         op1=ALU.mult))
            dve.sem_inc(S("x_ready"), 1)
            for layer in range(2):
                for g in (0, 1):
                    o = lv["normg2"].start + C * layer
                    link(stt(out=gain[:, 3 + g, :], in0=mod2[:, layer, 8:16, g], scalar=1.0, in1=vec[:, o:o + C],
                             op0=ALU.add, op1=ALU.mult))
                for src, rows in ((0, x), (1, c2)):
                    norm_rows([rows[:, tt, :] for tt in range(NT)], [xn3[:, 2 * src + tt, :] for tt in range(NT)])
                    modulated(("hT2", layer, src), lambda c: hT2[:, c, src * T:(src + 1) * T], 3 + src,
                              lambda c: mod2[:, layer, c, src:src + 1])
                    for cc in range(4):
                        at = (slice(None), slice(2 * cc, 2 * cc + 2), slice(src * T, (src + 1) * T))
                        in_rests(hT2[at], *[p[:, :].rearrange("p (c t) -> p c t", c=C)[at] for p in (in_high, in_rest)])
                dve.wait_ge(S("const2_loaded"), 16 * N_CONST2)
                if layer == 0:
                    for l2 in range(2):
                        for nm in ("aq", "nq"):
                            g = row2[:, lr2[f"{nm}{l2}"]]
                            link(ts_(g, g, 64.0 ** -0.5, None, ALU.mult))
                stored(dve, ("z", layer, Z_ORDER[Z_QK - 1], 1))
                n = 0
                for src in range(2):
                    for col, heads, _ in norm_spans(layer, src):
                        zz = z[:, 2 * src:2 * src + 2, col:col + heads * 64]
                        sq = rt[:, :, 0:heads * 64]
                        link(tt_(sq, zz, zz, ALU.mult))
                        link(nc.vector.tensor_reduce(rs[:, 0, n:n + 2 * heads].rearrange("p (t h) -> p t h", t=2),
                                                     sq.rearrange("p t (h n) -> p t h n", n=64), AX, ALU.add))
                        n += 2 * heads
                rsqrt(n, 64)
                n = 0
                for src in range(2):
                    for col, heads, names in norm_spans(layer, src):
                        for tt in range(NT):
                            zz = z[:, 2 * src + tt, col:col + heads * 64].rearrange("p (h n) -> p h n", n=64)
                            link(tt_(zz, zz, bc(rs[:, 3, n:n + heads], [P, heads, 64], 2), ALU.mult))
                            n += heads
                            for h, hs, name in names:
                                zh = zz[:, h:h + hs]
                                link(tt_(zh, zh, bc(row2[:, lr2[f"{name}{layer}"]], [P, hs, 64], 1), ALU.mult))
                    for tt in range(NT):
                        if src == 0:
                            q = z[:, tt, 0:640].rearrange("p (h n) -> p h n", n=64)
                            cs = cC[:, lc["cos"].start + tt * 64:lc["cos"].start + tt * 64 + 64]
                            sn = cC[:, lc["sin"].start + tt * 64:lc["sin"].start + tt * 64 + 64]
                            r0 = rt[:, 0, :].rearrange("p (h n) -> p h n", n=64)
                            link(tt_(r0, q, bc(cs, [P, 10, 64], 1), ALU.mult))
                            for hf in range(2):
                                for a in range(2):
                                    o, s = a * 32 + hf * 16, a * 32 + (1 - hf) * 16
                                    r1 = rt[:, 1, :].rearrange("p (h n) -> p h n", n=64)
                                    link(tt_(r1[:, :, o:o + 16], q[:, :, s:s + 16], bc(sn[:, o:o + 16], [P, 10, 16], 1),
                                             ALU.mult))
                            link(tt_(z[:, tt, 0:640], rt[:, 0, :], rt[:, 1, :], ALU.add))
                    dve.sem_inc(S("qk_ready"), 1)
                stored(dve, ("z", layer, Z_ORDER[-1], 0 if layer else 1))
                srcs = (0, 1) if layer == 0 else (0,)
                bufs = dict(aqT=aqT, akT=akT, nqT=nqT, nkT=nkT)

                def qk_out(src, n, buf, h):
                    if n % 2 == 0:
                        lo = src * T if buf in ("akT", "nkT") else 0
                        key = ("qk", layer, src, n)
                        bank = take(dve, key)
                        free(nc.vector.tensor_copy(bufs[buf][0:64, h:h + 2, lo:lo + T],
                                                   bank[0:64, :].rearrange("p (a t) -> p a t", a=2)), key)

                for n, (buf, h, col) in enumerate(qk_pairs(layer, 0)):
                    qk_out(0, n, buf, h)
                for n, (buf, h, col) in enumerate(qk_pairs(layer, 1)):
                    if buf in ("akT", "nkT"):
                        qk_out(1, n, buf, h)
                todo = attn_list(layer)
                for part in range(1 if layer else 2):
                    mine = [a for a in todo if a[1] == part]
                    if part == 1:
                        for n, (buf, h, col) in enumerate(qk_pairs(layer, 1)):
                            if buf in ("aqT", "nqT"):
                                qk_out(1, n, buf, h)

                    def negmax(a):
                        u = attn_index(a)
                        n = 512 if a[1] == 0 else T
                        bank = take(dve, ("s",) + a)
                        i = u % 16
                        nc.vector.tensor_reduce(tiny[:, 1, i:i + 1], bank[:, 0:n], AX, ALU.max, negate=True
                                                ).then_inc(S("negmax_ready"), 1)

                    negmax(mine[0])
                    negmax(mine[1])
                    if part == 0:
                        dve.wait_ge(S(f"rpb_loaded{layer}"), 16 * 16)
                        for tt in range(NT):
                            for h in range(HEADS):
                                link(tt_(bm[:, tt, h, :].rearrange("p (r c) -> p r c", r=4),
                                         braw[:, tt, h, :].rearrange("p (r c) -> p r c", r=4)[:, :, ::-1],
                                         bc(cC[:, lc["namask"]], [P, 4, GRID], 1), ALU.add))
                        dve.sem_inc(S("bias_ready"), 1)
                    def mixed(a):
                        _, src, kind, tt, h = a
                        g = attn_group(layer, src, kind, tt)
                        dve.wait_ge(S("att_filled"), g + 1)
                        hs = h + 1
                        zt, mo, gc = 2 * src + tt, (0 if kind == "a" else 768), (AG if kind == "a" else NG)
                        link(nc.vector.reciprocal(tiny[:, 4, 0:hs], tiny[:, 2 + g % 2, 0:hs]))
                        m = mix3[:, zt, mo:mo + hs * 64]
                        link(tt_(m.rearrange("p (h n) -> p h n", n=64),
                                 banks[6 + g % 2][:, 0:hs * 64].rearrange("p (h n) -> p h n", n=64),
                                 bc(tiny[:, 4, 0:hs], [P, hs, 64], 2), ALU.mult))
                        dve.sem_inc(S("att_free"), 1)
                        link(tt_(m, m, z[:, zt, gc:gc + hs * 64], ALU.mult))

                    ended = None
                    for i, a in enumerate(mine):
                        _, src, kind, tt, h = a
                        nst = 4 if src == 0 else 2
                        bank = take(dve, ("t",) + a)
                        free(nc.vector.tensor_copy(pt[:, attn_index(a) % 2, 0:nst, :],
                                                   bank[:, 0:nst * P].rearrange("p (s t) -> p s t", s=nst)),
                             ("t",) + a)
                        if i + 2 < len(mine):
                            negmax(mine[i + 2])
                        if ended is not None:
                            mixed(ended)
                            ended = None
                        if h == (7 if kind == "a" else 3):
                            ended = a
                    mixed(ended)
                    src = part
                    for gp in range(2):
                        key = ("pl", layer, src, gp)
                        bank = take(dve, key)
                        free(nc.vector.tensor_copy(plT[0:64, 2 * gp:2 * gp + 2, :],
                                                   bank[0:64, :].rearrange("p (a t) -> p a t", a=2)), key)
                    bank = take(dve, ("py", layer, src))
                    m = mix3[:, 2 * src:2 * src + 2, 512:768]
                    free(tt_(m, bank[:, :].rearrange("p (t n) -> p t n", t=NT),
                             bc(row2[:, lr2[f"pool{layer}"]], [P, NT, 256], 1), ALU.mult), ("py", layer, src))
                    stored(dve, ("py", layer, src))
                    link(tt_(m, m, z[:, 2 * src:2 * src + 2, BG:BG + 256], ALU.mult))
                for src in srcs:
                    if src == 1:
                        stored(dve, ("gb", layer, 0, 1))
                    link(tt_(diag2, id8, bc(mod2[:, layer, 16:24, src], [P, C, P], 2), ALU.mult))
                    dve.sem_inc(S("diag_ready"), 1)
                    dve.sem_inc(S("mix_ready"), 1)
                for src in srcs:
                    for cc in range(4):
                        in_rests(mixT3[:, src, 2 * cc:2 * cc + 2],
                                 *[p[:, :].rearrange("p (s c t) -> p s c t", s=2, c=C)[:, src, 2 * cc:2 * cc + 2]
                                   for p in (in_high, in_rest)])
                stored(dve, ("gb", layer, srcs[-1], 1))
                for i in range(N_OUT):
                    for src in srcs:
                        residual(("y2", layer, i, src), (x, c2)[src], g2b[:, src], i, ytmp2)
                if layer == 0:
                    dve.sem_inc(S("x_ready"), 1)
                else:
                    dve.sem_inc(S("x_final"), 1)


def weight_stream(i):
    def cols(w, starts):
        out = []
        for a in starts:
            t = w[:, a:a + WC]
            out.append(t.reshape(C, P, WC).transpose(1, 0, 2).reshape(P, WT))
        return out

    w_in = i["w_in"][0]
    small = np.concatenate([w_in[:, MG:MG + 16], w_in[:, GLR:GLR + 32], np.zeros((D, WC - 48), np.float32)], 1)
    mods = cols(i["w_mod"][0], range(0, 6 * D, WC))
    for l in range(2):
        mods += cols(i["w_mod_2"][l], range(0, 3 * D, WC))
    tiles = mods[:2 * MOD_FIRST] + cols(small, [0]) + cols(w_in, [a for a, _ in IN_TILES[1:]])
    tiles += mods[2 * MOD_FIRST:] + cols(i["w_out"][0], range(0, D, WC))
    tiles += cols(i["peer_wq"][0], range(0, 2048, WC))
    tiles.append(i["peer_keys"][0].transpose(3, 0, 1, 2).reshape(P, WT))
    u = i["peer_u"][0].reshape(P, N_PEER, 2, C, P).transpose(1, 4, 2, 3, 0).reshape(N_PEER, P, WT)
    v = i["peer_v"][0].reshape(P, N_PEER, 2, D).transpose(1, 0, 2, 3).reshape(N_PEER, P, WT)
    rest = []
    for l in range(2):
        rest += cols(i["w_in_2"][l], [WC * t for t in Z_ORDER]) + cols(i["w_out_2"][l], range(0, D, WC))
    return np.concatenate([np.stack(tiles), u, v, np.stack(rest)])


def small_inputs(i):
    _, _, _, lv, _, _ = layouts()
    col = lambda a: np.asarray(a).reshape(-1, P).T
    v = np.zeros((P, lv.n), np.float32)
    cs = [i["c"], i["c_ctx"], i["c_2"], i["c_ctx_2"]]
    v[:, lv["cond"]] = np.stack([col(c) for c in cs], 2).reshape(P, 4 * C)
    v[:, lv["bmod1"]] = col(i["b_mod"])
    v[:, lv["bmod2"]] = col(i["b_mod_2"])
    v[:, lv["norm1"]] = col(i["norm1_g"])
    v[:, lv["norm2"]] = col(i["norm2_g"])
    v[:, lv["normg2"]] = col(i["norm_gain_2"])
    v[:, lv["conv"]] = col(i["ml_conv_w"])
    v[:, lv["alpha_b"]] = col(i["gla_alpha_b"])
    v[0:HEADS, lv["gate_b"]] = i["ml_gate_b"].reshape(4, HEADS).T
    r1 = np.concatenate([i["ml_norm_g"].ravel(), i["gla_norm_g"].ravel()])[None]
    r2 = np.concatenate([i[n][l].ravel() for l in range(2) for n in
                         ("att_q_gain_2", "att_k_gain_2", "na_q_gain_2", "na_k_gain_2", "pool_scale_2")])[None]
    return v, r1, r2


def kernel(**inputs):
    import concourse.bacc as bacc
    from concourse.bass_utils import run_bass_kernel_spmd

    i = {k: np.asarray(v) for k, v in inputs.items()}
    a, b, c, pool = constants()
    vec, row1, row2 = small_inputs(i)
    arrays = dict(W=weight_stream(i), CA=a, CB=b, CC=c, POOL=pool, VEC=vec, ROW1=row1,
                  NORMF=i["norm_f_g"][None], ROW2=row2, LRW2=i["gla_lr_w2"][0], POOLW=i["pool_w_2"],
                  X=i["x"], CTX=i["ctx"], CTX2=i["ctx_2"], RPB=i["na_rpb_2"][..., ::-1])
    arrays = {k: np.ascontiguousarray(v) for k, v in arrays.items()}
    nc = bacc.Bacc("TRN2", target_bir_lowering=False, num_devices=1)
    aps = {k: nc.dram_tensor(k, v.shape, F32, kind="ExternalInput").ap() for k, v in arrays.items()}
    out = nc.dram_tensor("OUT", (1, T, D), F32, kind="ExternalOutput").ap()
    build(nc, OUT=out, **aps)
    r = run_bass_kernel_spmd(nc, [arrays], core_ids=[0])
    return r.results[0]["OUT"]
```
